# Optimizing a Trainium2 kernel written in Bass

```python
import math
import jax, jax.numpy as jnp
from jax import lax
import numpy as np

D_MODEL = 2048
BATCH = 1
SEQ = 256
DEPTH = 1

CHUNK = 64
EPS = 1e-6

S5_GROUPS = 32
S5_GROUP_DIM = 16
S5_WIDTH = S5_GROUPS * S5_GROUP_DIM
S5_STATE = 64
S5_DT_MIN = 1e-3
S5_DT_MAX = 1e-1

HG_HEADS = 6
HG_DK = 128
HG_DV = 128
HG_KEY_WIDTH = HG_HEADS * HG_DK
HG_WIDTH = HG_HEADS * HG_DV

ML_HEADS = 4
ML_DH = 192
ML_WIDTH = ML_HEADS * ML_DH
ML_CONV = 4

MIX_WIDTH = S5_WIDTH + HG_WIDTH + ML_WIDTH
N_BRANCH = 3

FFN_DIM = 5632
FFN_CONV = 3

IN_WIDTHS = (S5_WIDTH,
             HG_KEY_WIDTH, HG_KEY_WIDTH,
             HG_WIDTH, HG_WIDTH,
             ML_WIDTH, ML_WIDTH, ML_WIDTH,
             ML_HEADS, ML_HEADS,
             N_BRANCH * D_MODEL)
IN_TOTAL = 12040


def _split_points():
    pts, acc = [], 0
    for w in IN_WIDTHS[:-1]:
        acc += w
        pts.append(acc)
    return pts

def rms_norm(x, g):
    xf = x.astype(jnp.float32)
    y = xf * lax.rsqrt(jnp.mean(xf * xf, axis=-1, keepdims=True) + EPS)
    return (y * g.astype(jnp.float32)).astype(x.dtype)

def causal_dwconv(x, w, b):
    k, c = w.shape[0], x.shape[-1]
    y = lax.conv_general_dilated(x, w[:, None, :].astype(x.dtype), window_strides=(1,),
                                 padding=((k - 1, 0),), dimension_numbers=('NWC', 'WIO', 'NWC'),
                                 feature_group_count=c)
    return y + b.astype(x.dtype)

def to_chunks(t, n_heads, d):
    bsz, seq = t.shape[0], t.shape[1]
    return t.reshape(bsz, seq // CHUNK, CHUNK, n_heads, d).transpose(1, 0, 3, 2, 4)

def from_chunks(t):
    nc, bsz, h, l, d = t.shape
    return t.transpose(1, 0, 3, 2, 4).reshape(bsz, nc * l, h, d)

def s5_mixer(u, lam_re, lam_im, log_dt, b_re, b_im, c_re, c_im, d_skip, w_glu, b_glu):
    bsz, seq, _ = u.shape
    f32 = jnp.float32
    uf = u.astype(f32).reshape(bsz, seq, S5_GROUPS, S5_GROUP_DIM)
    dt = jnp.exp(log_dt.astype(f32))[:, None]
    lr, li = lam_re.astype(f32), lam_im.astype(f32)
    mag = jnp.exp(lr * dt)
    ar, ai = mag * jnp.cos(li * dt), mag * jnp.sin(li * dt)
    den = lr * lr + li * li
    cr = ((ar - 1.0) * lr + ai * li) / den
    ci = (ai * lr - (ar - 1.0) * li) / den
    br_, bi_ = b_re.astype(f32), b_im.astype(f32)
    bbr = cr[..., None] * br_ - ci[..., None] * bi_
    bbi = cr[..., None] * bi_ + ci[..., None] * br_
    xr = jnp.einsum('bsgp,gnp->bsgn', uf, bbr)
    xi = jnp.einsum('bsgp,gnp->bsgn', uf, bbi)
    ar_f = jnp.broadcast_to(ar, xr.shape)
    ai_f = jnp.broadcast_to(ai, xr.shape)

    def combine(e1, e2):
        a1r, a1i, x1r, x1i = e1
        a2r, a2i, x2r, x2i = e2
        return (a2r * a1r - a2i * a1i, a2r * a1i + a2i * a1r,
                a2r * x1r - a2i * x1i + x2r, a2r * x1i + a2i * x1r + x2i)

    _, _, sr, si = lax.associative_scan(combine, (ar_f, ai_f, xr, xi), axis=1)
    y = (jnp.einsum('bsgn,gpn->bsgp', sr, c_re.astype(f32))
         - jnp.einsum('bsgn,gpn->bsgp', si, c_im.astype(f32))
         + d_skip.astype(f32).reshape(S5_GROUPS, S5_GROUP_DIM) * uf)
    y = jax.nn.gelu(y.reshape(bsz, seq, S5_WIDTH))
    y = y * jax.nn.sigmoid(y @ w_glu.astype(f32) + b_glu.astype(f32))
    return y.astype(u.dtype)

def hgrn2_mixer(q_in, f_in, i_in, g_in, lb, norm_g):
    bsz, seq, _ = q_in.shape
    f32 = jnp.float32
    q = jax.nn.silu(q_in.astype(f32))
    lbf = lb.astype(f32)
    f = lbf + (1.0 - lbf) * jax.nn.sigmoid(f_in.astype(f32))
    logf = jnp.log(f)
    k = 1.0 - f
    v = i_in.astype(f32)
    qc, kc = to_chunks(q, HG_HEADS, HG_DK), to_chunks(k, HG_HEADS, HG_DK)
    vc, gc = to_chunks(v, HG_HEADS, HG_DV), to_chunks(logf, HG_HEADS, HG_DK)
    causal = jnp.tril(jnp.ones((CHUNK, CHUNK), dtype=bool))

    def step(state, xs):
        qb, kb, vb, gb = xs
        cum = jnp.cumsum(gb, axis=2)
        last = cum[:, :, -1:, :]
        inter = jnp.einsum('bhtk,bhkv->bhtv', qb * jnp.exp(cum), state)
        diff = cum[:, :, :, None, :] - cum[:, :, None, :, :]
        decay = jnp.exp(jnp.where(causal[:, :, None], diff, -jnp.inf))
        scores = jnp.einsum('bhtk,bhsk,bhtsk->bhts', qb, kb, decay)
        out = inter + jnp.einsum('bhts,bhsv->bhtv', scores, vb)
        new_state = (jnp.exp(last[:, :, 0, :])[..., None] * state
                     + jnp.einsum('bhsk,bhsv->bhkv', kb * jnp.exp(last - cum), vb))
        return new_state, out

    s0 = jnp.zeros((bsz, HG_HEADS, HG_DK, HG_DV), f32)
    _, o = lax.scan(step, s0, (qc, kc, vc, gc))
    o = rms_norm(from_chunks(o), norm_g.reshape(HG_HEADS, HG_DV))
    o = o.reshape(bsz, seq, HG_WIDTH) * jax.nn.silu(g_in.astype(f32))
    return o.astype(q_in.dtype)

def mlstm_mixer(cx, v_in, o_in, ig_in, fg_in, conv_w, conv_b, w_qk, b_ig, b_fg, norm_g):
    bsz, seq, _ = cx.shape
    f32 = jnp.float32
    ca = jax.nn.silu(causal_dwconv(cx, conv_w, conv_b)).reshape(bsz, seq, ML_HEADS, ML_DH)
    qk = jnp.einsum('bshd,hde->bshe', ca, w_qk.astype(ca.dtype)).astype(f32)
    q = qk[..., :ML_DH].reshape(bsz, seq, ML_WIDTH)
    k = (qk[..., ML_DH:] * (ML_DH ** -0.5)).reshape(bsz, seq, ML_WIDTH)
    v = v_in.astype(f32)
    ig = (ig_in + b_ig).astype(f32)
    lf = jax.nn.log_sigmoid((fg_in + b_fg).astype(f32))
    qc, kc, vc = to_chunks(q, ML_HEADS, ML_DH), to_chunks(k, ML_HEADS, ML_DH), to_chunks(v, ML_HEADS, ML_DH)
    nch = seq // CHUNK
    icc = ig.reshape(bsz, nch, CHUNK, ML_HEADS).transpose(1, 0, 3, 2)
    fcc = lf.reshape(bsz, nch, CHUNK, ML_HEADS).transpose(1, 0, 3, 2)
    causal = jnp.tril(jnp.ones((CHUNK, CHUNK), dtype=bool))

    def step(carry, xs):
        cmat, nvec, m = carry
        qb, kb, vb, ib, fb = xs
        bcum = jnp.cumsum(fb, axis=-1)
        dmat = jnp.where(causal, bcum[..., :, None] - bcum[..., None, :] + ib[..., None, :], -jnp.inf)
        inter_log = bcum + m[..., None]
        m_t = jnp.maximum(inter_log, jnp.max(dmat, axis=-1))
        w_inter = jnp.exp(inter_log - m_t)
        w_intra = jnp.exp(dmat - m_t[..., None]) * jnp.einsum('bhtd,bhsd->bhts', qb, kb)
        num = (w_inter[..., None] * jnp.einsum('bhtk,bhkv->bhtv', qb, cmat)
               + jnp.einsum('bhts,bhsv->bhtv', w_intra, vb))
        den = w_inter * jnp.einsum('bhtk,bhk->bht', qb, nvec) + jnp.sum(w_intra, axis=-1)
        h = num / jnp.maximum(jnp.abs(den), jnp.exp(-m_t))[..., None]
        m_new = m_t[..., -1]
        decay = jnp.exp(bcum[..., -1] + m - m_new)
        ws = jnp.exp(bcum[..., -1:] - bcum + ib - m_new[..., None])
        c_new = decay[..., None, None] * cmat + jnp.einsum('bhs,bhsk,bhsv->bhkv', ws, kb, vb)
        n_new = decay[..., None] * nvec + jnp.einsum('bhs,bhsk->bhk', ws, kb)
        return (c_new, n_new, m_new), h

    init = (jnp.zeros((bsz, ML_HEADS, ML_DH, ML_DH), f32),
            jnp.zeros((bsz, ML_HEADS, ML_DH), f32),
            jnp.zeros((bsz, ML_HEADS), f32))
    _, h = lax.scan(step, init, (qc, kc, vc, icc, fcc))
    h = rms_norm(from_chunks(h), norm_g.reshape(ML_HEADS, ML_DH))
    h = h.reshape(bsz, seq, ML_WIDTH) * jax.nn.sigmoid(o_in.astype(f32))
    return h.astype(cx.dtype)

def conv_ffn(h, w_up, conv_w, conv_b, w_down):
    up = causal_dwconv(h @ w_up, conv_w, conv_b)
    a, b = up[..., :FFN_DIM], up[..., FFN_DIM:]
    return (jax.nn.silu(a) * b) @ w_down

def first_inputs(seed: int = 0) -> dict:
    key = jax.random.key(seed)
    ks = jax.random.split(key, 32)
    f32 = jnp.float32
    L, G, N, P = DEPTH, S5_GROUPS, S5_STATE, S5_GROUP_DIM

    def nrm(k, shape, scale):
        return scale * jax.random.normal(k, shape, f32)

    n_idx = jnp.arange(N, dtype=f32)
    return {
        'x': nrm(ks[0], (BATCH, SEQ, D_MODEL), 1.0),
        'mix_norm': 1.0 + nrm(ks[1], (L, D_MODEL), 0.02),
        'w_in': nrm(ks[2], (L, D_MODEL, IN_TOTAL), D_MODEL ** -0.5),
        's5_lam_re': -0.5 + nrm(ks[3], (L, G, N), 0.01),
        's5_lam_im': math.pi * n_idx + nrm(ks[4], (L, G, N), 0.01),
        's5_log_dt': jax.random.uniform(ks[5], (L, G), f32, math.log(S5_DT_MIN), math.log(S5_DT_MAX)),
        's5_b_re': nrm(ks[6], (L, G, N, P), (2 * P) ** -0.5),
        's5_b_im': nrm(ks[7], (L, G, N, P), (2 * P) ** -0.5),
        's5_c_re': nrm(ks[8], (L, G, P, N), N ** -0.5),
        's5_c_im': nrm(ks[9], (L, G, P, N), N ** -0.5),
        's5_d': nrm(ks[10], (L, S5_WIDTH), 1.0),
        's5_w_glu': nrm(ks[11], (L, S5_WIDTH, S5_WIDTH), S5_WIDTH ** -0.5),
        's5_b_glu': nrm(ks[12], (L, S5_WIDTH), 0.02),
        'hg_lower_bounds': nrm(ks[13], (L, HG_KEY_WIDTH), 1.0),
        'hg_norm': 1.0 + nrm(ks[14], (L, HG_WIDTH), 0.02),
        'ml_conv_w': nrm(ks[15], (L, ML_CONV, ML_WIDTH), 0.5),
        'ml_conv_b': nrm(ks[16], (L, ML_WIDTH), 0.02),
        'ml_w_qk': nrm(ks[17], (L, ML_HEADS, ML_DH, 2 * ML_DH), ML_DH ** -0.5),
        'ml_b_ig': nrm(ks[18], (L, ML_HEADS), 0.1),
        'ml_b_fg': jnp.linspace(3.0, 6.0, ML_HEADS, dtype=f32)[None, :] + nrm(ks[19], (L, ML_HEADS), 0.01),
        'ml_norm': 1.0 + nrm(ks[20], (L, ML_WIDTH), 0.02),
        'w_branch': nrm(ks[21], (L, MIX_WIDTH, D_MODEL), (MIX_WIDTH / N_BRANCH) ** -0.5),
        'w_out': nrm(ks[22], (L, D_MODEL, D_MODEL), D_MODEL ** -0.5),
        'ffn_norm': 1.0 + nrm(ks[23], (L, D_MODEL), 0.02),
        'ffn_w_up': nrm(ks[24], (L, D_MODEL, 2 * FFN_DIM), D_MODEL ** -0.5),
        'ffn_conv_w': nrm(ks[25], (L, FFN_CONV, 2 * FFN_DIM), FFN_CONV ** -0.5),
        'ffn_conv_b': nrm(ks[26], (L, 2 * FFN_DIM), 0.02),
        'ffn_w_down': nrm(ks[27], (L, FFN_DIM, D_MODEL), FFN_DIM ** -0.5),
        'final_norm': 1.0 + nrm(ks[28], (D_MODEL,), 0.02),
    }

def first_block(x, mix_norm, w_in, s5_lam_re, s5_lam_im, s5_log_dt, s5_b_re, s5_b_im, s5_c_re, s5_c_im,
              s5_d, s5_w_glu, s5_b_glu, hg_lower_bounds, hg_norm, ml_conv_w, ml_conv_b, ml_w_qk,
              ml_b_ig, ml_b_fg, ml_norm, w_branch, w_out, ffn_norm, ffn_w_up, ffn_conv_w, ffn_conv_b,
              ffn_w_down, final_norm):
    lbs = jax.nn.softmax(hg_lower_bounds.astype(jnp.float32), axis=0)
    lbs = jnp.cumsum(lbs, axis=0) - lbs[0:1]
    splits = _split_points()
    r_a, r_b = S5_WIDTH, S5_WIDTH + HG_WIDTH
    for l in range(DEPTH):
        h = rms_norm(x, mix_norm[l])
        (u_a, q_b, f_b, i_b, og_b, cx_c, v_c, o_c, ig_c, fg_c, gates) = jnp.split(h @ w_in[l], splits, axis=-1)
        y_a = s5_mixer(u_a, s5_lam_re[l], s5_lam_im[l], s5_log_dt[l], s5_b_re[l], s5_b_im[l],
                       s5_c_re[l], s5_c_im[l], s5_d[l], s5_w_glu[l], s5_b_glu[l])
        y_b = hgrn2_mixer(q_b, f_b, i_b, og_b, lbs[l], hg_norm[l])
        y_c = mlstm_mixer(cx_c, v_c, o_c, ig_c, fg_c, ml_conv_w[l], ml_conv_b[l], ml_w_qk[l],
                          ml_b_ig[l], ml_b_fg[l], ml_norm[l])
        wb = w_branch[l]
        g_a, g_b, g_c = (gates[..., :D_MODEL], gates[..., D_MODEL:2 * D_MODEL], gates[..., 2 * D_MODEL:])
        merged = (jax.nn.sigmoid(g_a) * (y_a @ wb[:r_a])
                  + jax.nn.sigmoid(g_b) * (y_b @ wb[r_a:r_b])
                  + jax.nn.sigmoid(g_c) * (y_c @ wb[r_b:]))
        x = x + merged @ w_out[l]
        x = x + conv_ffn(rms_norm(x, ffn_norm[l]), ffn_w_up[l], ffn_conv_w[l], ffn_conv_b[l], ffn_w_down[l])
    return rms_norm(x, final_norm)


_first_inputs = first_inputs


def first_inputs(seed=0):
    import zlib

    import numpy as np

    out = dict(_first_inputs(seed))
    spreads = {}
    factors = {'mix_norm': 3.129,
     's5_lam_re': 64.0,
     's5_lam_im': 30.752,
     's5_log_dt': 32.408,
     's5_b_re': 44.208,
     's5_b_im': 44.712,
     's5_c_re': 43.576,
     's5_c_im': 43.92,
     's5_b_glu': 64.0,
     'hg_norm': 8.0,
     'ml_conv_b': 3.147,
     'ml_b_ig': 64.0,
     'ml_norm': 64.0,
     'ffn_norm': 11.756,
     'ffn_conv_b': 11.839,
     'final_norm': 7.458}
    for name, (base, spread) in spreads.items():
        noise = np.random.default_rng([zlib.crc32(name.encode()), seed]).standard_normal(out[name].shape)
        drawn = base * np.exp(spread * noise) if base else spread * noise
        out[name] = __import__('jax').numpy.asarray(drawn.astype(out[name].dtype))
    for name, factor in factors.items():
        out[name] = (out[name] * factor).astype(out[name].dtype)
    return out


_narrow_inputs = first_inputs


def first_inputs(seed=0):
    out = dict(_narrow_inputs(seed))
    wider = {'s5_w_glu': 3.14, 's5_b_glu': 5.24, 'hg_norm': 5.31, 'final_norm': 3.08}
    for name, times in wider.items():
        mean = out[name].mean()
        out[name] = (mean + times * (out[name] - mean)).astype(out[name].dtype)
    return out


MLA_HEADS = 8
Q_LORA = 512
KV_LORA = 512
QK_NOPE = 128
QK_ROPE = 64
V_DIM = 128
ROPE_THETA = 10000.0
Q_BLOCK = 128
DIL_HEADS = 8
DIL_DIM = 128
DIL_PATTERNS = ((128, 1), (512, 4), (2048, 16))
DIL_BLOCK = 64
N_BRANCH_2 = 2
D_FF = -(-8 * D_MODEL // (3 * 256)) * 256
RMS_EPS = 1e-6
NEG_INF = -1e30
D_IN = Q_LORA + KV_LORA + QK_ROPE + 3 * DIL_HEADS * DIL_DIM + N_BRANCH_2 * D_MODEL


def rms_norm_2(x, g):
    xf = x.astype(jnp.float32)
    y = xf * lax.rsqrt(jnp.mean(xf * xf, axis=-1, keepdims=True) + RMS_EPS)
    return (y * g.astype(jnp.float32)).astype(x.dtype)

def rope_tables(seq):
    inv = ROPE_THETA ** (-jnp.arange(0, QK_ROPE, 2, dtype=jnp.float32) / QK_ROPE)
    ang = jnp.arange(seq, dtype=jnp.float32)[:, None] * inv[None, :]
    return jnp.cos(ang), jnp.sin(ang)

def apply_rope(x, cos, sin):
    x1, x2 = jnp.split(x, 2, axis=-1)
    c = cos.astype(x.dtype)
    s = sin.astype(x.dtype)
    return jnp.concatenate([x1 * c - x2 * s, x1 * s + x2 * c], axis=-1)

def alibi_slopes(n_heads):
    return jnp.power(2.0, -8.0 * jnp.arange(1, n_heads + 1, dtype=jnp.float32) / n_heads)

def mla_attention(q_nope, q_rope, k_nope, k_rope, v):
    B, S, H, _ = q_nope.shape
    nq = S // Q_BLOCK
    scale = (QK_NOPE + QK_ROPE) ** -0.5

    def to_blocks(t):
        return jnp.moveaxis(t.reshape(B, nq, Q_BLOCK, *t.shape[2:]), 1, 0)

    def attend(blk):
        qn, qr = blk
        s = (jnp.einsum('bqhd,bkhd->bhqk', qn, k_nope, preferred_element_type=jnp.float32)
             + jnp.einsum('bqhd,bkd->bhqk', qr, k_rope, preferred_element_type=jnp.float32)) * scale
        p = jax.nn.softmax(s, axis=-1).astype(v.dtype)
        return jnp.einsum('bhqk,bkhd->bqhd', p, v)

    o = lax.map(attend, (to_blocks(q_nope), to_blocks(q_rope)))
    return jnp.moveaxis(o, 0, 1).reshape(B, S, H, v.shape[-1])

def strided_band_attention(q, k, v, slopes, n_side, dil):
    B, S, H, D = q.shape
    L = S // dil
    nb = -(-L // DIL_BLOCK)
    Lp = nb * DIL_BLOCK

    def to_sub(t):
        return t.reshape(B, L, dil, H, D).transpose(0, 2, 1, 3, 4)

    qs = jnp.pad(to_sub(q), ((0, 0), (0, 0), (0, Lp - L), (0, 0), (0, 0)))
    qs = qs.reshape(B, dil, nb, DIL_BLOCK, H, D)

    def windows(t):
        tp = jnp.pad(to_sub(t), ((0, 0), (0, 0), (DIL_BLOCK, DIL_BLOCK + Lp - L), (0, 0), (0, 0)))
        tb = tp.reshape(B, dil, nb + 2, DIL_BLOCK, H, D)
        return jnp.concatenate([tb[:, :, :-2], tb[:, :, 1:-1], tb[:, :, 2:]], axis=3)

    kw = windows(k)
    vw = windows(v)

    qi = jnp.arange(DIL_BLOCK)[:, None]
    kj = jnp.arange(3 * DIL_BLOCK)[None, :]
    delta = kj - DIL_BLOCK - qi
    kpos = (jnp.arange(nb)[:, None] - 1) * DIL_BLOCK + jnp.arange(3 * DIL_BLOCK)[None, :]
    valid = (jnp.abs(delta) <= n_side)[None] & ((kpos >= 0) & (kpos < L))[:, None, :]
    bias = -slopes[:, None, None] * (dil * jnp.abs(delta)).astype(jnp.float32)[None]

    s = jnp.einsum('bcnqhd,bcnkhd->bcnhqk', qs, kw, preferred_element_type=jnp.float32) * (D ** -0.5)
    s = jnp.where(valid[:, None], s + bias, NEG_INF)
    m = jnp.max(s, axis=-1, keepdims=True)
    p = jnp.exp(s - m)
    l = jnp.sum(p, axis=-1)
    o = jnp.einsum('bcnhqk,bcnkhd->bcnqhd', p.astype(v.dtype), vw).astype(jnp.float32)
    o = o / jnp.swapaxes(l, -1, -2)[..., None]
    lse = jnp.swapaxes(m[..., 0] + jnp.log(l), -1, -2)

    o = o.reshape(B, dil, Lp, H, D)[:, :, :L].transpose(0, 2, 1, 3, 4).reshape(B, S, H, D)
    lse = lse.reshape(B, dil, Lp, H)[:, :, :L].transpose(0, 2, 1, 3).reshape(B, S, H)
    return o, lse

def dilated_attention(q, k, v):
    slopes = alibi_slopes(q.shape[2])
    outs, lses = [], []
    for window, dil in DIL_PATTERNS:
        o, lse = strided_band_attention(q, k, v, slopes, window // (2 * dil), dil)
        outs.append(o)
        lses.append(lse)
    w = jax.nn.softmax(jnp.stack(lses), axis=0)
    o = sum(w[g][..., None] * outs[g] for g in range(len(DIL_PATTERNS)))
    return o.astype(v.dtype)

def hybrid_layer(x, cos, sin, g_mix, w_in, b_gate, g_cq, w_uq, g_ckv, w_ukv,
                 g_q_nope, g_q_rope, g_k_nope, g_k_rope, g_q_dil, g_k_dil,
                 w_o_mla, w_o_dil, w_o, g_ffn, w_gate_up, w_down):
    B, S, _ = x.shape
    h = rms_norm_2(x, g_mix)
    proj = h @ w_in
    dh = DIL_HEADS * DIL_DIM
    cuts = np.cumsum([Q_LORA, KV_LORA, QK_ROPE, dh, dh, dh]).tolist()
    c_q, c_kv, k_r, q_d, k_d, v_d, gate = jnp.split(proj, cuts, axis=-1)

    q = (rms_norm_2(c_q, g_cq) @ w_uq).reshape(B, S, MLA_HEADS, QK_NOPE + QK_ROPE)
    q_nope, q_rope = jnp.split(q, [QK_NOPE], axis=-1)
    q_nope = rms_norm_2(q_nope, g_q_nope)
    q_rope = apply_rope(rms_norm_2(q_rope, g_q_rope), cos[:, None, :], sin[:, None, :])
    kv = (rms_norm_2(c_kv, g_ckv) @ w_ukv).reshape(B, S, MLA_HEADS, QK_NOPE + V_DIM)
    k_nope, v_a = jnp.split(kv, [QK_NOPE], axis=-1)
    k_nope = rms_norm_2(k_nope, g_k_nope)
    k_rope = apply_rope(rms_norm_2(k_r, g_k_rope), cos, sin)
    o_a = mla_attention(q_nope, q_rope, k_nope, k_rope, v_a)
    y_a = o_a.reshape(B, S, MLA_HEADS * V_DIM) @ w_o_mla

    qd = rms_norm_2(q_d.reshape(B, S, DIL_HEADS, DIL_DIM), g_q_dil)
    kd = rms_norm_2(k_d.reshape(B, S, DIL_HEADS, DIL_DIM), g_k_dil)
    vd = v_d.reshape(B, S, DIL_HEADS, DIL_DIM)
    o_b = dilated_attention(qd, kd, vd)
    y_b = o_b.reshape(B, S, dh) @ w_o_dil

    g = jax.nn.sigmoid((gate + b_gate).astype(jnp.float32)).astype(x.dtype)
    g = g.reshape(B, S, N_BRANCH_2, D_MODEL)
    x = x + (g[:, :, 0] * y_a + g[:, :, 1] * y_b) @ w_o

    gt, up = jnp.split(rms_norm_2(x, g_ffn) @ w_gate_up, 2, axis=-1)
    return x + (jax.nn.silu(gt) * up) @ w_down

def second_inputs(seed: int = 0) -> dict:
    key = jax.random.key(seed)
    ks = jax.random.split(key, 22)

    def dense(k, fan_in, fan_out):
        return jax.random.normal(k, (DEPTH, fan_in, fan_out), jnp.float32) * fan_in ** -0.5

    def gain(k, n):
        return 1.0 + 0.05 * jax.random.normal(k, (DEPTH, n), jnp.float32)

    return {
        "x": jax.random.normal(ks[0], (BATCH, SEQ, D_MODEL), jnp.float32),
        "g_mix": gain(ks[1], D_MODEL),
        "w_in": dense(ks[2], D_MODEL, D_IN),
        "b_gate": 0.02 * jax.random.normal(ks[3], (DEPTH, N_BRANCH_2 * D_MODEL), jnp.float32),
        "g_cq": gain(ks[4], Q_LORA),
        "w_uq": dense(ks[5], Q_LORA, MLA_HEADS * (QK_NOPE + QK_ROPE)),
        "g_ckv": gain(ks[6], KV_LORA),
        "w_ukv": dense(ks[7], KV_LORA, MLA_HEADS * (QK_NOPE + V_DIM)),
        "g_q_nope": gain(ks[8], QK_NOPE),
        "g_q_rope": gain(ks[9], QK_ROPE),
        "g_k_nope": gain(ks[10], QK_NOPE),
        "g_k_rope": gain(ks[11], QK_ROPE),
        "g_q_dil": gain(ks[12], DIL_DIM),
        "g_k_dil": gain(ks[13], DIL_DIM),
        "w_o_mla": dense(ks[14], MLA_HEADS * V_DIM, D_MODEL),
        "w_o_dil": dense(ks[15], DIL_HEADS * DIL_DIM, D_MODEL),
        "w_o": dense(ks[16], D_MODEL, D_MODEL),
        "g_ffn": gain(ks[17], D_MODEL),
        "w_gate_up": dense(ks[18], D_MODEL, 2 * D_FF),
        "w_down": dense(ks[19], D_FF, D_MODEL),
    }

def second_block(x, g_mix, w_in, b_gate, g_cq, w_uq, g_ckv, w_ukv,
              g_q_nope, g_q_rope, g_k_nope, g_k_rope, g_q_dil, g_k_dil,
              w_o_mla, w_o_dil, w_o, g_ffn, w_gate_up, w_down):
    cos, sin = rope_tables(x.shape[1])
    for i in range(DEPTH):
        x = hybrid_layer(x, cos, sin, g_mix[i], w_in[i], b_gate[i], g_cq[i], w_uq[i],
                         g_ckv[i], w_ukv[i], g_q_nope[i], g_q_rope[i], g_k_nope[i],
                         g_k_rope[i], g_q_dil[i], g_k_dil[i], w_o_mla[i], w_o_dil[i],
                         w_o[i], g_ffn[i], w_gate_up[i], w_down[i])
    return x


def setup_inputs(seed=0):
    out = dict(first_inputs(seed))
    for name, value in second_inputs(seed + 1).items():
        if name != "x":
            out[name + "_2"] = value
    return out


def reference(
    x, mix_norm, w_in, s5_lam_re, s5_lam_im, s5_log_dt, s5_b_re, s5_b_im, s5_c_re, s5_c_im,
    s5_d, s5_w_glu, s5_b_glu, hg_lower_bounds, hg_norm, ml_conv_w, ml_conv_b, ml_w_qk, ml_b_ig,
    ml_b_fg, ml_norm, w_branch, w_out, ffn_norm, ffn_w_up, ffn_conv_w, ffn_conv_b, ffn_w_down,
    final_norm, g_mix_2, w_in_2, b_gate_2, g_cq_2, w_uq_2, g_ckv_2, w_ukv_2, g_q_nope_2,
    g_q_rope_2, g_k_nope_2, g_k_rope_2, g_q_dil_2, g_k_dil_2, w_o_mla_2, w_o_dil_2, w_o_2,
    g_ffn_2, w_gate_up_2, w_down_2,
):
    x = first_block(
        x, mix_norm, w_in, s5_lam_re, s5_lam_im, s5_log_dt, s5_b_re, s5_b_im, s5_c_re, s5_c_im,
        s5_d, s5_w_glu, s5_b_glu, hg_lower_bounds, hg_norm, ml_conv_w, ml_conv_b, ml_w_qk,
        ml_b_ig, ml_b_fg, ml_norm, w_branch, w_out, ffn_norm, ffn_w_up, ffn_conv_w, ffn_conv_b,
        ffn_w_down, final_norm,
    )
    return second_block(
        x, g_mix_2, w_in_2, b_gate_2, g_cq_2, w_uq_2, g_ckv_2, w_ukv_2, g_q_nope_2, g_q_rope_2,
        g_k_nope_2, g_k_rope_2, g_q_dil_2, g_k_dil_2, w_o_mla_2, w_o_dil_2, w_o_2, g_ffn_2,
        w_gate_up_2, w_down_2,
    )


_drawn_inputs = setup_inputs


def setup_inputs(seed=0):
    import zlib

    import numpy as np

    out = dict(_drawn_inputs(seed))
    spreads = {}
    factors = {'g_mix_2': 8.0,
     'b_gate_2': 8.0,
     'g_cq_2': 8.0,
     'w_uq_2': 8.0,
     'g_ckv_2': 8.0,
     'w_ukv_2': 6.286,
     'g_q_nope_2': 8.0,
     'g_q_rope_2': 8.0,
     'g_k_nope_2': 8.0,
     'g_k_rope_2': 8.0,
     'g_q_dil_2': 64.0,
     'g_k_dil_2': 64.0,
     'w_o_mla_2': 6.285,
     'g_ffn_2': 29.765}
    for name, (base, spread) in spreads.items():
        noise = np.random.default_rng([zlib.crc32(name.encode()), seed]).standard_normal(out[name].shape)
        drawn = base * np.exp(spread * noise) if base else spread * noise
        out[name] = __import__('jax').numpy.asarray(drawn.astype(out[name].dtype))
    for name, factor in factors.items():
        out[name] = (out[name] * factor).astype(out[name].dtype)
    return out
```

```python
from contextlib import ExitStack

import numpy as np
import concourse.bass as bass
from concourse import mybir

F32 = mybir.dt.float32
I32 = mybir.dt.int32
ALU = mybir.AluOpType
ACT = mybir.ActivationFunctionType
AX = mybir.AxisListType

P = 128
T = 256
TB = T // P
D = 2048
KT = D // P
EPS = 1e-6
RING = 4
UNIT = KT * P

S5_TILES = 4
S5_STATES = 16
S5_STEPS = 8
HG = 6
ML = 4
ML_DH = 192
ML_TILES = 6
FF = 5632
FF_TILES = FF // P
DOWN = FF_TILES // 4
HEADS = 8
SLOPES = [2.0 ** -(h + 1) for h in range(HEADS)]
MASKED = -1e30
TWO_PI = 2 * np.pi
PI_HI, PI_MID = 6.28125, 0.0019350051879882812
PI_LO = TWO_PI - PI_HI - PI_MID
ROUND = 1.5 * 2 ** 23
PI_IN = 3.1415925

VEC = [("mix_norm", 16), ("final_norm", 16), ("ffn_norm", 16), ("g_mix", 16), ("g_ffn", 16),
       ("b_gate", 32), ("ffn_conv", 4 * 88), ("ml_conv", 5 * 6), ("s5_d", 4), ("b_glu", 4), ("hg_lb", 6),
       ("hg_norm", 6), ("ml_norm", 6), ("g_cq", 4), ("g_ckv", 4), ("g_q_nope", 1), ("g_k_nope", 1),
       ("g_q_rope", 2), ("g_k_rope", 2), ("g_q_dil", 1), ("g_k_dil", 1), ("lam_re", 16), ("lam_im", 16),
       ("log_dt", 16), ("b_ig", 1), ("b_fg", 1)]
VAT, _n = {}, 0
for _name, _w in VEC:
    VAT[_name] = _n
    _n += _w
VCOLS = _n

U0, CX0, F0, O0, Q0, OG0 = 0, 4, 10, 16, 22, 28
M_TILES = 34

PIECES = []
for _h in range(ML):
    _j = 3 * (_h // 2)
    PIECES.append([(_j, 0, 128, 0), (_j + 1, 0, 64, 128)] if _h % 2 == 0
                  else [(_j + 1, 64, 128, 0), (_j + 2, 0, 128, 64)])


class Count:

    def __init__(self, sem):
        self.sem, self.base, self.i, self.per, self.k = sem, 0, None, 0, 0

    def add(self, n=1):
        self.k += n

    def value(self):
        if self.i is None or self.per == 0:
            return self.base + self.k
        return self.i * self.per + (self.base + self.k)

    def enter(self, i, per):
        self.base, self.k, self.i, self.per = self.base + self.k, 0, i, per

    def leave(self, rounds):
        assert self.k == self.per, (self.k, self.per)
        self.base, self.k, self.i, self.per = self.base + self.per * rounds, 0, None, 0


class Units:

    def __init__(self, landed, consumed, drained):
        self.pos = 0
        self.landed = [Count(s) for s in landed]
        self.consumed = [Count(s) for s in consumed]
        self.drained = [Count(s) for s in drained]

    def next(self, drained=True):
        s = self.pos % RING
        self.pos += 1
        self.landed[s].add(16)
        before, free = self.consumed[s].value(), self.drained[s].value()
        self.consumed[s].add()
        if drained:
            self.drained[s].add()
        return s, self.landed[s].value(), before, self.consumed[s].value(), free

    def enter(self, i, turns=1, drained=1):
        for c in self.landed:
            c.enter(i, 16 * turns)
        for c in self.consumed:
            c.enter(i, turns)
        for c in self.drained:
            c.enter(i, turns * drained)

    def leave(self, n):
        for c in self.landed + self.consumed + self.drained:
            c.leave(n)

    def skip(self, n, drained=True):
        for _ in range(n):
            self.next(drained)

    def all_drained(self):
        return [(c.sem, c.value()) for c in self.drained]


def build(nc, t, out):
    with ExitStack() as ctx:
        def sb(name, shape, dt=F32):
            return ctx.enter_context(nc.sbuf_tensor(name, shape, dt))

        ring = sb("ring", [P, RING, UNIT])
        xT = sb("xT", [P, KT, T])
        hT = sb("hT", [P, KT, T])
        vec = sb("vec", [P, VCOLS])
        cst = sb("cst", [P, 5, P])
        sel = sb("sel", [ML, ML, P])
        w_if = sb("w_if", [P, KT, 8])
        ones = sb("ones", [P, P])
        acol = sb("acol", [P, TB, ML])
        lb = sb("lb", [P, 4, HG])
        s5c = sb("s5c", [P, 16, S5_STATES])
        s5p = sb("s5p", [P, S5_STEPS, 3, S5_STATES])
        small = sb("small", [P, 2, 8])
        xms = sb("xms", [P, T])
        xrs = sb("xrs", [P, T])
        xtmp = sb("xtmp", [P, T])
        ARENA = nc.sbuf_bytes_remaining // 4 // 16 * 16
        arena = sb("arena", [P, ARENA])

        def tiles(at, n):
            assert at + n * T <= ARENA, (at + n * T, ARENA)
            return arena[:, at:at + n * T].rearrange("p (k t) -> p k t", t=T)

        MT = tiles(0, M_TILES)
        VN = arena[:, 34 * T:46 * T].rearrange("p (b h c) -> p b h c", b=TB, c=P)
        G = tiles(46 * T, 48)
        W = 94 * T
        CA, QH, KH = tiles(W, 6), tiles(W + 6 * T, 6), tiles(W + 12 * T, 6)
        rows = arena[0:ML, W + 18 * T:W + 24 * T].rearrange("p (k t) -> p k t", t=T)
        MB, TH = tiles(W + 24 * T, 4), tiles(W + 28 * T, 4)
        PM = arena[:, W:W + 6 * T].rearrange("p (h c) -> p h c", h=ML)
        HH, MSQ, MMS, MRS = CA, QH, KH[:, 0:4], MB
        HK, HPR, HX1 = tiles(W, 6), tiles(W + 6 * T, 6), tiles(W + 12 * T, 6)
        HX0, HF, HQ = MT[:, CX0:CX0 + 6], MT[:, F0:F0 + 6], MT[:, Q0:Q0 + 6]
        PD = tiles(W + 18 * T, 6)
        PO = arena[:, W + 24 * T:W + 27 * T].rearrange("p (h c) -> p h c", h=HG)
        HRS = tiles(W, 6)
        hmask = arena[:, W + 32 * T:W + 36 * T].bitcast(I32).rearrange("p (l c) -> p l c", l=8)
        HO, HSQ, HMS = HX1, HX0, HF
        SR = tiles(W, S5_STATES)
        SI = tiles(OG0 * T, S5_STATES)
        pads = arena[:, W + 16 * T:W + 22 * T].rearrange("p (n c) -> p n c", n=4)
        GA = tiles(W + 24 * T, 4)
        ACTS = tiles(0, FF_TILES)
        cv = tiles(46 * T, 8)
        P2 = tiles(0, 26)
        VD = arena[:, 26 * T:34 * T].rearrange("p (b h c) -> p b h c", b=TB, c=P)
        G2 = tiles(34 * T, 32)
        QN, QR, KN = tiles(66 * T, 8), tiles(74 * T, 4), tiles(78 * T, 8)
        VM = arena[:, 86 * T:94 * T].rearrange("p (b h c) -> p b h c", b=TB, c=P)
        SQ, MS, RS = tiles(94 * T, 8), tiles(102 * T, 8), tiles(110 * T, 8)
        band = tiles(118 * T, 6)
        CQ, CKV, KR = P2[:, 0:4], P2[:, 4:8], P2[:, 8:10]
        QD, KD = P2[:, 10:18], P2[:, 18:26]
        OA = P2[:, 0:8]
        ES = [SQ[:, 0:2], SQ[:, 2:4]]
        PS = [SQ[:, 4:6], SQ[:, 6:8]]
        BS = [MS[:, 0:2], MS[:, 2:4]]

        bank = [ctx.enter_context(nc.psum_tensor(f"bank{i}", [P, 2, T], F32)) for i in range(8)]
        bank_row = [b[:].rearrange("p a t -> p (a t)") for b in bank]

        def sem(name):
            return ctx.enter_context(nc.semaphore(name))

        landed = [sem(f"unit_landed{s}") for s in range(RING)]
        consumed = [sem(f"unit_consumed{s}") for s in range(RING)]
        drained = [sem(f"bank_drained{s}") for s in range(RING)]
        x_landed, vec_landed, cst_landed = sem("x_landed"), sem("vec_landed"), sem("cst_landed")
        hmask_landed, band_landed, x_stored = sem("hmask_landed"), sem("band_landed"), sem("x_stored")
        ones_set = sem("ones_set")
        dve_chain, act_chain = sem("dve_chain"), sem("act_chain")
        norm_squared, norm_summed = sem("norm_squared"), sem("norm_summed")
        norm_mean, norm_rooted, norm_done = sem("norm_mean"), sem("norm_rooted"), sem("norm_done")
        conv_ready, conv_act, qk_ready = sem("ml_conv_ready"), sem("ml_conv_act"), sem("ml_qk_ready")
        if_summed, rows_abs, rows_log, rows_ready, rows_thr = (sem("ml_if_summed"), sem("ml_rows_abs"),
                                                               sem("ml_rows_log"), sem("ml_rows_ready"),
                                                               sem("ml_rows_threshold"))
        cast_done, cast_taken = sem("ml_broadcast_done"), sem("ml_broadcast_taken")
        ml_scored, ml_arg, ml_exp, ml_p = sem("ml_scored"), sem("ml_arg"), sem("ml_exp"), sem("ml_p")
        ml_den, ml_rden, ml_num, ml_h = sem("ml_den"), sem("ml_rden"), sem("ml_num"), sem("ml_h")
        ml_done = sem("ml_done")
        hg_x, hg_scored, hg_taken, hg_out, hg_kept = (sem("hg_x"), sem("hg_scored"), sem("hg_taken"),
                                                      sem("hg_out"), sem("hg_kept"))
        hg_done = sem("hg_done")
        lb_arg, lb_exp = sem("hg_bound_arg"), sem("hg_bound_exp")
        s5_arg, s5_fn = sem("s5_arg"), sem("s5_function")
        s5_fed, s5_in, s5_states = sem("s5_fed"), sem("s5_input_kept"), sem("s5_states")
        s5_pre, s5_gelu = sem("s5_pre"), sem("s5_gelu")
        s5_gate, s5_done = sem("s5_gate"), sem("s5_done")
        silu_pair, ff_done = sem("silu_pair"), sem("ff_act_done")
        down_drained = [sem(f"down_drained{b}") for b in range(2)]
        at_scored, at_max, at_exp, at_p = sem("at_scored"), sem("at_max"), sem("at_exp"), sem("at_p")
        at_turned, at_pt, at_out, at_kept = sem("at_turned"), sem("at_pt"), sem("at_out"), sem("at_kept")
        at_bias, at_sum = sem("at_bias"), sem("at_biased")

        block = ctx.enter_context(nc.Block())

        def v(name, n=0, rows_=P):
            c = VAT[name] + n
            return vec[0:rows_, c:c + 1]

        def all_tiles(sq, n):
            return [[(ones[:], sq[:, k]) for k in range(n)]]

        def each_tile(sq, n):
            return [[(ones[:], sq[:, k])] for k in range(n)]

        blk32, ident, causal = cst[:, 0], cst[:, 1], cst[:, 2]
        NORMS = [
            dict(src=xT, sq=hT, ms=xms, rs=xrs, groups=all_tiles(hT, KT), n=D),
            dict(src=HH, sq=MSQ, ms=MMS, rs=MRS, n=ML_DH, groups=[
                [(cst[:, 3 + a // 64] if b - a < P else ones[:], MSQ[:, k]) for k, a, b, _ in PIECES[h]]
                for h in range(ML)]),
            dict(src=HO, sq=HSQ, ms=HMS, rs=HRS, groups=each_tile(HSQ, HG), n=P),
            dict(src=xT, sq=hT, ms=xms, rs=xrs, groups=all_tiles(hT, KT), n=D),
            dict(src=xT, sq=hT, ms=xms, rs=xrs, groups=all_tiles(hT, KT), n=D),
            dict(src=xT, sq=hT, ms=xms, rs=xrs, groups=all_tiles(hT, KT), n=D),
            dict(src=CQ, sq=SQ[:, 0:4], ms=MS[:, 0:1], rs=RS[:, 0:1], groups=all_tiles(SQ, 4), n=512),
            dict(src=CKV, sq=SQ[:, 0:4], ms=MS[:, 0:1], rs=RS[:, 0:1], groups=all_tiles(SQ, 4), n=512),
            dict(src=KR, sq=SQ[:, 0:2], ms=MS[:, 0:1], rs=RS[:, 0:1], n=64,
                 groups=[[(blk32, SQ[:, 0]), (blk32, SQ[:, 1])]]),
            dict(src=QD, sq=SQ, ms=MS, rs=RS, groups=each_tile(SQ, HEADS), n=P),
            dict(src=KD, sq=SQ, ms=MS, rs=RS, groups=each_tile(SQ, HEADS), n=P),
            dict(src=QN, sq=SQ, ms=MS, rs=RS, groups=each_tile(SQ, HEADS), n=P),
            dict(src=QR, sq=SQ[:, 0:4], ms=MS[:, 0:2], rs=RS[:, 0:2], n=64,
                 groups=[[(blk32, SQ[:, g]), (blk32, SQ[:, 2 + g])] for g in range(2)]),
            dict(src=KN, sq=SQ, ms=MS, rs=RS, groups=each_tile(SQ, HEADS), n=P),
            dict(src=xT, sq=hT, ms=xms, rs=xrs, groups=all_tiles(hT, KT), n=D),
        ]

        @block.sync
        def _(sp):
            units = Units(landed, consumed, drained)
            sp.dma_start(xT[:], t["xT"]).then_inc(x_landed, 16)
            sp.dma_start(vec[:], t["vec"]).then_inc(vec_landed, 16)

            def load(src, cols=UNIT):
                s, _, before, _, _ = units.next(False)
                if not isinstance(before, int) or before > 0:
                    sp.wait_ge(consumed[s], before)
                sp.dma_start(ring[:, s, 0:cols], src).then_inc(landed[s], 16)

            def stream(src, rounds, cols=UNIT):
                with sp.Fori(0, rounds) as i:
                    units.enter(i, drained=0)
                    for j in range(RING):
                        load(src[i * RING + j], cols)
                units.leave(rounds)

            w = t["w_mix"]
            for j in range(RING):
                load(w[j])
            sp.dma_start(cst[:], t["cst"]).then_inc(cst_landed, 16)
            sp.dma_start(sel[:], t["sel"]).then_inc(cst_landed, 16)
            sp.dma_start(w_if[:], t["w_if"]).then_inc(cst_landed, 16)
            sp.dma_start(hmask, t["hmask"]).then_inc(hmask_landed, 16)
            for j in range(RING, 10):
                load(w[j])
            stream(w[10:46], 9)
            for part in range(2):
                load(t["w_qk"][part], 8 * ML_DH)
            stream(t["w_gates"][0:24], 6)
            for part in range(2):
                load(t["s5_b"][part])
            stream(t["w_gates"][24:48], 6)
            for part in range(2):
                load(t["s5_c"][part])
            load(t["w_glu"][0])
            stream(t["w_branch"], 4)
            stream(t["w_out"], 4)
            stream(t["w_up"], 22)
            stream(t["w_down"], 16, DOWN * P)
            stream(t["w_in2"][0:24], 6)
            sp.wait_ge(norm_done, 6)
            sp.dma_start(band, t["band"]).then_inc(band_landed, 16)
            for j in (24, 25):
                load(t["w_in2"][j])
            stream(t["w_in2"][26:34], 2)
            for j in range(3):
                load(t["w_uq"][j])
            for j in range(4):
                load(t["w_ukv"][j])
            stream(t["w_in2"][34:66], 8)
            stream(t["w_mix2"], 4)
            stream(t["w_o2"], 4)
            stream(t["w_up2"], 22)
            stream(t["w_down2"], 16, DOWN * P)
            for b in range(2):
                sp.wait_ge(down_drained[b], 1 + 2 * KT // 2)
            sp.dma_start(out, xT[:]).then_inc(x_stored, 16)
            sp.wait_ge(x_stored, 16)

        @block.tensor
        def _(pe):
            units = Units(landed, consumed, drained)
            down_free = [Count(s) for s in down_drained]
            for c in down_free:
                c.base = 1
            norm = [0]

            def mm(o, lhsT, rhs, first=True, last=True):
                return nc.tensor.matmul(o, lhsT, rhs, start=first, stop=last)

            def take():
                s, there, _, _, _ = units.next(False)
                pe.wait_ge(landed[s], there)
                return s

            def unit(body):
                s, there, _, _, free = units.next()
                pe.wait_ge(landed[s], there)
                if not isinstance(free, int) or free > 0:
                    pe.wait_ge(drained[s], free)
                body(s).then_inc(consumed[s], 1)

            def rounds(n, body):
                with pe.Fori(0, n) as i:
                    units.enter(i)
                    for j in range(RING):
                        unit(body)
                units.leave(n)

            def project(s):
                for k in range(KT):
                    last = mm(bank[s][:, 0], ring[:, s, k * P:(k + 1) * P], hT[:, k], k == 0, k == KT - 1)
                return last

            def project_tokens(s):
                for b in range(TB):
                    for k in range(KT):
                        last = mm(bank[s][:, b, 0:P], hT[:, k, b * P:(b + 1) * P], ring[:, s, k * P:(k + 1) * P],
                                  k == 0, k == KT - 1)
                return last

            def drained_all():
                for s, n in units.all_drained():
                    pe.wait_ge(s, n)

            def sum_squares():
                n = NORMS[norm[0]]
                norm[0] += 1
                pe.wait_ge(norm_squared, norm[0])
                for g, parts in enumerate(n["groups"]):
                    for k, (one, sq) in enumerate(parts):
                        last = mm(bank[4 + g // 2][:, g % 2], one, sq, k == 0, k == len(parts) - 1)
                last.then_inc(norm_summed, 1)

            def banks_back():
                pe.wait_ge(norm_mean, norm[0])

            def down():
                with pe.Fori(0, 8) as i:
                    units.enter(i, turns=2, drained=0)
                    for c in down_free:
                        c.enter(i, 1)
                    for b in range(2):
                        pe.wait_ge(down_drained[b], down_free[b].value())
                        down_free[b].add()
                        for q in range(4):
                            s = take()
                            for k in range(DOWN):
                                last = mm(bank[4 + b][:, 0], ring[:, s, k * P:(k + 1) * P], ACTS[:, q * DOWN + k],
                                          q == 0 and k == 0, q == 3 and k == DOWN - 1)
                            last.then_inc(consumed[s], 1)
                units.leave(8)
                for c in down_free:
                    c.leave(8)

            pe.wait_ge(ones_set, 1)
            sum_squares()
            pe.wait_ge(norm_done, 1)
            for j in range(10):
                unit(project)
            rounds(3, project_tokens)
            rounds(6, project)

            pe.wait_ge(cst_landed, 48)
            for g in range(2):
                for k in range(KT):
                    last = mm(bank[7][0:ML, g], w_if[:, k, g * ML:(g + 1) * ML], hT[:, k], k == 0, k == KT - 1)
            last.then_inc(if_summed, 1)

            pe.wait_ge(conv_act, 1)
            for part in range(2):
                s = take()
                if part:
                    pe.wait_ge(qk_ready, 1)
                for h in range(ML):
                    for o, q0, q1, e in PIECES[h]:
                        for n, (k, _, _, _) in enumerate(PIECES[h]):
                            c = (2 * h + n) * ML_DH + e
                            last = mm(bank[4 + o // 2][q0:q1, o % 2], ring[:, s, c:c + q1 - q0], CA[:, k],
                                      n == 0, n == 1)
                last.then_inc(consumed[s], 1)
            rounds(1, project)

            pe.wait_ge(rows_ready, 1)
            pe.wait_ge(qk_ready, 2)
            for b in range(TB):
                mm(bank[4][:, 0, b * ML:(b + 1) * ML], rows[:, 2, b * P:(b + 1) * P], ident[0:ML, 0:ML])
            for h in range(ML):
                last = mm(bank[5 + h // 2][:, h % 2], sel[:, h], rows[:, 3])
            last.then_inc(cast_done, 1)
            pe.wait_ge(rows_thr, 1)
            pe.wait_ge(cast_taken, 1)
            for h in range(ML):
                last = mm(bank[5 + h // 2][:, h % 2], sel[:, h], rows[:, 5])
            last.then_inc(cast_done, 1)
            pe.wait_ge(cast_taken, 2)
            for h in range(ML):
                for b in range(TB):
                    for n, (k, p0, p1, _) in enumerate(PIECES[h]):
                        last = mm(bank[4 + h][:, b, b * P:T], KH[p0:p1, k, b * P:(b + 1) * P],
                                  QH[p0:p1, k, b * P:T], n == 0, n == 1)
                last.then_inc(ml_scored, 1)
            rounds(1, project)
            pe.wait_ge(ml_p, ML)
            for h in range(ML):
                mm(bank[4 + h // 2][:, h % 2], ones[:], PM[:, h, 0:T], True, False)
                last = mm(bank[4 + h // 2][:, h % 2, P:T], ones[:], PM[:, h, T:T + P], False, True)
            last.then_inc(ml_den, 1)
            pe.wait_ge(ml_rden, 1)
            vals = VN[:, :, 6:12].rearrange("p b h c -> p b (h c)")
            for h in range(ML):
                for k, p0, p1, e in PIECES[h]:
                    c = h * ML_DH + e
                    mm(bank[4 + k // 2][p0:p1, k % 2], vals[:, 0, c:c + p1 - p0], PM[:, h, 0:T], True, False)
                    last = mm(bank[4 + k // 2][p0:p1, k % 2, P:T], vals[:, 1, c:c + p1 - p0],
                              PM[:, h, T:T + P], False, True)
            last.then_inc(ml_num, 1)
            rounds(1, project)
            sum_squares()
            banks_back()

            for lvl in range(9):
                pe.wait_ge(hg_x, lvl + 1)
                if lvl:
                    pe.wait_ge(hg_taken, lvl)
                X = [HX0, HX1][lvl % 2]
                for h in range(HG):
                    if lvl == 8:
                        last = mm(bank_row[4 + h // 4][:, h % 4 * P:(h % 4 + 1) * P], X[:, h, 0:P], X[:, h, P:T])
                    else:
                        for b in range(TB):
                            c = slice(b * P, (b + 1) * P)
                            last = mm(bank[4 + h // 2][:, h % 2, c], (X if lvl else HK)[:, h, c],
                                      (X if lvl else HQ)[:, h, c])
                last.then_inc(hg_scored, 1)
                if lvl in (1, 4):
                    rounds(1, project)
            pe.wait_ge(hg_taken, 9)
            for h in range(HG):
                mm(bank[4 + h // 2][:, h % 2, 0:P], VN[:, 0, h], PD[:, h, 0:P])
                mm(bank[4 + h // 2][:, h % 2, P:T], VN[:, 0, h], PO[:, h], True, False)
                last = mm(bank[4 + h // 2][:, h % 2, P:T], VN[:, 1, h], PD[:, h, P:T], False, True)
            last.then_inc(hg_out, 1)
            rounds(1, project)
            sum_squares()
            banks_back()

            sre, sim_ = take(), take()
            pe.wait_ge(norm_done, 3)
            for n in range(S5_STATES):
                if n >= 4:
                    pe.wait_ge(s5_in, n - 3)
                c = slice(n * P, (n + 1) * P)
                last = mm(bank[4 + n % 4][:, 0], ring[:, sre, c], MT[:, U0 + n // 4])
                if n == S5_STATES - 1:
                    last.then_inc(consumed[sre], 1)
                last = mm(bank[4 + n % 4][:, 1], ring[:, sim_, c], MT[:, U0 + n // 4])
                last.then_inc(consumed[sim_] if n == S5_STATES - 1 else s5_fed, 1)
            rounds(6, project)

            cre, cim = take(), take()
            pe.wait_ge(s5_states, S5_STATES)
            for f in range(S5_TILES):
                for part, (slot, st) in enumerate(((cre, SR), (cim, SI))):
                    for n in range(4):
                        c = (4 * f + n) * P
                        last = mm(bank[4 + f][:, part], ring[:, slot, c:c + P], st[:, 4 * f + n], n == 0, n == 3)
                    if f == S5_TILES - 1:
                        last.then_inc(consumed[slot], 1)
            pe.wait_ge(s5_gelu, 1)
            s = take()
            for f in range(S5_TILES):
                for k in range(S5_TILES):
                    c = (f * S5_TILES + k) * P
                    last = mm(bank[4 + f // 2][:, f % 2], ring[:, s, c:c + P], GA[:, k], k == 0, k == 3)
            last.then_inc(consumed[s], 1)

            Y = [MT[:, U0 + k] for k in range(4)] + [HQ[:, k] for k in range(6)] + [MT[:, O0 + k] for k in range(6)]

            def branches(s):
                for o, lo, hi in ((bank[s][:, 0], 0, 4), (bank[s][:, 1], 4, 10), (bank[4 + s][:, 0], 10, 16)):
                    for k in range(lo, hi):
                        last = mm(o, ring[:, s, k * P:(k + 1) * P], Y[k], k == lo, k == hi - 1)
                return last

            pe.wait_ge(s5_done, 1)
            rounds(4, branches)
            drained_all()
            rounds(4, project)
            sum_squares()
            pe.wait_ge(norm_done, 4)
            rounds(22, project)
            pe.wait_ge(ff_done, FF_TILES)
            down()
            sum_squares()
            banks_back()
            sum_squares()
            pe.wait_ge(norm_done, 6)
            rounds(6, project)
            unit(project)
            unit(project)
            rounds(2, project_tokens)
            sum_squares()
            banks_back()
            sum_squares()
            banks_back()

            def latent(src):
                def body(s):
                    for o in range(4):
                        for k in range(4):
                            c = (o * 4 + k) * P
                            last = mm(bank[s if o < 2 else 4 + s][:, o % 2], ring[:, s, c:c + P], src[:, k],
                                      k == 0, k == 3)
                    return last
                return body

            def latent_tokens(s):
                for b in range(TB):
                    for k in range(4):
                        last = mm(bank_row[s + 4 * b], CKV[:, k, b * P:(b + 1) * P],
                                  ring[:, s, k * 512:(k + 1) * 512], k == 0, k == 3)
                return last

            pe.wait_ge(norm_done, 8)
            for j in range(3):
                unit(latent(CQ))
            for j in range(2):
                unit(latent(CKV))
            for j in range(2):
                unit(latent_tokens)
            drained_all()
            for j in range(6):
                sum_squares()
                banks_back()
                if j in (0, 2, 4):
                    rounds(1, project)

            pe.wait_ge(norm_done, 14)

            def scores(h):
                if h >= 2:
                    pe.wait_ge(at_exp, h - 1)
                for b in range(TB):
                    c = slice(b * P, (b + 1) * P)
                    if h < HEADS:
                        r = slice(32 * (h % 4), 32 * (h % 4) + 32)
                        mm(bank[4 + h % 2][:, b], QN[:, h, c], KN[:, h], True, False)
                        mm(bank[4 + h % 2][:, b], QR[r, h // 4, c], KR[r, 0], False, False)
                        last = mm(bank[4 + h % 2][:, b], QR[r, 2 + h // 4, c], KR[r, 1], False, True)
                    else:
                        last = mm(bank[4 + h % 2][:, b], QD[:, h - HEADS, c], KD[:, h - HEADS])
                last.then_inc(at_scored, 1)

            scores(0)
            for h in range(2 * HEADS):
                if h + 1 < 2 * HEADS:
                    scores(h + 1)
                if h in (0, 3, 6, 9, 12):
                    rounds(1, project)
                pe.wait_ge(at_p, h + 1)
                if h:
                    pe.wait_ge(at_pt, h)
                for b in range(TB):
                    for c in range(TB):
                        last = nc.tensor.transpose(bank[6][:, c, b * P:(b + 1) * P],
                                                   ES[h % 2][:, b, c * P:(c + 1) * P], ident)
                last.then_inc(at_turned, 1)
                pe.wait_ge(at_pt, h + 1)
                if h:
                    pe.wait_ge(at_kept, h)
                for b in range(TB):
                    last = mm(bank[7][:, 0], (VM if h < HEADS else VD)[:, b, h % HEADS], PS[h % 2][:, b],
                              b == 0, b == TB - 1)
                last.then_inc(at_out, 1)

            def branches2(s):
                for half, y in enumerate((OA, QD)):
                    for k in range(HEADS):
                        c = (half * HEADS + k) * P
                        last = mm(bank[s][:, half], ring[:, s, c:c + P], y[:, k], k == 0, k == HEADS - 1)
                return last

            pe.wait_ge(at_kept, 2 * HEADS)
            rounds(4, branches2)
            drained_all()
            rounds(4, project)
            sum_squares()
            pe.wait_ge(norm_done, 15)
            rounds(22, project)
            drained_all()
            down()

        @block.scalar
        def _(act):
            units = Units(landed, consumed, drained)
            chain = Count(act_chain)
            norm = [0]
            A = nc.scalar.activation

            def link(ins):
                ins.then_inc(act_chain, 1)
                chain.add()
                act.wait_ge(act_chain, chain.value())

            def drain(body):
                s, _, _, there, _ = units.next()
                act.wait_ge(consumed[s], there)
                body(s).then_inc(drained[s], 1)

            def rounds(n, body):
                with act.Fori(0, n) as i:
                    units.enter(i)
                    for j in range(RING):
                        drain(lambda s: body(s, i * RING + j))
                units.leave(n)

            def skip(n, turns=1, kept=True):
                units.skip(n * RING * turns, kept)

            def square():
                n = NORMS[norm[0]]
                norm[0] += 1
                if norm[0] > 1:
                    act.wait_ge(norm_done, norm[0] - 1)
                A(n["sq"][:] if n["sq"] is hT else n["sq"], n["src"][:] if n["src"] is xT else n["src"],
                  ACT.Square).then_inc(norm_squared, 1)

            def root():
                n = NORMS[norm[0] - 1]
                act.wait_ge(norm_mean, norm[0])
                m, r = ((n[k][:] if n[k] in (xms, xrs) else n[k]) for k in ("ms", "rs"))
                A(r, m, ACT.Sqrt).then_inc(norm_rooted, 1)

            def drained_all():
                for s, n in units.all_drained():
                    act.wait_ge(s, n)

            act.wait_ge(x_landed, 16)
            square()
            root()
            act.wait_ge(vec_landed, 16)
            c = VAT["log_dt"]
            A(s5c[:, 0], vec[:, c:c + S5_STATES], ACT.Exp).then_inc(s5_fn, 1)
            act.wait_ge(s5_arg, 1)
            A(s5c[:, 7], s5c[:, 1], ACT.Exp)
            act.wait_ge(lb_arg, 1)
            A(lb[:, 1], lb[:, 0], ACT.Exp).then_inc(lb_exp, 1)
            A(s5c[:, 8], s5c[:, 4], ACT.Sin)
            A(s5c[:, 9], s5c[:, 6], ACT.Sin).then_inc(s5_fn, 1)

            for j in range(10):
                drain(lambda s: A(MT[:, U0 + j], bank[s][:, 0], ACT.Copy))
            rounds(3, lambda s, n: A(VN[:, :, bass.ds(n, 1)].rearrange("p a b c -> p a (b c)"),
                                     bank[s][:, :, 0:P], ACT.Copy))
            rounds(3, lambda s, n: A(MT[:, bass.ds(n + F0, 1)], bank[s][:, 0:1], ACT.Sigmoid))
            rounds(3, lambda s, n: A(MT[:, bass.ds(n + Q0, 1)], bank[s][:, 0:1], ACT.Silu))

            def gates(at, n):
                def body(s, m):
                    if isinstance(m, int):
                        return A(G[:, at + m], bank[s][:, 0], ACT.Sigmoid)
                    return A(G[:, bass.ds(m + at, 1)], bank[s][:, 0:1], ACT.Sigmoid)
                rounds(n, body)

            act.wait_ge(conv_ready, 1)
            A(CA, CA, ACT.Silu).then_inc(conv_act, 1)
            act.wait_ge(rows_abs, 1)
            link(A(rows[:, 0], rows[:, 0], ACT.Exp, scale=-1.0))
            A(rows[:, 0], rows[:, 0], ACT.Ln, bias=1.0).then_inc(rows_log, 1)
            for dst, scale in ((QH, 1.0), (KH, ML_DH ** -0.5)):
                s, _, _, there, _ = units.next(False)
                act.wait_ge(consumed[s], there)
                for j in range(3):
                    last = A(dst[:, 2 * j:2 * j + 2], bank[4 + j][:], ACT.Copy, scale=scale)
                last.then_inc(qk_ready, 1)
            act.wait_ge(rows_ready, 1)
            A(rows[:, 5], rows[:, 4], ACT.Exp, scale=-1.0).then_inc(rows_thr, 1)
            gates(0, 1)
            act.wait_ge(cast_done, 1)
            A(acol[:], bank[4][:, 0, 0:TB * ML].rearrange("p (b h) -> p b h", h=ML), ACT.Copy)
            for j in range(2):
                last = A(MB[:, 2 * j:2 * j + 2], bank[5 + j][:], ACT.Copy)
            last.then_inc(cast_taken, 1)
            act.wait_ge(cast_done, 2)
            for j in range(2):
                last = A(TH[:, 2 * j:2 * j + 2], bank[5 + j][:], ACT.Copy)
            last.then_inc(cast_taken, 1)
            for h in range(ML):
                act.wait_ge(ml_arg, h + 1)
                A(PM[:, h], PM[:, h], ACT.Exp, scale=-1.0).then_inc(ml_exp, 1)
            gates(4, 1)
            gates(8, 1)
            act.wait_ge(ml_h, 1)
            square()
            root()

            gates(12, 1)
            gates(16, 1)
            act.wait_ge(hg_out, 1)
            for j in range(3):
                last = A(HO[:, 2 * j:2 * j + 2], bank[4 + j][:], ACT.Copy)
            link(last)
            square()
            gates(20, 1)
            root()

            units.next(False)
            _s, _, _, last_fed, _ = units.next(False)
            for n in range(S5_STATES):
                if n < S5_STATES - 1:
                    act.wait_ge(s5_fed, n + 1)
                else:
                    act.wait_ge(consumed[_s], last_fed)
                A(SR[:, n], bank[4 + n % 4][:, 0], ACT.Copy)
                A(SI[:, n], bank[4 + n % 4][:, 1], ACT.Copy).then_inc(s5_in, 1)
            gates(24, 6)
            units.next(False)
            units.next(False)
            act.wait_ge(s5_pre, 1)
            A(GA, GA, ACT.Gelu_apprx_tanh).then_inc(s5_gelu, 1)
            s, _, _, there, _ = units.next(False)
            act.wait_ge(consumed[s], there)
            for f in range(S5_TILES):
                last = A(MT[:, U0 + f], bank[4 + f // 2][:, f % 2], ACT.Sigmoid, bias=v("b_glu", f))
            last.then_inc(s5_gate, 1)
            skip(8)
            drained_all()
            square()
            root()

            with act.Fori(0, 22) as i:
                units.enter(i)
                for j in range(2):
                    s, _, _, _, free = units.next()
                    units.next()
                    act.wait_ge(drained[s], free + 1)
                    A(cv[:, 2 * j], cv[:, 2 * j], ACT.Silu).then_inc(silu_pair, 1)
            units.leave(22)
            skip(16, kept=False)
            for b in range(2):
                act.wait_ge(down_drained[b], 1 + KT // 2)
            square()
            root()
            square()
            root()

            rounds(6, lambda s, n: A(P2[:, bass.ds(n, 1)], bank[s][:, 0:1], ACT.Copy))
            for j in (24, 25):
                drain(lambda s: A(P2[:, j], bank[s][:, 0], ACT.Copy))
            rounds(2, lambda s, n: A(VD[:, :, bass.ds(n, 1)].rearrange("p a b c -> p a (b c)"),
                                     bank[s][:, :, 0:P], ACT.Copy))
            drained_all()
            square()
            root()
            square()
            root()

            def two_banks(a, b):
                def body(s):
                    A(a, bank[s][:], ACT.Copy)
                    return A(b, bank[4 + s][:], ACT.Copy)
                return body

            def tokens(j):
                def body(s):
                    A(VM[:, 0, 4 * j:4 * j + 4].rearrange("p h c -> p (h c)"), bank_row[s], ACT.Copy)
                    return A(VM[:, 1, 4 * j:4 * j + 4].rearrange("p h c -> p (h c)"), bank_row[4 + s], ACT.Copy)
                return body

            for dst, j in ((QN, 0), (QN, 1), (QR, 0), (KN, 0), (KN, 1)):
                drain(two_banks(dst[:, 4 * j:4 * j + 2], dst[:, 4 * j + 2:4 * j + 4]))
            for j in range(2):
                drain(tokens(j))
            drained_all()

            def gates2(at, n):
                for j in range(RING * n):
                    drain(lambda s: A(G2[:, at + j], bank[s][:, 0], ACT.Sigmoid, bias=v("b_gate", at + j)))

            at = 0
            for j in range(6):
                square()
                root()
                if j in (0, 2, 4):
                    gates2(at, 1)
                    at += RING

            act.wait_ge(band_landed, 16)
            for h in range(2 * HEADS):
                e, p = ES[h % 2], PS[h % 2]
                if h == HEADS:
                    for g in (0, 1):
                        A(BS[g], band[:, 0:2], ACT.Copy, scale=SLOPES[g]).then_inc(at_bias, 1)
                act.wait_ge(at_max, h + 1)
                if h >= 2:
                    act.wait_ge(at_turned, h - 1)
                if h < HEADS:
                    for b in range(TB):
                        last = A(e[:, b], bank[4 + h % 2][:, b], ACT.Exp, bias=small[:, h % 2, 2 + b:3 + b],
                                 scale=192 ** -0.5, accum_out=small[:, h % 2, 4 + b:5 + b])
                else:
                    for b in range(TB):
                        last = A(e[:, b], e[:, b], ACT.Exp, bias=small[:, h % 2, 2 + b:3 + b])
                last.then_inc(at_exp, 1)
                if HEADS <= h < 2 * HEADS - 2:
                    A(BS[h % 2], band[:, 0:2], ACT.Copy, scale=SLOPES[h + 2 - HEADS]).then_inc(at_bias, 1)
                if h in (0, 3, 6, 9, 12):
                    gates2(at, 1)
                    at += RING
                act.wait_ge(at_turned, h + 1)
                if h >= 2:
                    act.wait_ge(at_out, h - 1)
                A(p, bank[6][:], ACT.Copy).then_inc(at_pt, 1)
                act.wait_ge(at_out, h + 1)
                A((OA if h < HEADS else QD)[:, h % HEADS], bank[7][:, 0], ACT.Copy).then_inc(at_kept, 1)
            skip(8)
            drained_all()
            square()
            root()
            with act.Fori(0, 22) as i:
                units.enter(i)
                for j in range(2):
                    s, _, _, there, _ = units.next()
                    su, _, _, _, used = units.next()
                    act.wait_ge(consumed[s], there)
                    act.wait_ge(drained[su], used)
                    A(cv[:, 2 * j], bank[s][:, 0], ACT.Silu).then_inc(drained[s], 1)
            units.leave(22)

        @block.vector
        def _(dve):
            V = nc.vector
            units = Units(landed, consumed, drained)
            chain = Count(dve_chain)
            norm = [0]
            M, ADD, SUB, MAX, MIN = ALU.mult, ALU.add, ALU.subtract, ALU.max, ALU.min

            def link(ins):
                ins.then_inc(dve_chain, 1)
                chain.add()
                dve.wait_ge(dve_chain, chain.value())

            def stt(o, a, s, b, op0=M, op1=M, **kw):
                return V.scalar_tensor_tensor(out=o, in0=a, scalar=s, in1=b, op0=op0, op1=op1, **kw)

            def tt(o, a, b, op=M):
                return V.tensor_tensor(o, a, b, op)

            def reciprocal_root():
                n = NORMS[norm[0]]
                norm[0] += 1
                dve.wait_ge(norm_summed, norm[0])
                G_ = len(n["groups"])
                one = n["ms"] is xms
                ms, rs = (n["ms"][:], n["rs"][:]) if one else (n["ms"], n["rs"])
                if G_ == 1:
                    last = V.tensor_scalar(ms if one else ms[:, 0], bank[4][:, 0], 1.0 / n["n"], EPS, M, ADD)
                else:
                    for j in range(G_ // 2):
                        last = V.tensor_scalar(ms[:, 2 * j:2 * j + 2], bank[4 + j][:], 1.0 / n["n"], EPS, M, ADD)
                last.then_inc(norm_mean, 1)
                dve.wait_ge(norm_rooted, norm[0])
                tmp = xtmp[:] if one else n["sq"][:, 0:G_]
                link(V.reciprocal(rs, rs))
                link(tt(tmp, ms, rs))
                link(tt(tmp, tmp, rs))
                link(V.tensor_scalar(tmp, tmp, -0.5, 1.5, M, ADD))
                link(tt(rs, rs, tmp))
                return rs

            def normalise(dst, src, gain):
                rs = reciprocal_root()
                for k in range(KT):
                    last = stt(dst[:, k], src[:, k], v(gain, k), rs)
                last.then_inc(norm_done, 1)

            def drained_all():
                for s, n in units.all_drained():
                    dve.wait_ge(s, n)

            def skip(n, kept=True):
                units.skip(n * RING, kept)

            V.memset(ones[:], 1.0).then_inc(ones_set, 1)
            for b in range(2):
                V.memset(small[:, b], 0.0).then_inc(down_drained[b], 1)
            dve.wait_ge(vec_landed, 16)
            dve.wait_ge(x_landed, 16)
            rs = reciprocal_root()
            for k in range(KT):
                last = stt(hT[:, k], xT[:, k], v("mix_norm", k), rs)
            last.then_inc(norm_done, 1)

            c = VAT["lam_re"]
            lr, li = vec[:, c:c + S5_STATES], vec[:, c + S5_STATES:c + 2 * S5_STATES]
            dt_, e_, th, kk, r1, kc, r2, mag, sn, cs, den, cr, ci, nci, t1, am1 = (s5c[:, j] for j in range(16))
            dve.wait_ge(s5_fn, 1)
            link(tt(e_, lr, dt_))
            link(tt(th, li, dt_))

            def reduced(o, k, shift):
                link(V.tensor_scalar(k, th, 1.0 / TWO_PI, shift / TWO_PI, M, ADD))
                link(V.tensor_scalar(k, k, ROUND, None, ADD))
                link(V.tensor_scalar(k, k, ROUND, None, SUB))
                link(stt(o, k, -PI_HI, th, M, ADD))
                link(stt(o, k, -PI_MID, o, M, ADD))
                link(stt(o, k, -PI_LO, o, M, ADD))
                link(V.tensor_scalar(o, o, shift, PI_IN, ADD, MIN))
                return V.tensor_scalar(o, o, -PI_IN, None, MAX)

            reduced(r1, kk, 0.0)
            reduced(r2, kc, float(np.pi / 2)).then_inc(s5_arg, 1)
            c = VAT["hg_lb"]
            tt(lb[:, 0], vec[:, c:c + HG], vec[:, c:c + HG], SUB).then_inc(lb_arg, 1)
            dve.wait_ge(lb_exp, 1)
            link(V.reciprocal(lb[:, 2], lb[:, 1]))
            link(tt(lb[:, 2], lb[:, 2], lb[:, 1]))
            link(tt(lb[:, 0], lb[:, 2], lb[:, 2], SUB))
            link(V.tensor_scalar(lb[:, 1], lb[:, 0], -1.0, 1.0, M, ADD))
            dve.wait_ge(s5_fn, 2)
            zr, zi, nzi = s5p[:, 0, 0], s5p[:, 0, 1], s5p[:, 0, 2]
            link(tt(zr, mag, cs))
            link(tt(zi, mag, sn))
            link(V.tensor_scalar(nzi, zi, -1.0, None, M))
            for k in range(1, S5_STEPS):
                a, b = s5p[:, k - 1], s5p[:, k]
                link(tt(t1, a[:, 1], a[:, 1]))
                link(tt(b[:, 0], a[:, 0], a[:, 0]))
                link(tt(b[:, 0], b[:, 0], t1, SUB))
                link(stt(b[:, 1], a[:, 0], 2.0, a[:, 1]))
                link(V.tensor_scalar(b[:, 2], b[:, 1], -1.0, None, M))
            link(tt(den, lr, lr))
            link(tt(t1, li, li))
            link(tt(den, den, t1, ADD))
            link(V.reciprocal(den, den))
            link(V.tensor_scalar(am1, zr, -1.0, None, ADD))
            link(tt(cr, am1, lr))
            link(tt(t1, zi, li))
            link(tt(cr, cr, t1, ADD))
            link(tt(cr, cr, den))
            link(tt(ci, zi, lr))
            link(tt(t1, am1, li))
            link(tt(ci, ci, t1, SUB))
            link(tt(ci, ci, den))
            link(V.tensor_scalar(nci, ci, -1.0, None, M))

            units.skip(10)
            drained_all()
            for k in range(ML_TILES):
                x, o = MT[:, CX0 + k], CA[:, k]
                w = [v("ml_conv", 5 * k + j) for j in range(5)]
                link(V.tensor_scalar(o, x, w[3], w[4], M, ADD))
                for j in range(1, 4):
                    last = stt(o[:, j:], x[:, 0:T - j], w[3 - j], o[:, j:], M, ADD)
                    if k < ML_TILES - 1 or j < 3:
                        link(last)
            last.then_inc(conv_ready, 1)
            skip(9)
            dve.wait_ge(if_summed, 1)
            link(V.tensor_scalar(rows[:, 2], bank[7][0:ML, 0], v("b_ig", 0, ML), None, ADD))
            link(V.tensor_scalar(rows[:, 3], bank[7][0:ML, 1], v("b_fg", 0, ML), None, ADD))
            stt(rows[:, 0], rows[:, 3], -1.0, rows[:, 3], M, MAX).then_inc(rows_abs, 1)
            link(V.tensor_scalar(rows[:, 3], rows[:, 3], 0.0, None, MIN))
            dve.wait_ge(rows_log, 1)
            link(tt(rows[:, 3], rows[:, 3], rows[:, 0], SUB))
            link(V.memset(rows[:, 4], 1.0))
            link(V.tensor_tensor_scan(rows[:, 1], rows[:, 4], rows[:, 3], 0.0, M, ADD))
            link(tt(rows[:, 2], rows[:, 2], rows[:, 1], SUB))
            link(V.tensor_tensor_scan(rows[:, 3], rows[:, 2], rows[:, 2], 0.0, MAX, MAX))
            tt(rows[:, 4], rows[:, 1], rows[:, 3], ADD).then_inc(rows_ready, 1)
            units.skip(2, False)
            skip(1)
            dve.wait_ge(qk_ready, 2)
            dve.wait_ge(cast_taken, 1)
            for h in range(ML):
                V.tensor_scalar(PM[:, h, 0:T], MB[:, h], acol[:, 0, h:h + 1], 0.0, SUB, MAX)
                V.tensor_scalar(PM[:, h, T:], MB[:, h, P:], acol[:, 1, h:h + 1], 0.0, SUB, MAX).then_inc(ml_arg, 1)
            dve.wait_ge(cst_landed, 48)
            for h in range(ML):
                dve.wait_ge(ml_exp, h + 1)
                dve.wait_ge(ml_scored, h + 1)
                link(tt(PM[:, h, 0:T], PM[:, h, 0:T], bank[4 + h][:, 0]))
                link(tt(PM[:, h, T:], PM[:, h, T:], bank[4 + h][:, 1, P:]))
                for at in (0, T):
                    last = tt(PM[:, h, at:at + P], PM[:, h, at:at + P], causal)
                last.then_inc(ml_p, 1)
            skip(1)
            dve.wait_ge(cast_taken, 2)
            dve.wait_ge(ml_den, 1)
            for j in range(2):
                th = TH[:, 2 * j:2 * j + 2]
                link(stt(th, bank[4 + j][:], -1.0, th, M, MAX))
                link(tt(th, bank[4 + j][:], th, MAX))
            V.reciprocal(TH, TH).then_inc(ml_rden, 1)
            dve.wait_ge(ml_rden, 1)
            dve.wait_ge(ml_num, 1)
            for h in range(ML):
                for k, p0, p1, _ in PIECES[h]:
                    last = tt(HH[p0:p1, k], bank[4 + k // 2][p0:p1, k % 2], TH[p0:p1, h])
            last.then_inc(ml_h, 1)
            skip(1)
            rs = reciprocal_root()
            for h in range(ML):
                for k, p0, p1, _ in PIECES[h]:
                    c = VAT["ml_norm"] + k
                    link(stt(HH[p0:p1, k], HH[p0:p1, k], vec[p0:p1, c:c + 1], rs[p0:p1, h]))
            drained_all()
            tt(MT[:, O0:O0 + 6], HH, MT[:, O0:O0 + 6]).then_inc(norm_done, 1)
            dve.wait_ge(norm_done, 2)

            for h in range(HG):
                link(V.tensor_scalar(HF[:, h], HF[:, h], lb[:, 1, h:h + 1], lb[:, 0, h:h + 1], M, ADD))
            V.tensor_scalar(HK, HF, -1.0, 1.0, M, ADD).then_inc(hg_x, 1)
            V.memset(PD, 0.0)
            link(V.memset(HPR, 1.0))
            dve.wait_ge(hg_x, 1)
            dve.wait_ge(hmask_landed, 16)

            def halves(ap, B):
                return ap.rearrange("p k t -> p (k t)").rearrange("p (n two b) -> p n two b", two=2, b=B)

            def meet(lvl):
                B = 1 << (lvl - 1)
                X = [HX0, HX1][lvl % 2]
                if lvl >= 3:
                    dve.wait_ge(hg_scored, lvl - 1)
                x, q, k, pf, pr = (halves(a, B) for a in (X, HQ, HK, HF, HPR))
                tt(x[:, :, 1], q[:, :, 1], pf[:, :, 1])
                tt(x[:, :, 0], k[:, :, 0], pr[:, :, 0]).then_inc(hg_x, 1)
                if B < P:
                    n = [P, HG * T // (2 * B), B]
                    link(tt(pr[:, :, 0], pr[:, :, 0], pf[:, :, 1, B - 1:B].broadcast_to(n)))
                    link(tt(pf[:, :, 1], pf[:, :, 1], pf[:, :, 0, B - 1:B].broadcast_to(n)))

            meet(1)
            meet(2)
            for lvl in range(9):
                dve.wait_ge(hg_scored, lvl + 1)
                if lvl == 8:
                    V.tensor_copy(PO[:, 0:4].rearrange("p h c -> p (h c)"), bank_row[4])
                    V.tensor_copy(PO[:, 4:6].rearrange("p h c -> p (h c)"), bank_row[5][:, 0:2 * P]).then_inc(hg_taken, 1)
                else:
                    m = hmask[:, lvl:lvl + 1].broadcast_to([P, 4, P])
                    for j in range(3):
                        last = V.copy_predicated(PD[:, 2 * j:2 * j + 2].rearrange("p k (b c) -> p (k b) c", c=P), m,
                                                 bank_row[4 + j].rearrange("p (k c) -> p k c", c=P))
                    last.then_inc(hg_taken, 1)
                if 1 <= lvl <= 6:
                    meet(lvl + 2)
            skip(2)
            skip(1)
            rs = reciprocal_root()
            for h in range(HG):
                link(stt(HO[:, h], HO[:, h], v("hg_norm", h), rs[:, h]))
            tt(HQ, HO, MT[:, OG0:OG0 + 6]).then_inc(norm_done, 1)
            dve.wait_ge(norm_done, 3)

            units.skip(2, False)
            link(V.memset(pads, 0.0))
            dve.wait_ge(s5_in, S5_STATES)
            with dve.Fori(0, S5_STATES) as i:
                chain.enter(i, 4 + 4 * S5_STEPS - 1)

                def coef(ap):
                    return ap[:, bass.ds(i, 1)]

                def state(ap):
                    return ap[:, bass.ds(i, 1)].rearrange("p k t -> p (k t)")

                now = [pads[:, 0, P:], pads[:, 1, P:]]
                link(V.tensor_scalar(now[0], state(SR), coef(cr), None, M))
                link(V.tensor_scalar(now[1], state(SI), coef(cr), None, M))
                link(stt(now[0], state(SI), coef(nci), now[0], M, ADD))
                link(stt(now[1], state(SR), coef(ci), now[1], M, ADD))
                for k in range(S5_STEPS):
                    a, b, d = 2 * (k % 2), 2 * ((k + 1) % 2), 1 << k
                    cur, old = ([pads[:, a + j, at:at + T] for j in range(2)] for at in (P, P - d))
                    if k < S5_STEPS - 1:
                        new = [pads[:, b + j, P:] for j in range(2)]
                    else:
                        new = [state(SR), state(SI)]
                    cr_, ci_, nci_ = (coef(s5p[:, k, j]) for j in range(3))
                    link(stt(new[0], old[0], cr_, cur[0], M, ADD))
                    link(stt(new[1], old[1], cr_, cur[1], M, ADD))
                    link(stt(new[0], old[1], nci_, new[0], M, ADD))
                    last = stt(new[1], old[0], ci_, new[1], M, ADD)
                    if k < S5_STEPS - 1:
                        link(last)
                last.then_inc(s5_states, 1)
            chain.leave(S5_STATES)
            skip(6)
            units.skip(1, False)
            s, _, _, there, _ = units.next(False)
            dve.wait_ge(consumed[s], there)
            for f in range(S5_TILES):
                link(stt(GA[:, f], MT[:, U0 + f], v("s5_d", f), bank[4 + f][:, 0], M, ADD))
                last = tt(GA[:, f], GA[:, f], bank[4 + f][:, 1], SUB)
            last.then_inc(s5_pre, 1)
            units.next(False)
            dve.wait_ge(s5_gate, 1)
            tt(MT[:, U0:U0 + 4], MT[:, U0:U0 + 4], GA).then_inc(s5_done, 1)

            def rounds(n, body):
                with dve.Fori(0, n) as i:
                    units.enter(i)
                    for j in range(RING):
                        s, _, _, there, _ = units.next()
                        dve.wait_ge(consumed[s], there)
                        body(s, i * RING + j).then_inc(drained[s], 1)
                units.leave(n)

            def looped(n, per, body):
                with dve.Fori(0, n) as i:
                    units.enter(i)
                    chain.enter(i, per)
                    body(i)
                units.leave(n)
                chain.leave(n)

            def gated(parts):
                def body(i):
                    for j in range(RING):
                        s, _, _, there, _ = units.next()
                        dve.wait_ge(consumed[s], there)
                        n = i * RING + j
                        o = hT[:, bass.ds(n, 1)]
                        tmp = xtmp[:].rearrange("p (k t) -> p k t", k=1)
                        for m, (g, at, b, half) in enumerate(parts):
                            x = bank[b + s][:, half:half + 1]
                            gate = g[:, bass.ds(n + at, 1)]
                            if m == 0:
                                link(tt(o, gate, x))
                            else:
                                link(tt(tmp, gate, x))
                                last = tt(o, o, tmp, ADD)
                                if m < len(parts) - 1:
                                    link(last)
                        last.then_inc(drained[s], 1)
                return body

            def add_residual(s, n):
                return tt(xT[:, bass.ds(n, 1)], xT[:, bass.ds(n, 1)], bank[s][:, 0:1], ADD)

            def down():
                with dve.Fori(0, 8) as i:
                    units.enter(i, turns=2, drained=0)
                    for b in range(2):
                        for q in range(4):
                            s, _, _, there, _ = units.next(False)
                        dve.wait_ge(consumed[s], there)
                        n = i * 2 + b
                        tt(xT[:, bass.ds(n, 1)], xT[:, bass.ds(n, 1)], bank[4 + b][:, 0:1], ADD)\
                            .then_inc(down_drained[b], 1)
                units.leave(8)

            looped(4, 4 * 4, gated([(G, 0, 0, 0), (G, 16, 0, 1), (G, 32, 4, 0)]))
            rounds(4, add_residual)
            drained_all()
            normalise(hT, xT, "ffn_norm")

            pairs = Count(silu_pair)

            def conv_pairs(i):
                pairs.enter(i, 2)
                for j in range(2):
                    for half in range(2):
                        s, _, _, there, free = units.next()
                        dve.wait_ge(consumed[s], there)
                        n = i * RING + (2 * j + half)
                        o, x = cv[:, 2 * j + half], bank[s][:, 0]

                        def w(c):
                            return vec[:, bass.ds(n * 4 + (VAT["ffn_conv"] + c), 1)]

                        link(V.tensor_scalar(o, x, w(2), w(3), M, ADD))
                        link(stt(o[:, 1:], x[:, 0:T - 1], w(1), o[:, 1:], M, ADD))
                        stt(o[:, 2:], x[:, 0:T - 2], w(0), o[:, 2:], M, ADD).then_inc(drained[s], 1)
                    dve.wait_ge(drained[s], free + 1)
                    pairs.add()
                    dve.wait_ge(silu_pair, pairs.value())
                    tt(ACTS[:, bass.ds(i * 2 + j, 1)], cv[:, 2 * j:2 * j + 1], cv[:, 2 * j + 1:2 * j + 2])\
                        .then_inc(ff_done, 1)

            looped(22, 8, conv_pairs)
            pairs.leave(22)
            down()
            for b in range(2):
                dve.wait_ge(down_drained[b], 1 + KT // 2)
            normalise(xT, xT, "final_norm")
            dve.wait_ge(norm_done, 5)
            normalise(hT, xT, "g_mix")

            skip(6)
            units.skip(2)
            skip(2)
            drained_all()
            for src, gain in ((CQ, "g_cq"), (CKV, "g_ckv")):
                rs = reciprocal_root()
                for k in range(4):
                    last = stt(src[:, k], src[:, k], v(gain, k), rs[:, 0])
                last.then_inc(norm_done, 1)
            units.skip(7)
            drained_all()
            cos, sin = band[:, 4:5], band[:, 5:6]

            def rope(x1, x2, n):
                c, s = cos.broadcast_to([P, n, T]), sin.broadcast_to([P, n, T])
                a, b, c2 = MS[:, 0:n], MS[:, 2:2 + n], MS[:, 4:4 + n]
                link(tt(a, x1, c))
                link(tt(b, x2, s))
                link(tt(c2, x1, s))
                link(tt(x1, a, b, SUB))
                link(tt(b, x2, c))
                tt(x2, c2, b, ADD).then_inc(norm_done, 1)

            def heads(x, gain):
                rs = reciprocal_root()
                n = x.shape[1]
                link(tt(x, x, rs))
                V.tensor_scalar(x, x, v(gain), None, M).then_inc(norm_done, 1)

            rs = reciprocal_root()
            for half in range(2):
                last = stt(KR[:, half], KR[:, half], v("g_k_rope", half), rs[:, 0])
            link(last)
            dve.wait_ge(band_landed, 16)
            rope(KR[:, 0:1], KR[:, 1:2], 1)
            heads(QD, "g_q_dil")
            heads(KD, "g_k_dil")
            skip(1)
            heads(QN, "g_q_nope")
            rs = reciprocal_root()
            for half in range(2):
                for g in range(2):
                    k = 2 * half + g
                    last = stt(QR[:, k], QR[:, k], v("g_q_rope", half), rs[:, g])
            link(last)
            rope(QR[:, 0:2], QR[:, 2:4], 2)
            heads(KN, "g_k_nope")
            skip(2)
            dve.wait_ge(norm_done, 14)

            for h in range(2 * HEADS):
                e, m = ES[h % 2], small[:, h % 2]
                s = bank[4 + h % 2]
                dve.wait_ge(at_scored, h + 1)
                if h < HEADS:
                    link(V.tensor_reduce(m[:, 0:2], s[:], axis=AX.X, op=MAX))
                    V.tensor_scalar(m[:, 2:4], m[:, 0:2], -(192 ** -0.5), None, M).then_inc(at_max, 1)
                    dve.wait_ge(at_exp, h + 1)
                else:
                    dve.wait_ge(at_bias, h - HEADS + 1)
                    if h >= 2:
                        dve.wait_ge(at_turned, h - 1)
                    link(stt(e, s[:], P ** -0.5, BS[h % 2], M, ADD))
                    link(V.tensor_reduce(m[:, 0:2], e, axis=AX.X, op=MAX))
                    V.tensor_scalar(m[:, 2:4], m[:, 0:2], -1.0, None, M).then_inc(at_max, 1)
                    dve.wait_ge(at_exp, h + 1)
                    for b in range(TB):
                        last = stt(e[:, b], e[:, b], 1.0, band[:, 2 + b], M, M, accum_out=m[:, 4 + b:5 + b])
                    link(last)
                link(V.reciprocal(m[:, 4:6], m[:, 4:6]))
                for b in range(TB):
                    last = V.tensor_scalar(e[:, b], e[:, b], m[:, 4 + b:5 + b], None, M)
                last.then_inc(at_p, 1)
            skip(5)
            looped(4, 4 * 2, gated([(G2, 0, 0, 0), (G2, 16, 0, 1)]))
            rounds(4, add_residual)
            drained_all()
            normalise(hT, xT, "g_ffn")

            with dve.Fori(0, 22) as i:
                units.enter(i)
                for j in range(2):
                    sg, _, _, _, gate_free = units.next()
                    s, _, _, there, _ = units.next()
                    dve.wait_ge(consumed[s], there)
                    dve.wait_ge(drained[sg], gate_free + 1)
                    tt(ACTS[:, bass.ds(i * 2 + j, 1)], cv[:, 2 * j:2 * j + 1], bank[s][:, 0:1]).then_inc(drained[s], 1)
            units.leave(22)
            down()


_OUT = (P, KT, T)


def kernel(**inputs):
    import concourse.bacc as _bacc
    from concourse.bass_utils import run_bass_kernel_spmd as _run

    arrays = host_layout({k: np.asarray(a) for k, a in inputs.items()})
    nc = _bacc.Bacc("TRN2", target_bir_lowering=False, num_devices=1)
    t = {k: nc.dram_tensor("in_" + k, a.shape, mybir.dt.from_np(a.dtype), kind="ExternalInput").ap()
         for k, a in arrays.items()}
    out = nc.dram_tensor("out", _OUT, F32, kind="ExternalOutput").ap()
    build(nc, t, out)
    r = _run(nc, [{"in_" + k: a for k, a in arrays.items()}], core_ids=[0])
    y = np.asarray(r.results[0]["out"])
    return np.ascontiguousarray(y.transpose(2, 1, 0)).reshape(1, T, D)


def unit_tiles(w, group=1):
    K, N = w.shape
    a = w.reshape(K // P, P, N // P, P).transpose(2, 1, 0, 3).reshape(N // P // group, group, P, K)
    return np.ascontiguousarray(a.transpose(0, 2, 1, 3)).reshape(N // P // group, P, group * K)


def down_tiles(w):
    a = w.reshape(4, DOWN, P, KT, P).transpose(3, 0, 2, 1, 4)
    return np.ascontiguousarray(a).reshape(4 * KT, P, DOWN * P)


def columns(x):
    return x.reshape(-1, P).T


def host_layout(g):
    a = {}
    w = g["w_in"][0]
    at = np.cumsum([0, 512, 768, 768, 768, 768, 768, 768, 768, 4, 4])
    cut = [w[:, at[n]:at[n + 1]] for n in range(10)]
    a["w_mix"] = unit_tiles(np.concatenate([cut[n] for n in (0, 5, 3, 6, 2, 7, 1, 4)], axis=1))
    a["w_gates"] = unit_tiles(w[:, at[10]:])
    a["w_if"] = np.ascontiguousarray(w[:, at[8]:at[10]].reshape(KT, P, 8).transpose(1, 0, 2))
    qk = np.zeros((2, P, ML, 2, ML_DH), np.float32)
    for h in range(ML):
        for n, (_, lo, hi, e) in enumerate(PIECES[h]):
            for part in range(2):
                qk[part, lo:hi, h, n] = g["ml_w_qk"][0][h, e:e + hi - lo, part * ML_DH:(part + 1) * ML_DH]
    a["w_qk"] = qk.reshape(2, P, 8 * ML_DH)
    s5b = np.zeros((2, P, S5_STATES, P), np.float32)
    s5c = np.zeros((2, P, S5_STATES, P), np.float32)
    for part in range(2):
        b = g[("s5_b_re", "s5_b_im")[part]][0]
        c = g[("s5_c_re", "s5_c_im")[part]][0]
        for q in range(32):
            f, n, s = 16 * (q % 8), q // 2, 64 * (q % 2)
            s5b[part, f:f + 16, n, s:s + 64] = b[q].T
            s5c[part, s:s + 64, n, f:f + 16] = c[q].T
    a["s5_b"], a["s5_c"] = s5b.reshape(2, P, UNIT), s5c.reshape(2, P, UNIT)
    a["w_glu"] = unit_tiles(g["s5_w_glu"][0], 4)
    a["w_branch"] = unit_tiles(g["w_branch"][0])
    a["w_out"] = unit_tiles(g["w_out"][0])
    swap = np.stack([np.arange(FF_TILES), FF_TILES + np.arange(FF_TILES)], axis=1).ravel()
    a["w_up"] = unit_tiles(g["ffn_w_up"][0])[swap]
    a["w_down"] = down_tiles(g["ffn_w_down"][0])

    w = g["w_in_2"][0]
    x1, x2 = w[:, 1024:1056], w[:, 1056:1088]
    a["w_in2"] = unit_tiles(np.concatenate([w[:, 0:1024], x1, x1, x1, x1, x2, x2, x2, x2, w[:, 1088:]], axis=1))
    uq = g["w_uq_2"][0].reshape(512, HEADS, 192)
    a["w_uq"] = unit_tiles(np.concatenate([uq[:, :, 0:128].reshape(512, -1), uq[:, :, 128:160].reshape(512, -1),
                                           uq[:, :, 160:192].reshape(512, -1)], axis=1), 4)
    ukv = g["w_ukv_2"][0].reshape(512, HEADS, 256)
    vals = ukv[:, :, 128:].reshape(4, P, 2, 512).transpose(2, 1, 0, 3).reshape(2, P, UNIT)
    a["w_ukv"] = np.concatenate([unit_tiles(ukv[:, :, 0:128].reshape(512, -1), 4), vals], axis=0)
    a["w_mix2"] = unit_tiles(np.concatenate([g["w_o_mla_2"][0], g["w_o_dil_2"][0]], axis=0))
    a["w_o2"] = unit_tiles(g["w_o_2"][0])
    a["w_up2"] = unit_tiles(g["w_gate_up_2"][0])[swap]
    a["w_down2"] = down_tiles(g["w_down_2"][0])

    vec = np.zeros((P, VCOLS), np.float32)

    def put(name, cols, rows=P):
        vec[0:rows, VAT[name]:VAT[name] + cols.shape[1]] = cols

    put("mix_norm", columns(g["mix_norm"][0]))
    put("final_norm", columns(g["final_norm"]))
    put("ffn_norm", columns(g["ffn_norm"][0]))
    put("g_mix", columns(g["g_mix_2"][0]))
    put("g_ffn", columns(g["g_ffn_2"][0]))
    put("b_gate", columns(g["b_gate_2"][0]))
    taps = np.concatenate([g["ffn_conv_w"][0], g["ffn_conv_b"]], axis=0).reshape(4, 2 * FF_TILES, P)
    put("ffn_conv", taps[:, swap].transpose(2, 1, 0).reshape(P, -1))
    taps = np.concatenate([g["ml_conv_w"][0], g["ml_conv_b"]], axis=0).reshape(5, ML_TILES, P)
    put("ml_conv", taps.transpose(2, 1, 0).reshape(P, -1))
    put("s5_d", columns(g["s5_d"][0]))
    put("b_glu", columns(g["s5_b_glu"][0]))
    put("hg_lb", columns(g["hg_lower_bounds"][0]))
    put("hg_norm", columns(g["hg_norm"][0]))
    put("ml_norm", columns(g["ml_norm"][0]))
    put("g_cq", columns(g["g_cq_2"][0]))
    put("g_ckv", columns(g["g_ckv_2"][0]))
    for name in ("g_q_nope", "g_k_nope", "g_q_dil", "g_k_dil"):
        put(name, g[name + "_2"][0].reshape(P, 1))
    for name in ("g_q_rope", "g_k_rope"):
        put(name, np.tile(g[name + "_2"][0].reshape(2, 32).T, (4, 1)))
    put("lam_re", columns(g["s5_lam_re"][0].reshape(-1)))
    put("lam_im", columns(g["s5_lam_im"][0].reshape(-1)))
    put("log_dt", columns(np.repeat(g["s5_log_dt"][0], 64)))
    put("b_ig", g["ml_b_ig"][0].reshape(ML, 1), ML)
    put("b_fg", g["ml_b_fg"][0].reshape(ML, 1), ML)
    a["vec"] = vec
    a["xT"] = np.ascontiguousarray(g["x"][0].T.reshape(KT, P, T).transpose(1, 0, 2))

    i = np.arange(P)
    cst = np.zeros((P, 5, P), np.float32)
    cst[:, 0] = i[:, None] // 32 == i[None] // 32
    cst[:, 1] = np.eye(P)
    cst[:, 2] = i[:, None] <= i[None]
    cst[:, 3] = i[:, None] < 64
    cst[:, 4] = i[:, None] >= 64
    a["cst"] = cst
    a["sel"] = np.ascontiguousarray(np.repeat(np.eye(ML, dtype=np.float32)[:, :, None], P, axis=2))
    hm = np.zeros((P, 8, P), np.int32)
    hm[:, 0] = np.eye(P)
    for lvl in range(1, 8):
        B = 1 << (lvl - 1)
        s, q = i[:, None], i[None]
        hm[:, lvl] = (s // (2 * B) == q // (2 * B)) & (s // B % 2 == 0) & (q // B % 2 == 1)
    a["hmask"] = hm
    d = np.abs(np.arange(T)[:, None] - np.arange(T)[None])
    cover = sum(((d % dil == 0) & (d // dil <= win // (2 * dil))).astype(np.float32)
                for win, dil in ((128, 1), (512, 4), (2048, 16)))
    away = np.where(cover > 0, -d, MASKED).astype(np.float32)
    inv = np.float32(10000.0) ** (-np.arange(0, 64, 2, dtype=np.float32) / np.float32(64))
    ang = np.arange(T, dtype=np.float32)[None] * inv[:, None]
    band = np.zeros((P, 6, T), np.float32)
    band[:, 0:2] = away.reshape(2, P, T).transpose(1, 0, 2)
    band[:, 2:4] = cover.reshape(2, P, T).transpose(1, 0, 2)
    band[:, 4] = np.tile(np.cos(ang), (4, 1))
    band[:, 5] = np.tile(np.sin(ang), (4, 1))
    a["band"] = band
    return a
```

```python
from contextlib import ExitStack

import numpy as np
import concourse.bass as bass
from concourse import mybir

F32 = mybir.dt.float32
R32 = mybir.dt.float32r
I32 = mybir.dt.int32
ALU = mybir.AluOpType
ACT = mybir.ActivationFunctionType
AX = mybir.AxisListType

P = 128
T = 256
TB = T // P
D = 2048
KT = D // P
EPS = 1e-6
RING = 4
UNIT = KT * P
AHEAD = 2

S5_TILES = 4
S5_STATES = 16
S5_STEPS = 8
S5_SIDE = 16
HG = 6
ML = 4
ML_DH = 192
ML_TILES = 6
FF = 5632
FF_TILES = FF // P
DOWN = FF_TILES // 4
SPLIT_UP = 34
HEADS = 8
SLOPES = [2.0 ** -(h + 1) for h in range(HEADS)]
MASKED = -1e30
TWO_PI = 2 * np.pi
PI_HI, PI_MID = 6.28125, 0.0019350051879882812
PI_LO = TWO_PI - PI_HI - PI_MID
ROUND = 1.5 * 2 ** 23
PI_IN = 3.1415925

VEC = [("mix_norm", 16), ("final_norm", 16), ("ffn_norm", 16), ("g_mix", 16), ("g_ffn", 16),
       ("b_gate", 32), ("ffn_conv", 4 * 88), ("ml_conv", 5 * 6), ("s5_d", 4), ("b_glu", 4), ("hg_lb", 6),
       ("hg_norm", 6), ("ml_norm", 6), ("g_cq", 4), ("g_ckv", 4), ("g_q_nope", 1), ("g_k_nope", 1),
       ("g_q_rope", 2), ("g_k_rope", 2), ("g_q_dil", 1), ("g_k_dil", 1), ("lam_re", 16), ("lam_im", 16),
       ("log_dt", 16), ("b_ig", 1), ("b_fg", 1)]
VAT, _n = {}, 0
for _name, _w in VEC:
    VAT[_name] = _n
    _n += _w
VCOLS = _n

U0, CX0, F0, O0, Q0, OG0 = 0, 4, 10, 16, 22, 28
M_TILES = 34

PIECES = []
for _h in range(ML):
    _j = 3 * (_h // 2)
    PIECES.append([(_j, 0, 128, 0), (_j + 1, 0, 64, 128)] if _h % 2 == 0
                  else [(_j + 1, 64, 128, 0), (_j + 2, 0, 128, 64)])


class Count:

    def __init__(self, sem):
        self.sem, self.base, self.i, self.per, self.k = sem, 0, None, 0, 0

    def add(self, n=1):
        self.k += n

    def value(self):
        if self.i is None or self.per == 0:
            return self.base + self.k
        return self.i * self.per + (self.base + self.k)

    def enter(self, i, per):
        self.base, self.k, self.i, self.per = self.base + self.k, 0, i, per

    def leave(self, rounds):
        assert self.k == self.per, (self.k, self.per)
        self.base, self.k, self.i, self.per = self.base + self.per * rounds, 0, None, 0


class Units:

    def __init__(self, landed, rounded, lowered, consumed, drained):
        self.pos = 0
        self.landed, self.rounded, self.lowered, self.consumed, self.drained = (
            [Count(s) for s in sems] for sems in (landed, rounded, lowered, consumed, drained))

    def next(self, drained=True, split=False):
        s = self.pos % RING
        self.pos += 1
        self.landed[s].add(16)
        before, free = self.consumed[s].value(), self.drained[s].value()
        self.consumed[s].add()
        if split:
            self.rounded[s].add()
            self.lowered[s].add()
        if drained:
            self.drained[s].add()
        return s, self.landed[s].value(), before, self.consumed[s].value(), free

    def enter(self, i, turns=1, drained=1, split=0):
        self.turns = turns
        for counts, per in ((self.landed, 16), (self.rounded, split), (self.lowered, split),
                            (self.consumed, 1), (self.drained, drained)):
            for c in counts:
                c.enter(i, per * turns)

    def leave(self, n):
        self.pos += (n - 1) * self.turns * RING
        for c in self.landed + self.rounded + self.lowered + self.consumed + self.drained:
            c.leave(n)

    def skip(self, n, drained=True, split=False):
        for _ in range(n):
            self.next(drained, split)

    def all_drained(self):
        return [(c.sem, c.value()) for c in self.drained]


def build(nc, t, out):
    with ExitStack() as ctx:
        def sb(name, shape, dt=F32):
            return ctx.enter_context(nc.sbuf_tensor(name, shape, dt))

        def alias(name, base, shape, at=0):
            return nc.alloc_sbuf_tensor_at(name, shape, R32, offset=base + at * T * 4)

        ring = sb("ring", [P, RING, UNIT])
        ring_base = nc.sbuf_base - RING * UNIT * 4
        xT = sb("xT", [P, KT, T])
        hT = sb("hT", [P, KT, T])
        hT_base = nc.sbuf_base - KT * T * 4
        vec = sb("vec", [P, VCOLS])
        cst = sb("cst", [P, 5, P])
        sel = sb("sel", [ML, ML, P])
        w_if = sb("w_if", [P, KT, 8])
        ones = sb("ones", [P, P])
        acol = sb("acol", [P, TB, ML])
        lb = sb("lb", [P, 4, HG])
        s5c = sb("s5c", [P, 16, S5_STATES])
        s5p = sb("s5p", [P, S5_STEPS, 2, S5_STATES])
        small = sb("small", [P, 2, 8])
        xms = sb("xms", [P, T])
        xrs = sb("xrs", [P, T])
        xtmp = sb("xtmp", [P, T])
        ARENA = nc.sbuf_bytes_remaining // 4 // 16 * 16
        arena = sb("arena", [P, ARENA])
        arena_base = nc.sbuf_base - ARENA * 4

        def tiles(at, n):
            assert at + n * T <= ARENA, (at + n * T, ARENA)
            return arena[:, at:at + n * T].rearrange("p (k t) -> p k t", t=T)

        w_low = alias("w_low", ring_base, [P, RING, UNIT])
        w_high = alias("w_high", arena_base, [P, RING, UNIT], 94)
        h_low = alias("h_low", hT_base, [P, KT, T])
        mix_high, mix_low = (alias(f"mix_{n}", arena_base, [P, KT, T], a) for n, a in (("high", 46), ("low", 62)))
        in2_high, in2_low = (alias(f"in2_{n}", arena_base, [P, KT, T], a) for n, a in (("high", 34), ("low", 50)))
        out_high = alias("out_high", arena_base, [P, KT, T], 28)
        out2_high = alias("out2_high", arena_base, [P, KT, T], 18)
        up_high = alias("up_high", arena_base, [P, KT, T], 78)
        acts_low = alias("acts_low", arena_base, [P, FF_TILES, T], 0)
        acts_high = alias("acts_high", arena_base, [P, FF_TILES, T], 44)

        MT = tiles(0, M_TILES)
        VN = arena[:, 34 * T:46 * T].rearrange("p (b h c) -> p b h c", b=TB, c=P)
        G = tiles(46 * T, 48)
        W = 94 * T
        CA, QH, KH = tiles(78 * T, 6), tiles(W + 6 * T, 6), tiles(W + 12 * T, 6)
        rows = arena[0:ML, W + 18 * T:W + 24 * T].rearrange("p (k t) -> p k t", t=T)
        MB, TH = tiles(W + 24 * T, 4), tiles(W + 28 * T, 4)
        PM = arena[:, 78 * T:84 * T].rearrange("p (h c) -> p h c", h=ML)
        HH, MSQ, MMS, MRS = CA, QH, KH[:, 0:4], MB
        HK, HPR, HX1 = tiles(W, 6), tiles(W + 6 * T, 6), tiles(W + 12 * T, 6)
        HX0, HF, HQ = MT[:, CX0:CX0 + 6], MT[:, F0:F0 + 6], MT[:, Q0:Q0 + 6]
        PD = tiles(W + 18 * T, 6)
        PO = arena[:, W + 24 * T:W + 27 * T].rearrange("p (h c) -> p h c", h=HG)
        HRS = tiles(W, 6)
        hmask = arena[:, W + 32 * T:W + 36 * T].bitcast(I32).rearrange("p (l c) -> p l c", l=8)
        HO, HSQ, HMS = HX1, HX0, HF
        SR = tiles(W, S5_STATES)
        SI = tiles(OG0 * T, S5_STATES)
        turn_c, turn_s = tiles(W + 16 * T, 4), tiles(W + 20 * T, 4)
        tmp_r, tmp_i = tiles(W + 24 * T, 4), tiles(W + 28 * T, 4)
        GA = tiles(W + 32 * T, 4)
        powers = arena[:, 90 * T:94 * T].rearrange("p (j n a) -> p j n a", j=4, a=S5_SIDE)
        ACTS = tiles(0, FF_TILES)
        cv = tiles(126 * T, 4)
        P2 = tiles(0, 26)
        VD = arena[:, 26 * T:34 * T].rearrange("p (b h c) -> p b h c", b=TB, c=P)
        G2 = tiles(34 * T, 32)
        QN, QR, KN = tiles(66 * T, 8), tiles(74 * T, 4), tiles(78 * T, 8)
        VM = arena[:, 86 * T:94 * T].rearrange("p (b h c) -> p b h c", b=TB, c=P)
        SQ, MS, RS = tiles(94 * T, 8), tiles(102 * T, 8), tiles(110 * T, 8)
        band = tiles(118 * T, 6)
        CQ, CKV, KR = P2[:, 0:4], P2[:, 4:8], P2[:, 8:10]
        QD, KD = P2[:, 10:18], P2[:, 18:26]
        OA = P2[:, 0:8]
        ES = [SQ[:, 0:2], SQ[:, 2:4]]
        PS = [SQ[:, 4:6], SQ[:, 6:8]]
        BS = [MS[:, 0:2], MS[:, 2:4]]

        bank = [ctx.enter_context(nc.psum_tensor(f"bank{i}", [P, 2, T], F32)) for i in range(8)]
        bank_row = [b[:].rearrange("p a t -> p (a t)") for b in bank]

        def sem(name):
            return ctx.enter_context(nc.semaphore(name))

        landed = [sem(f"unit_landed{s}") for s in range(RING)]
        rounded = [sem(f"unit_rounded{s}") for s in range(RING)]
        lowered = [sem(f"unit_lowered{s}") for s in range(RING)]
        consumed = [sem(f"unit_consumed{s}") for s in range(RING)]
        drained = [sem(f"bank_drained{s}") for s in range(RING)]
        x_landed, vec_landed, cst_landed = sem("x_landed"), sem("vec_landed"), sem("cst_landed")
        hmask_landed, band_landed, x_stored = sem("hmask_landed"), sem("band_landed"), sem("x_stored")
        ones_set = sem("ones_set")
        dve_chain, act_chain = sem("dve_chain"), sem("act_chain")
        norm_squared, norm_summed = sem("norm_squared"), sem("norm_summed")
        norm_mean, norm_rooted, norm_done = sem("norm_mean"), sem("norm_rooted"), sem("norm_done")
        conv_ready, conv_act, qk_ready = sem("ml_conv_ready"), sem("ml_conv_act"), sem("ml_qk_ready")
        if_summed, rows_abs, rows_log, rows_ready, rows_thr = (sem("ml_if_summed"), sem("ml_rows_abs"),
                                                               sem("ml_rows_log"), sem("ml_rows_ready"),
                                                               sem("ml_rows_threshold"))
        cast_done, cast_taken = sem("ml_broadcast_done"), sem("ml_broadcast_taken")
        ml_scored, ml_arg, ml_exp, ml_p = sem("ml_scored"), sem("ml_arg"), sem("ml_exp"), sem("ml_p")
        ml_den, ml_rden, ml_num, ml_h = sem("ml_den"), sem("ml_rden"), sem("ml_num"), sem("ml_h")
        ml_done = sem("ml_done")
        hg_x, hg_scored, hg_taken, hg_out, hg_kept = (sem("hg_x"), sem("hg_scored"), sem("hg_taken"),
                                                      sem("hg_out"), sem("hg_kept"))
        hg_done = sem("hg_done")
        lb_arg, lb_exp = sem("hg_bound_arg"), sem("hg_bound_exp")
        s5_arg, s5_fn = sem("s5_arg"), sem("s5_function")
        s5_fed, s5_in, s5_states = sem("s5_fed"), sem("s5_input_kept"), sem("s5_states")
        s5_scaled, s5_tabled = sem("s5_input_scaled"), sem("s5_turns_made")
        s5_pre, s5_gelu = sem("s5_pre"), sem("s5_gelu")
        s5_gate, s5_done = sem("s5_gate"), sem("s5_done")
        silu_pair, ff_done = sem("silu_pair"), sem("ff_act_done")
        h_scaled, h_rounded = sem("h_scaled"), sem("h_rounded")
        h_lowered_pool, h_lowered_vector = sem("h_lowered_by_pool"), sem("h_lowered_by_vector")
        merged_rounded, merged_lowered = sem("merged_rounded"), sem("merged_lowered")
        acts_rounded, acts_lowered = sem("acts_rounded"), sem("acts_lowered")
        down_drained = [sem(f"down_drained{b}") for b in range(2)]
        at_scored, at_max, at_exp, at_p = sem("at_scored"), sem("at_max"), sem("at_exp"), sem("at_p")
        at_turned, at_pt, at_out, at_kept = sem("at_turned"), sem("at_pt"), sem("at_out"), sem("at_kept")
        at_bias, at_sum = sem("at_bias"), sem("at_biased")

        block = ctx.enter_context(nc.Block())

        def v(name, n=0, rows_=P):
            c = VAT[name] + n
            return vec[0:rows_, c:c + 1]

        def all_tiles(sq, n):
            return [[(ones[:], sq[:, k]) for k in range(n)]]

        def each_tile(sq, n):
            return [[(ones[:], sq[:, k])] for k in range(n)]

        blk32, ident, causal = cst[:, 0], cst[:, 1], cst[:, 2]
        NORMS = [
            dict(src=xT, sq=hT, ms=xms, rs=xrs, groups=all_tiles(hT, KT), n=D),
            dict(src=HH, sq=MSQ, ms=MMS, rs=MRS, n=ML_DH, groups=[
                [(cst[:, 3 + a // 64] if b - a < P else ones[:], MSQ[:, k]) for k, a, b, _ in PIECES[h]]
                for h in range(ML)]),
            dict(src=HO, sq=HSQ, ms=HMS, rs=HRS, groups=each_tile(HSQ, HG), n=P),
            dict(src=xT, sq=hT, ms=xms, rs=xrs, groups=all_tiles(hT, KT), n=D),
            dict(src=xT, sq=hT, ms=xms, rs=xrs, groups=all_tiles(hT, KT), n=D),
            dict(src=xT, sq=hT, ms=xms, rs=xrs, groups=all_tiles(hT, KT), n=D),
            dict(src=CQ, sq=SQ[:, 0:4], ms=MS[:, 0:1], rs=RS[:, 0:1], groups=all_tiles(SQ, 4), n=512),
            dict(src=CKV, sq=SQ[:, 0:4], ms=MS[:, 0:1], rs=RS[:, 0:1], groups=all_tiles(SQ, 4), n=512),
            dict(src=KR, sq=SQ[:, 0:2], ms=MS[:, 0:1], rs=RS[:, 0:1], n=64,
                 groups=[[(blk32, SQ[:, 0]), (blk32, SQ[:, 1])]]),
            dict(src=QD, sq=SQ, ms=MS, rs=RS, groups=each_tile(SQ, HEADS), n=P),
            dict(src=KD, sq=SQ, ms=MS, rs=RS, groups=each_tile(SQ, HEADS), n=P),
            dict(src=QN, sq=SQ, ms=MS, rs=RS, groups=each_tile(SQ, HEADS), n=P),
            dict(src=QR, sq=SQ[:, 0:4], ms=MS[:, 0:2], rs=RS[:, 0:2], n=64,
                 groups=[[(blk32, SQ[:, g]), (blk32, SQ[:, 2 + g])] for g in range(2)]),
            dict(src=KN, sq=SQ, ms=MS, rs=RS, groups=each_tile(SQ, HEADS), n=P),
            dict(src=xT, sq=hT, ms=xms, rs=xrs, groups=all_tiles(hT, KT), n=D),
        ]

        @block.sync
        def _(sp):
            units = Units(landed, rounded, lowered, consumed, drained)
            sp.dma_start(xT[:], t["xT"]).then_inc(x_landed, 16)
            sp.dma_start(vec[:], t["vec"]).then_inc(vec_landed, 16)

            def load(src, cols=UNIT):
                s, _, before, _, _ = units.next(False)
                if not isinstance(before, int) or before > 0:
                    sp.wait_ge(consumed[s], before)
                sp.dma_start(ring[:, s, 0:cols], src).then_inc(landed[s], 16)

            def stream(src, rounds, cols=UNIT):
                with sp.Fori(0, rounds) as i:
                    units.enter(i, drained=0)
                    for j in range(RING):
                        load(src[i * RING + j], cols)
                units.leave(rounds)

            w = t["w_mix"]
            for j in range(RING):
                load(w[j])
            sp.dma_start(cst[:], t["cst"]).then_inc(cst_landed, 16)
            sp.dma_start(sel[:], t["sel"]).then_inc(cst_landed, 16)
            sp.dma_start(w_if[:], t["w_if"]).then_inc(cst_landed, 16)
            sp.dma_start(hmask, t["hmask"]).then_inc(hmask_landed, 16)
            for j in range(RING, 10):
                load(w[j])
            stream(w[10:46], 9)
            for part in range(2):
                load(t["w_qk"][part], 8 * ML_DH)
            stream(t["w_gates"][0:24], 6)
            for part in range(2):
                load(t["s5_b"][part])
            stream(t["w_gates"][24:48], 6)
            for part in range(2):
                load(t["s5_c"][part])
            load(t["w_glu"][0])
            stream(t["w_branch"], 4)
            stream(t["w_out"], 4)
            stream(t["w_up"], 22)
            stream(t["w_down"], 16, DOWN * P)
            stream(t["w_in2"][0:24], 6)
            for j in (24, 25):
                load(t["w_in2"][j])
            stream(t["w_in2"][26:34], 2)
            for j in range(3):
                load(t["w_uq"][j])
            for j in range(4):
                load(t["w_ukv"][j])
            sp.dma_start(band, t["band"]).then_inc(band_landed, 16)
            stream(t["w_in2"][34:66], 8)
            stream(t["w_mix2"], 4)
            stream(t["w_o2"], 4)
            stream(t["w_up2"], 22)
            stream(t["w_down2"], 16, DOWN * P)
            for b in range(2):
                sp.wait_ge(down_drained[b], 1 + 2 * KT // 2)
            sp.dma_start(out, xT[:]).then_inc(x_stored, 16)
            sp.wait_ge(x_stored, 16)

        @block.tensor
        def _(pe):
            units = Units(landed, rounded, lowered, consumed, drained)
            down_free = [Count(s) for s in down_drained]
            for c in down_free:
                c.base = 1
            norm = [0]

            def mm(o, lhsT, rhs, first=True, last=True):
                return nc.tensor.matmul(o, lhsT, rhs, start=first, stop=last)

            def take():
                s, there, _, _, _ = units.next(False)
                pe.wait_ge(landed[s], there)
                return s

            def unit(body):
                s, there, _, _, free = units.next()
                pe.wait_ge(landed[s], there)
                if not isinstance(free, int) or free > 0:
                    pe.wait_ge(drained[s], free)
                body(s).then_inc(consumed[s], 1)

            def unit_split(body):
                s, _, _, _, free = units.next(split=True)
                pe.wait_ge(lowered[s], units.lowered[s].value())
                if not isinstance(free, int) or free > 0:
                    pe.wait_ge(drained[s], free)
                body(s).then_inc(consumed[s], 1)

            def rounds(n, body):
                with pe.Fori(0, n) as i:
                    units.enter(i)
                    for j in range(RING):
                        unit(body)
                units.leave(n)

            def rounds_split(n, body):
                with pe.Fori(0, n) as i:
                    units.enter(i, split=1)
                    for j in range(RING):
                        unit_split(body)
                units.leave(n)

            def mm3(o, s, c, high, low, first, last):
                c = slice(c * P, (c + 1) * P)
                mm(o, w_high[:, s, c], high, first, False)
                mm(o, w_high[:, s, c], low, False, False)
                return mm(o, w_low[:, s, c], high, False, last)

            def project_split(high, low, waits=None):
                def body(s):
                    for k in range(KT):
                        if waits:
                            waits(k)
                        last = mm3(bank[s][:, 0], s, k, high[:, k], low[:, k], k == 0, k == KT - 1)
                    return last
                return body

            splits = [0]

            def after_norm(high, low):
                n = splits[0]
                splits[0] += 1

                def waits(k):
                    if k == 0:
                        pe.wait_ge(h_lowered_pool, 2 * n + 1)
                    if k == 4:
                        pe.wait_ge(h_lowered_pool, 2 * n + 2)
                    if k == 8:
                        pe.wait_ge(h_lowered_vector, 2 * n + 1)
                    if k == 12:
                        pe.wait_ge(h_lowered_vector, 2 * n + 2)
                unit_split(project_split(high, low, waits))

            def project(s):
                for k in range(KT):
                    last = mm(bank[s][:, 0], ring[:, s, k * P:(k + 1) * P], hT[:, k], k == 0, k == KT - 1)
                return last

            def project_tokens(s):
                for b in range(TB):
                    for k in range(KT):
                        last = mm(bank[s][:, b, 0:P], hT[:, k, b * P:(b + 1) * P], ring[:, s, k * P:(k + 1) * P],
                                  k == 0, k == KT - 1)
                return last

            def drained_all():
                for s, n in units.all_drained():
                    pe.wait_ge(s, n)

            def sum_squares():
                n = NORMS[norm[0]]
                norm[0] += 1
                pe.wait_ge(norm_squared, norm[0])
                for g, parts in enumerate(n["groups"]):
                    for k, (one, sq) in enumerate(parts):
                        last = mm(bank[4 + g // 2][:, g % 2], one, sq, k == 0, k == len(parts) - 1)
                last.then_inc(norm_summed, 1)

            def banks_back():
                pe.wait_ge(norm_mean, norm[0])

            def down(acts_before):
                pe.wait_ge(acts_lowered, acts_before + SPLIT_UP)
                with pe.Fori(0, 8) as i:
                    units.enter(i, turns=2, drained=0, split=1)
                    for c in down_free:
                        c.enter(i, 1)
                    for b in range(2):
                        pe.wait_ge(down_drained[b], down_free[b].value())
                        down_free[b].add()
                        for q in range(4):
                            s, _, _, _, _ = units.next(False, split=True)
                            pe.wait_ge(lowered[s], units.lowered[s].value())
                            for k in range(DOWN):
                                n = q * DOWN + k
                                if n == SPLIT_UP:
                                    pe.wait_ge(acts_lowered, acts_before + SPLIT_UP + 1)
                                last = mm3(bank[4 + b][:, 0], s, k, acts_high[:, n], acts_low[:, n],
                                           n == 0, n == FF_TILES - 1)
                            last.then_inc(consumed[s], 1)
                units.leave(8)
                for c in down_free:
                    c.leave(8)

            pe.wait_ge(ones_set, 1)
            sum_squares()
            after_norm(mix_high, mix_low)
            for j in range(9):
                unit_split(project_split(mix_high, mix_low))
            rounds(3, project_tokens)
            rounds_split(6, project_split(mix_high, mix_low))

            pe.wait_ge(cst_landed, 48)
            for g in range(2):
                for k in range(KT):
                    last = mm(bank[7][0:ML, g], w_if[:, k, g * ML:(g + 1) * ML], hT[:, k], k == 0, k == KT - 1)
            last.then_inc(if_summed, 1)

            pe.wait_ge(conv_act, 1)
            for part in range(2):
                s = take()
                if part:
                    pe.wait_ge(qk_ready, 1)
                for h in range(ML):
                    for o, q0, q1, e in PIECES[h]:
                        for n, (k, _, _, _) in enumerate(PIECES[h]):
                            c = (2 * h + n) * ML_DH + e
                            last = mm(bank[4 + o // 2][q0:q1, o % 2], ring[:, s, c:c + q1 - q0], CA[:, k],
                                      n == 0, n == 1)
                last.then_inc(consumed[s], 1)
            rounds(1, project)

            pe.wait_ge(rows_ready, 1)
            pe.wait_ge(qk_ready, 2)
            for b in range(TB):
                mm(bank[4][:, 0, b * ML:(b + 1) * ML], rows[:, 2, b * P:(b + 1) * P], ident[0:ML, 0:ML])
            for h in range(ML):
                last = mm(bank[5 + h // 2][:, h % 2], sel[:, h], rows[:, 3])
            last.then_inc(cast_done, 1)
            pe.wait_ge(rows_thr, 1)
            pe.wait_ge(cast_taken, 1)
            for h in range(ML):
                last = mm(bank[5 + h // 2][:, h % 2], sel[:, h], rows[:, 5])
            last.then_inc(cast_done, 1)
            pe.wait_ge(cast_taken, 2)
            for h in range(ML):
                for b in range(TB):
                    for n, (k, p0, p1, _) in enumerate(PIECES[h]):
                        last = mm(bank[4 + h][:, b, b * P:T], KH[p0:p1, k, b * P:(b + 1) * P],
                                  QH[p0:p1, k, b * P:T], n == 0, n == 1)
                last.then_inc(ml_scored, 1)
            rounds(1, project)
            pe.wait_ge(ml_p, ML)
            for h in range(ML):
                mm(bank[4 + h // 2][:, h % 2], ones[:], PM[:, h, 0:T], True, False)
                last = mm(bank[4 + h // 2][:, h % 2, P:T], ones[:], PM[:, h, T:T + P], False, True)
            last.then_inc(ml_den, 1)
            pe.wait_ge(ml_rden, 1)
            vals = VN[:, :, 6:12].rearrange("p b h c -> p b (h c)")
            for h in range(ML):
                for k, p0, p1, e in PIECES[h]:
                    c = h * ML_DH + e
                    mm(bank[4 + k // 2][p0:p1, k % 2], vals[:, 0, c:c + p1 - p0], PM[:, h, 0:T], True, False)
                    last = mm(bank[4 + k // 2][p0:p1, k % 2, P:T], vals[:, 1, c:c + p1 - p0],
                              PM[:, h, T:T + P], False, True)
            last.then_inc(ml_num, 1)
            rounds(1, project)
            sum_squares()
            banks_back()

            for lvl in range(9):
                pe.wait_ge(hg_x, lvl + 1)
                if lvl:
                    pe.wait_ge(hg_taken, lvl)
                X = [HX0, HX1][lvl % 2]
                for h in range(HG):
                    if lvl == 8:
                        last = mm(bank_row[4 + h // 4][:, h % 4 * P:(h % 4 + 1) * P], X[:, h, 0:P], X[:, h, P:T])
                    else:
                        for b in range(TB):
                            c = slice(b * P, (b + 1) * P)
                            last = mm(bank[4 + h // 2][:, h % 2, c], (X if lvl else HK)[:, h, c],
                                      (X if lvl else HQ)[:, h, c])
                last.then_inc(hg_scored, 1)
                if lvl in (1, 4):
                    rounds(1, project)
            pe.wait_ge(hg_taken, 9)
            for h in range(HG):
                mm(bank[4 + h // 2][:, h % 2, 0:P], VN[:, 0, h], PD[:, h, 0:P])
                mm(bank[4 + h // 2][:, h % 2, P:T], VN[:, 0, h], PO[:, h], True, False)
                last = mm(bank[4 + h // 2][:, h % 2, P:T], VN[:, 1, h], PD[:, h, P:T], False, True)
            last.then_inc(hg_out, 1)
            rounds(1, project)
            sum_squares()
            banks_back()

            sre, sim_ = take(), take()
            pe.wait_ge(norm_done, 3)
            for n in range(S5_STATES):
                if n >= 4:
                    pe.wait_ge(s5_in, n - 3)
                c = slice(n * P, (n + 1) * P)
                last = mm(bank[4 + n % 4][:, 0], ring[:, sre, c], MT[:, U0 + n // 4])
                if n == S5_STATES - 1:
                    last.then_inc(consumed[sre], 1)
                last = mm(bank[4 + n % 4][:, 1], ring[:, sim_, c], MT[:, U0 + n // 4])
                last.then_inc(consumed[sim_] if n == S5_STATES - 1 else s5_fed, 1)
            rounds(6, project)

            cre, cim = take(), take()
            for f in range(S5_TILES):
                pe.wait_ge(s5_states, f + 1)
                for part, (slot, st) in enumerate(((cre, SR), (cim, SI))):
                    for n in range(4):
                        c = (4 * f + n) * P
                        last = mm(bank[4 + f][:, part], ring[:, slot, c:c + P], st[:, 4 * f + n], n == 0, n == 3)
                    if f == S5_TILES - 1:
                        last.then_inc(consumed[slot], 1)
            pe.wait_ge(s5_gelu, 1)
            s = take()
            for f in range(S5_TILES):
                for k in range(S5_TILES):
                    c = (f * S5_TILES + k) * P
                    last = mm(bank[4 + f // 2][:, f % 2], ring[:, s, c:c + P], GA[:, k], k == 0, k == 3)
            last.then_inc(consumed[s], 1)

            Y = [MT[:, U0 + k] for k in range(4)] + [HQ[:, k] for k in range(6)] + [MT[:, O0 + k] for k in range(6)]

            def branches(s):
                for o, lo, hi in ((bank[s][:, 0], 0, 4), (bank[s][:, 1], 4, 10), (bank[4 + s][:, 0], 10, 16)):
                    for k in range(lo, hi):
                        last = mm(o, ring[:, s, k * P:(k + 1) * P], Y[k], k == lo, k == hi - 1)
                return last

            pe.wait_ge(s5_done, 1)
            rounds(4, branches)
            drained_all()
            pe.wait_ge(merged_lowered, KT)
            rounds_split(4, project_split(out_high, h_low))
            sum_squares()
            after_norm(up_high, h_low)
            for j in range(3):
                unit_split(project_split(up_high, h_low))
            rounds_split(21, project_split(up_high, h_low))
            down(0)
            sum_squares()
            banks_back()
            sum_squares()
            after_norm(in2_high, in2_low)
            unit_split(project_split(in2_high, in2_low))
            rounds_split(6, project_split(in2_high, in2_low))
            rounds(2, project_tokens)
            sum_squares()
            banks_back()
            sum_squares()
            banks_back()

            def latent(src):
                def body(s):
                    for o in range(4):
                        for k in range(4):
                            c = (o * 4 + k) * P
                            last = mm(bank[s if o < 2 else 4 + s][:, o % 2], ring[:, s, c:c + P], src[:, k],
                                      k == 0, k == 3)
                    return last
                return body

            def latent_tokens(s):
                for b in range(TB):
                    for k in range(4):
                        last = mm(bank_row[s + 4 * b], CKV[:, k, b * P:(b + 1) * P],
                                  ring[:, s, k * 512:(k + 1) * 512], k == 0, k == 3)
                return last

            pe.wait_ge(norm_done, 8)
            for j in range(3):
                unit(latent(CQ))
            for j in range(2):
                unit(latent(CKV))
            for j in range(2):
                unit(latent_tokens)
            drained_all()
            for j in range(6):
                sum_squares()
                banks_back()
                if j in (0, 2, 4):
                    rounds(1, project)

            pe.wait_ge(norm_done, 14)

            def scores(h):
                if h >= 2:
                    pe.wait_ge(at_exp, h - 1)
                for b in range(TB):
                    c = slice(b * P, (b + 1) * P)
                    if h < HEADS:
                        r = slice(32 * (h % 4), 32 * (h % 4) + 32)
                        mm(bank[4 + h % 2][:, b], QN[:, h, c], KN[:, h], True, False)
                        mm(bank[4 + h % 2][:, b], QR[r, h // 4, c], KR[r, 0], False, False)
                        last = mm(bank[4 + h % 2][:, b], QR[r, 2 + h // 4, c], KR[r, 1], False, True)
                    else:
                        last = mm(bank[4 + h % 2][:, b], QD[:, h - HEADS, c], KD[:, h - HEADS])
                last.then_inc(at_scored, 1)

            scores(0)
            for h in range(2 * HEADS):
                if h + 1 < 2 * HEADS:
                    scores(h + 1)
                if h in (0, 3, 6, 9, 12):
                    rounds(1, project)
                pe.wait_ge(at_p, h + 1)
                if h:
                    pe.wait_ge(at_pt, h)
                for b in range(TB):
                    for c in range(TB):
                        last = nc.tensor.transpose(bank[6][:, c, b * P:(b + 1) * P],
                                                   ES[h % 2][:, b, c * P:(c + 1) * P], ident)
                last.then_inc(at_turned, 1)
                pe.wait_ge(at_pt, h + 1)
                if h:
                    pe.wait_ge(at_kept, h)
                for b in range(TB):
                    last = mm(bank[7][:, 0], (VM if h < HEADS else VD)[:, b, h % HEADS], PS[h % 2][:, b],
                              b == 0, b == TB - 1)
                last.then_inc(at_out, 1)

            def branches2(s):
                for half, y in enumerate((OA, QD)):
                    for k in range(HEADS):
                        c = (half * HEADS + k) * P
                        last = mm(bank[s][:, half], ring[:, s, c:c + P], y[:, k], k == 0, k == HEADS - 1)
                return last

            pe.wait_ge(at_kept, 2 * HEADS)
            rounds(4, branches2)
            drained_all()
            pe.wait_ge(merged_lowered, 2 * KT)
            rounds_split(4, project_split(out2_high, h_low))
            sum_squares()
            after_norm(up_high, h_low)
            for j in range(3):
                unit_split(project_split(up_high, h_low))
            rounds_split(21, project_split(up_high, h_low))
            drained_all()
            down(SPLIT_UP + 1)

        @block.scalar
        def _(act):
            units = Units(landed, rounded, lowered, consumed, drained)
            chain = Count(act_chain)
            norm = [0]
            A = nc.scalar.activation

            def link(ins):
                ins.then_inc(act_chain, 1)
                chain.add()
                act.wait_ge(act_chain, chain.value())

            def drain(body):
                s, _, _, there, _ = units.next()
                act.wait_ge(consumed[s], there)
                body(s).then_inc(drained[s], 1)

            def rounds(n, body, split=0):
                with act.Fori(0, n) as i:
                    units.enter(i)
                    if split:
                        ahead.enter(i, drained=0, split=1)
                    for j in range(RING):
                        if split:
                            round_weights(UNIT)
                        drain(lambda s: body(s, i * RING + j))
                units.leave(n)
                if split:
                    ahead.leave(n)

            ahead = Units(landed, rounded, lowered, consumed, drained)

            def round_weights(cols):
                s, there, _, _, _ = ahead.next(False, split=True)
                act.wait_ge(landed[s], there)
                A(w_high[:, s, 0:cols], ring[:, s, 0:cols], ACT.Copy).then_inc(rounded[s], 1)

            def round_rounds(n, cols):
                with act.Fori(0, n) as i:
                    ahead.enter(i, drained=0, split=1)
                    for j in range(RING):
                        round_weights(cols)
                ahead.leave(n)

            splits = [0]

            def round_input(high):
                for g in range(4):
                    act.wait_ge(h_scaled, 4 * splits[0] + g + 1)
                    A(high[:, 4 * g:4 * g + 4], hT[:, 4 * g:4 * g + 4], ACT.Copy).then_inc(h_rounded, 1)
                splits[0] += 1

            merged = Count(merged_rounded)

            def round_merged(n, high):
                s, _, _, _, free = units.next()
                act.wait_ge(drained[s], free + 1)
                A(high[:, bass.ds(n, 1)], hT[:, bass.ds(n, 1)], ACT.Copy).then_inc(merged_rounded, 1)

            def merge(high):
                with act.Fori(0, 3) as i:
                    units.enter(i)
                    for j in range(RING):
                        round_merged(i * RING + j, high)
                units.leave(3)
                ahead.skip(units.pos + RING - ahead.pos, False)
                for j in range(RING):
                    if j >= RING - AHEAD:
                        round_weights(UNIT)
                    round_merged(3 * RING + j, high)

            def skip(n, turns=1, kept=True):
                units.skip(n * RING * turns, kept)

            def square():
                n = NORMS[norm[0]]
                norm[0] += 1
                if norm[0] > 1:
                    act.wait_ge(norm_done, norm[0] - 1)
                A(n["sq"][:] if n["sq"] is hT else n["sq"], n["src"][:] if n["src"] is xT else n["src"],
                  ACT.Square).then_inc(norm_squared, 1)

            def root():
                n = NORMS[norm[0] - 1]
                act.wait_ge(norm_mean, norm[0])
                m, r = ((n[k][:] if n[k] in (xms, xrs) else n[k]) for k in ("ms", "rs"))
                A(r, m, ACT.Sqrt).then_inc(norm_rooted, 1)

            def drained_all():
                for s, n in units.all_drained():
                    act.wait_ge(s, n)

            act.wait_ge(x_landed, 16)
            square()
            root()
            for j in range(AHEAD):
                round_weights(UNIT)
            round_input(mix_high)

            for j in range(10):
                if j < 10 - AHEAD:
                    round_weights(UNIT)
                drain(lambda s: A(MT[:, U0 + j], bank[s][:, 0], ACT.Copy))
            act.wait_ge(vec_landed, 16)
            c = VAT["log_dt"]
            A(s5c[:, 0], vec[:, c:c + S5_STATES], ACT.Exp).then_inc(s5_fn, 1)
            act.wait_ge(s5_arg, 1)
            A(s5c[:, 7], s5c[:, 1], ACT.Exp)
            act.wait_ge(lb_arg, 1)
            A(lb[:, 1], lb[:, 0], ACT.Exp).then_inc(lb_exp, 1)
            A(s5c[:, 8], s5c[:, 4], ACT.Sin)
            A(s5c[:, 9], s5c[:, 6], ACT.Sin).then_inc(s5_fn, 1)

            rounds(2, lambda s, n: A(VN[:, :, bass.ds(n, 1)].rearrange("p a b c -> p a (b c)"),
                                     bank[s][:, :, 0:P], ACT.Copy))
            ahead.skip(12, False)
            for j in range(RING):
                if j >= RING - AHEAD:
                    round_weights(UNIT)
                drain(lambda s: A(VN[:, :, 2 * RING + j], bank[s][:, :, 0:P], ACT.Copy))
            rounds(3, lambda s, n: A(MT[:, bass.ds(n + F0, 1)], bank[s][:, 0:1], ACT.Sigmoid), split=1)
            rounds(2, lambda s, n: A(MT[:, bass.ds(n + Q0, 1)], bank[s][:, 0:1], ACT.Silu), split=1)
            for j in range(RING):
                if j < AHEAD:
                    round_weights(UNIT)
                drain(lambda s: A(MT[:, Q0 + 2 * RING + j], bank[s][:, 0], ACT.Silu))

            def gates(at, n):
                def body(s, m):
                    if isinstance(m, int):
                        return A(G[:, at + m], bank[s][:, 0], ACT.Sigmoid)
                    return A(G[:, bass.ds(m + at, 1)], bank[s][:, 0:1], ACT.Sigmoid)
                rounds(n, body)

            act.wait_ge(conv_ready, 1)
            A(CA, CA, ACT.Silu).then_inc(conv_act, 1)
            act.wait_ge(rows_abs, 1)
            link(A(rows[:, 0], rows[:, 0], ACT.Exp, scale=-1.0))
            A(rows[:, 0], rows[:, 0], ACT.Ln, bias=1.0).then_inc(rows_log, 1)
            for dst, scale in ((QH, 1.0), (KH, ML_DH ** -0.5)):
                s, _, _, there, _ = units.next(False)
                act.wait_ge(consumed[s], there)
                for j in range(3):
                    last = A(dst[:, 2 * j:2 * j + 2], bank[4 + j][:], ACT.Copy, scale=scale)
                last.then_inc(qk_ready, 1)
            act.wait_ge(rows_ready, 1)
            A(rows[:, 5], rows[:, 4], ACT.Exp, scale=-1.0).then_inc(rows_thr, 1)
            gates(0, 1)
            act.wait_ge(cast_done, 1)
            A(acol[:], bank[4][:, 0, 0:TB * ML].rearrange("p (b h) -> p b h", h=ML), ACT.Copy)
            for j in range(2):
                last = A(MB[:, 2 * j:2 * j + 2], bank[5 + j][:], ACT.Copy)
            last.then_inc(cast_taken, 1)
            act.wait_ge(cast_done, 2)
            for j in range(2):
                last = A(TH[:, 2 * j:2 * j + 2], bank[5 + j][:], ACT.Copy)
            last.then_inc(cast_taken, 1)
            for h in range(ML):
                act.wait_ge(ml_arg, h + 1)
                A(PM[:, h], PM[:, h], ACT.Exp, scale=-1.0).then_inc(ml_exp, 1)
            gates(4, 1)
            gates(8, 1)
            act.wait_ge(ml_h, 1)
            square()
            root()

            gates(12, 1)
            gates(16, 1)
            act.wait_ge(hg_out, 1)
            for j in range(3):
                last = A(HO[:, 2 * j:2 * j + 2], bank[4 + j][:], ACT.Copy)
            link(last)
            square()
            gates(20, 1)
            root()

            units.next(False)
            _s, _, _, last_fed, _ = units.next(False)
            for n in range(S5_STATES):
                if n < S5_STATES - 1:
                    act.wait_ge(s5_fed, n + 1)
                else:
                    act.wait_ge(consumed[_s], last_fed)
                A(SR[:, n], bank[4 + n % 4][:, 0], ACT.Copy, scale=s5c[:, 11, n:n + 1])
                A(SI[:, n], bank[4 + n % 4][:, 1], ACT.Copy, scale=s5c[:, 11, n:n + 1]).then_inc(s5_scaled, 1)
            gates(24, 5)
            act.wait_ge(s5_tabled, S5_TILES)
            gates(44, 1)
            units.next(False)
            units.next(False)
            act.wait_ge(s5_pre, 1)
            A(GA, GA, ACT.Gelu_apprx_tanh).then_inc(s5_gelu, 1)
            s, _, _, there, _ = units.next(False)
            act.wait_ge(consumed[s], there)
            for f in range(S5_TILES):
                last = A(MT[:, U0 + f], bank[4 + f // 2][:, f % 2], ACT.Sigmoid, bias=v("b_glu", f))
            last.then_inc(s5_gate, 1)
            merge(out_high)
            round_rounds(4, UNIT)
            skip(4)
            drained_all()
            square()
            root()
            round_input(up_high)

            acts = Count(ff_done)

            def round_act(n):
                A(acts_high[:, bass.ds(n, 1)], ACTS[:, bass.ds(n, 1)], ACT.Copy).then_inc(acts_rounded, 1)

            def conv_round(i, cols, split):
                for j in range(2):
                    s, _, _, _, free = units.next()
                    round_weights(cols[2 * j])
                    act.wait_ge(drained[s], free + 1)
                    A(cv[:, 2 * j], cv[:, 2 * j], ACT.Silu).then_inc(silu_pair, 1)
                    units.next()
                    round_weights(cols[2 * j + 1])
                    acts.add()
                    if split:
                        act.wait_ge(ff_done, acts.value())
                        round_act(i * 2 + j)

            def conv_rounds(first, n, split):
                with act.Fori(0, n) as i:
                    units.enter(i)
                    ahead.enter(i, drained=0, split=1)
                    acts.enter(i, 2)
                    conv_round(i + first if first else i, [UNIT] * RING, split)
                units.leave(n)
                ahead.leave(n)
                acts.leave(n)

            def last_acts():
                A(acts_high[:, SPLIT_UP:], ACTS[:, SPLIT_UP:], ACT.Copy).then_inc(acts_rounded, 1)

            conv_rounds(0, SPLIT_UP // 2, True)
            conv_rounds(SPLIT_UP // 2, 21 - SPLIT_UP // 2, False)
            conv_round(21, [UNIT] * 2 + [DOWN * P] * 2, False)
            act.wait_ge(ff_done, FF_TILES)
            last_acts()
            round_rounds(15, DOWN * P)
            for j in range(2):
                round_weights(DOWN * P)
            for j in range(AHEAD):
                round_weights(UNIT)
            skip(16, kept=False)
            for b in range(2):
                act.wait_ge(down_drained[b], 1 + KT // 2)
            square()
            root()
            square()
            root()
            round_input(in2_high)

            rounds(6, lambda s, n: A(P2[:, bass.ds(n, 1)], bank[s][:, 0:1], ACT.Copy), split=1)
            for j in (24, 25):
                drain(lambda s: A(P2[:, j], bank[s][:, 0], ACT.Copy))
            rounds(2, lambda s, n: A(VD[:, :, bass.ds(n, 1)].rearrange("p a b c -> p a (b c)"),
                                     bank[s][:, :, 0:P], ACT.Copy))
            drained_all()
            square()
            root()
            square()
            root()

            def two_banks(a, b):
                def body(s):
                    A(a, bank[s][:], ACT.Copy)
                    return A(b, bank[4 + s][:], ACT.Copy)
                return body

            def tokens(j):
                def body(s):
                    A(VM[:, 0, 4 * j:4 * j + 4].rearrange("p h c -> p (h c)"), bank_row[s], ACT.Copy)
                    return A(VM[:, 1, 4 * j:4 * j + 4].rearrange("p h c -> p (h c)"), bank_row[4 + s], ACT.Copy)
                return body

            for dst, j in ((QN, 0), (QN, 1), (QR, 0), (KN, 0), (KN, 1)):
                drain(two_banks(dst[:, 4 * j:4 * j + 2], dst[:, 4 * j + 2:4 * j + 4]))
            for j in range(2):
                drain(tokens(j))
            drained_all()

            def gates2(at, n):
                for j in range(RING * n):
                    drain(lambda s: A(G2[:, at + j], bank[s][:, 0], ACT.Sigmoid, bias=v("b_gate", at + j)))

            at = 0
            for j in range(6):
                square()
                root()
                if j in (0, 2, 4):
                    gates2(at, 1)
                    at += RING

            act.wait_ge(band_landed, 16)
            for h in range(2 * HEADS):
                e, p = ES[h % 2], PS[h % 2]
                if h == HEADS:
                    for g in (0, 1):
                        A(BS[g], band[:, 0:2], ACT.Copy, scale=SLOPES[g]).then_inc(at_bias, 1)
                act.wait_ge(at_max, h + 1)
                if h >= 2:
                    act.wait_ge(at_turned, h - 1)
                if h < HEADS:
                    for b in range(TB):
                        last = A(e[:, b], bank[4 + h % 2][:, b], ACT.Exp, bias=small[:, h % 2, 2 + b:3 + b],
                                 scale=192 ** -0.5, accum_out=small[:, h % 2, 4 + b:5 + b])
                else:
                    for b in range(TB):
                        last = A(e[:, b], e[:, b], ACT.Exp, bias=small[:, h % 2, 2 + b:3 + b])
                last.then_inc(at_exp, 1)
                if HEADS <= h < 2 * HEADS - 2:
                    A(BS[h % 2], band[:, 0:2], ACT.Copy, scale=SLOPES[h + 2 - HEADS]).then_inc(at_bias, 1)
                if h in (0, 3, 6, 9, 12):
                    gates2(at, 1)
                    at += RING
                act.wait_ge(at_turned, h + 1)
                if h >= 2:
                    act.wait_ge(at_out, h - 1)
                A(p, bank[6][:], ACT.Copy).then_inc(at_pt, 1)
                act.wait_ge(at_out, h + 1)
                A((OA if h < HEADS else QD)[:, h % HEADS], bank[7][:, 0], ACT.Copy).then_inc(at_kept, 1)
            merge(out2_high)
            round_rounds(4, UNIT)
            skip(4)
            drained_all()
            square()
            root()
            round_input(up_high)

            def gate_round(i, cols, split):
                for j in range(2):
                    s, _, _, there, _ = units.next()
                    su, _, _, _, used = units.next()
                    round_weights(cols[2 * j])
                    act.wait_ge(consumed[s], there)
                    act.wait_ge(drained[su], used)
                    A(cv[:, 2 * j], bank[s][:, 0], ACT.Silu).then_inc(drained[s], 1)
                    round_weights(cols[2 * j + 1])
                    if split:
                        act.wait_ge(drained[su], used + 1)
                        round_act(i * 2 + j)

            def gate_rounds(first, n, split):
                with act.Fori(0, n) as i:
                    units.enter(i)
                    ahead.enter(i, drained=0, split=1)
                    gate_round(i + first if first else i, [UNIT] * RING, split)
                units.leave(n)
                ahead.leave(n)

            gate_rounds(0, SPLIT_UP // 2, True)
            gate_rounds(SPLIT_UP // 2, 21 - SPLIT_UP // 2, False)
            gate_round(21, [UNIT] * 2 + [DOWN * P] * 2, False)
            drained_all()
            last_acts()
            round_rounds(15, DOWN * P)
            for j in range(2):
                round_weights(DOWN * P)

        @block.vector
        def _(dve):
            V = nc.vector
            units = Units(landed, rounded, lowered, consumed, drained)
            chain = Count(dve_chain)
            norm = [0]
            M, ADD, SUB, MAX, MIN = ALU.mult, ALU.add, ALU.subtract, ALU.max, ALU.min

            def link(ins):
                ins.then_inc(dve_chain, 1)
                chain.add()
                dve.wait_ge(dve_chain, chain.value())

            def stt(o, a, s, b, op0=M, op1=M, **kw):
                return V.scalar_tensor_tensor(out=o, in0=a, scalar=s, in1=b, op0=op0, op1=op1, **kw)

            def tt(o, a, b, op=M):
                return V.tensor_tensor(o, a, b, op)

            ahead = Units(landed, rounded, lowered, consumed, drained)

            def lower_weights(cols):
                s, _, _, _, _ = ahead.next(False, split=True)
                dve.wait_ge(rounded[s], ahead.rounded[s].value())
                tt(w_low[:, s, 0:cols], ring[:, s, 0:cols], w_high[:, s, 0:cols].bitcast(F32), SUB)\
                    .then_inc(lowered[s], 1)

            def lower_rounds(n, cols):
                with dve.Fori(0, n) as i:
                    ahead.enter(i, drained=0, split=1)
                    for j in range(RING):
                        lower_weights(cols)
                ahead.leave(n)

            splits = [0]

            def normalise_split(gain, high, low):
                rs = reciprocal_root()
                for k in range(KT):
                    last = stt(hT[:, k], xT[:, k], v(gain, k), rs)
                    if k % 4 == 3:
                        last.then_inc(h_scaled, 1)
                if splits[0] == 0:
                    lower_weights(UNIT)
                for g in (2, 3):
                    c = slice(4 * g, 4 * g + 4)
                    dve.wait_ge(h_rounded, 4 * splits[0] + g + 1)
                    last = tt(low[:, c], hT[:, c], high[:, c].bitcast(F32), SUB)
                    last.then_inc(h_lowered_vector, 1)
                dve.wait_ge(h_lowered_pool, 2 * splits[0] + 2)
                splits[0] += 1
                V.tensor_copy(xtmp[:, 0:1], rs[:, 0:1]).then_inc(norm_done, 1)

            def reciprocal_root():
                n = NORMS[norm[0]]
                norm[0] += 1
                dve.wait_ge(norm_summed, norm[0])
                G_ = len(n["groups"])
                one = n["ms"] is xms
                ms, rs = (n["ms"][:], n["rs"][:]) if one else (n["ms"], n["rs"])
                if G_ == 1:
                    last = V.tensor_scalar(ms if one else ms[:, 0], bank[4][:, 0], 1.0 / n["n"], EPS, M, ADD)
                else:
                    for j in range(G_ // 2):
                        last = V.tensor_scalar(ms[:, 2 * j:2 * j + 2], bank[4 + j][:], 1.0 / n["n"], EPS, M, ADD)
                last.then_inc(norm_mean, 1)
                dve.wait_ge(norm_rooted, norm[0])
                tmp = xtmp[:] if one else n["sq"][:, 0:G_]
                link(V.reciprocal(rs, rs))
                link(tt(tmp, ms, rs))
                link(tt(tmp, tmp, rs))
                link(V.tensor_scalar(tmp, tmp, -0.5, 1.5, M, ADD))
                link(tt(rs, rs, tmp))
                return rs

            def normalise(dst, src, gain):
                rs = reciprocal_root()
                for k in range(KT):
                    last = stt(dst[:, k], src[:, k], v(gain, k), rs)
                last.then_inc(norm_done, 1)

            def drained_all():
                for s, n in units.all_drained():
                    dve.wait_ge(s, n)

            def skip(n, kept=True):
                units.skip(n * RING, kept)

            V.memset(ones[:], 1.0).then_inc(ones_set, 1)
            for b in range(2):
                V.memset(small[:, b], 0.0).then_inc(down_drained[b], 1)
            dve.wait_ge(vec_landed, 16)
            dve.wait_ge(x_landed, 16)
            normalise_split("mix_norm", mix_high, mix_low)
            for j in range(9):
                lower_weights(UNIT)

            c = VAT["lam_re"]
            lr, li = vec[:, c:c + S5_STATES], vec[:, c + S5_STATES:c + 2 * S5_STATES]
            dt_, e_, th, kk, r1, kc, r2, mag, sn, cs, den, cr, ci, nci, t1, am1 = (s5c[:, j] for j in range(16))
            dve.wait_ge(s5_fn, 1)
            link(tt(e_, lr, dt_))
            link(tt(th, li, dt_))

            def reduced(o, k, shift):
                link(V.tensor_scalar(k, th, 1.0 / TWO_PI, shift / TWO_PI, M, ADD))
                link(V.tensor_scalar(k, k, ROUND, None, ADD))
                link(V.tensor_scalar(k, k, ROUND, None, SUB))
                link(stt(o, k, -PI_HI, th, M, ADD))
                link(stt(o, k, -PI_MID, o, M, ADD))
                link(stt(o, k, -PI_LO, o, M, ADD))
                link(V.tensor_scalar(o, o, shift, PI_IN, ADD, MIN))
                return V.tensor_scalar(o, o, -PI_IN, None, MAX)

            reduced(r1, kk, 0.0)
            reduced(r2, kc, float(np.pi / 2)).then_inc(s5_arg, 1)
            c = VAT["hg_lb"]
            tt(lb[:, 0], vec[:, c:c + HG], vec[:, c:c + HG], SUB).then_inc(lb_arg, 1)
            dve.wait_ge(lb_exp, 1)
            link(V.reciprocal(lb[:, 2], lb[:, 1]))
            link(tt(lb[:, 2], lb[:, 2], lb[:, 1]))
            link(tt(lb[:, 0], lb[:, 2], lb[:, 2], SUB))
            link(V.tensor_scalar(lb[:, 1], lb[:, 0], -1.0, 1.0, M, ADD))
            dve.wait_ge(s5_fn, 2)
            zr, zi = s5c[:, 2], s5c[:, 3]
            link(tt(zr, mag, cs))
            link(tt(zi, mag, sn))

            def unit_modulus(re, im):
                link(tt(den, re, re))
                link(tt(t1, im, im))
                link(tt(den, den, t1, ADD))
                link(V.tensor_scalar(den, den, -0.5, 1.5, M, ADD))
                link(tt(re, re, den))
                link(tt(im, im, den))

            link(V.tensor_copy(s5p[:, 0, 0], cs))
            link(V.tensor_copy(s5p[:, 0, 1], sn))
            unit_modulus(s5p[:, 0, 0], s5p[:, 0, 1])
            for k in range(1, S5_STEPS):
                a, b = s5p[:, k - 1], s5p[:, k]
                link(tt(t1, a[:, 1], a[:, 1]))
                link(tt(b[:, 0], a[:, 0], a[:, 0]))
                link(tt(b[:, 0], b[:, 0], t1, SUB))
                link(stt(b[:, 1], a[:, 0], 2.0, a[:, 1]))
                unit_modulus(b[:, 0], b[:, 1])
            for j in range(2):
                link(V.memset(powers[:, 2 * j, :, 0:1], 1.0))
                link(V.memset(powers[:, 2 * j + 1, :, 0:1], 0.0))
                tmp = xtmp[:].rearrange("p (n a) -> p n a", a=S5_SIDE)
                for k in range(4):
                    d = 1 << k
                    re, im = powers[:, 2 * j, :, 0:d], powers[:, 2 * j + 1, :, 0:d]
                    to_re, to_im = powers[:, 2 * j, :, d:2 * d], powers[:, 2 * j + 1, :, d:2 * d]
                    cw, sw = (s5p[:, 4 * j + k, c].rearrange("p (n o) -> p n o", o=1)
                              .broadcast_to([P, S5_STATES, d]) for c in range(2))
                    link(tt(to_re, re, cw))
                    link(tt(tmp[:, :, 0:d], im, sw))
                    link(tt(to_re, to_re, tmp[:, :, 0:d], SUB))
                    link(tt(to_im, re, sw))
                    link(tt(tmp[:, :, 0:d], im, cw))
                    link(tt(to_im, to_im, tmp[:, :, 0:d], ADD))
            link(tt(den, lr, lr))
            link(tt(t1, li, li))
            link(tt(den, den, t1, ADD))
            link(V.reciprocal(den, den))
            link(V.tensor_scalar(am1, zr, -1.0, None, ADD))
            link(tt(cr, am1, lr))
            link(tt(t1, zi, li))
            link(tt(cr, cr, t1, ADD))
            link(tt(cr, cr, den))
            link(tt(ci, zi, lr))
            link(tt(t1, am1, li))
            link(tt(ci, ci, t1, SUB))
            link(tt(ci, ci, den))
            link(V.tensor_scalar(nci, ci, -1.0, None, M))

            units.skip(10)
            drained_all()
            ahead.skip(12, False)
            for k in range(ML_TILES):
                x, o = MT[:, CX0 + k], CA[:, k]
                w = [v("ml_conv", 5 * k + j) for j in range(5)]
                link(V.tensor_scalar(o, x, w[3], w[4], M, ADD))
                for j in range(1, 4):
                    last = stt(o[:, j:], x[:, 0:T - j], w[3 - j], o[:, j:], M, ADD)
                    if k < ML_TILES - 1 or j < 3:
                        link(last)
            last.then_inc(conv_ready, 1)
            lower_rounds(6, UNIT)
            skip(9)
            dve.wait_ge(if_summed, 1)
            link(V.tensor_scalar(rows[:, 2], bank[7][0:ML, 0], v("b_ig", 0, ML), None, ADD))
            link(V.tensor_scalar(rows[:, 3], bank[7][0:ML, 1], v("b_fg", 0, ML), None, ADD))
            stt(rows[:, 0], rows[:, 3], -1.0, rows[:, 3], M, MAX).then_inc(rows_abs, 1)
            link(V.tensor_scalar(rows[:, 3], rows[:, 3], 0.0, None, MIN))
            dve.wait_ge(rows_log, 1)
            link(tt(rows[:, 3], rows[:, 3], rows[:, 0], SUB))
            link(V.memset(rows[:, 4], 1.0))
            link(V.tensor_tensor_scan(rows[:, 1], rows[:, 4], rows[:, 3], 0.0, M, ADD))
            link(tt(rows[:, 2], rows[:, 2], rows[:, 1], SUB))
            link(V.tensor_tensor_scan(rows[:, 3], rows[:, 2], rows[:, 2], 0.0, MAX, MAX))
            tt(rows[:, 4], rows[:, 1], rows[:, 3], ADD).then_inc(rows_ready, 1)
            units.skip(2, False)
            skip(1)
            dve.wait_ge(qk_ready, 2)
            dve.wait_ge(cast_taken, 1)
            for h in range(ML):
                V.tensor_scalar(PM[:, h, 0:T], MB[:, h], acol[:, 0, h:h + 1], 0.0, SUB, MAX)
                V.tensor_scalar(PM[:, h, T:], MB[:, h, P:], acol[:, 1, h:h + 1], 0.0, SUB, MAX).then_inc(ml_arg, 1)
            dve.wait_ge(cst_landed, 48)
            for h in range(ML):
                dve.wait_ge(ml_exp, h + 1)
                dve.wait_ge(ml_scored, h + 1)
                link(tt(PM[:, h, 0:T], PM[:, h, 0:T], bank[4 + h][:, 0]))
                link(tt(PM[:, h, T:], PM[:, h, T:], bank[4 + h][:, 1, P:]))
                for at in (0, T):
                    last = tt(PM[:, h, at:at + P], PM[:, h, at:at + P], causal)
                last.then_inc(ml_p, 1)
            skip(1)
            dve.wait_ge(cast_taken, 2)
            dve.wait_ge(ml_den, 1)
            for j in range(2):
                th = TH[:, 2 * j:2 * j + 2]
                link(stt(th, bank[4 + j][:], -1.0, th, M, MAX))
                link(tt(th, bank[4 + j][:], th, MAX))
            V.reciprocal(TH, TH).then_inc(ml_rden, 1)
            dve.wait_ge(ml_rden, 1)
            dve.wait_ge(ml_num, 1)
            for h in range(ML):
                for k, p0, p1, _ in PIECES[h]:
                    last = tt(HH[p0:p1, k], bank[4 + k // 2][p0:p1, k % 2], TH[p0:p1, h])
            last.then_inc(ml_h, 1)
            skip(1)
            rs = reciprocal_root()
            for h in range(ML):
                for k, p0, p1, _ in PIECES[h]:
                    c = VAT["ml_norm"] + k
                    link(stt(HH[p0:p1, k], HH[p0:p1, k], vec[p0:p1, c:c + 1], rs[p0:p1, h]))
            drained_all()
            tt(MT[:, O0:O0 + 6], HH, MT[:, O0:O0 + 6]).then_inc(norm_done, 1)
            dve.wait_ge(norm_done, 2)

            for h in range(HG):
                link(V.tensor_scalar(HF[:, h], HF[:, h], lb[:, 1, h:h + 1], lb[:, 0, h:h + 1], M, ADD))
            V.tensor_scalar(HK, HF, -1.0, 1.0, M, ADD).then_inc(hg_x, 1)
            V.memset(PD, 0.0)
            link(V.memset(HPR, 1.0))
            dve.wait_ge(hg_x, 1)
            dve.wait_ge(hmask_landed, 16)

            def halves(ap, B):
                return ap.rearrange("p k t -> p (k t)").rearrange("p (n two b) -> p n two b", two=2, b=B)

            def meet(lvl):
                B = 1 << (lvl - 1)
                X = [HX0, HX1][lvl % 2]
                if lvl >= 3:
                    dve.wait_ge(hg_scored, lvl - 1)
                x, q, k, pf, pr = (halves(a, B) for a in (X, HQ, HK, HF, HPR))
                tt(x[:, :, 1], q[:, :, 1], pf[:, :, 1])
                tt(x[:, :, 0], k[:, :, 0], pr[:, :, 0]).then_inc(hg_x, 1)
                if B < P:
                    n = [P, HG * T // (2 * B), B]
                    link(tt(pr[:, :, 0], pr[:, :, 0], pf[:, :, 1, B - 1:B].broadcast_to(n)))
                    link(tt(pf[:, :, 1], pf[:, :, 1], pf[:, :, 0, B - 1:B].broadcast_to(n)))

            meet(1)
            meet(2)
            for lvl in range(9):
                dve.wait_ge(hg_scored, lvl + 1)
                if lvl == 8:
                    V.tensor_copy(PO[:, 0:4].rearrange("p h c -> p (h c)"), bank_row[4])
                    V.tensor_copy(PO[:, 4:6].rearrange("p h c -> p (h c)"), bank_row[5][:, 0:2 * P]).then_inc(hg_taken, 1)
                else:
                    m = hmask[:, lvl:lvl + 1].broadcast_to([P, 4, P])
                    for j in range(3):
                        last = V.copy_predicated(PD[:, 2 * j:2 * j + 2].rearrange("p k (b c) -> p (k b) c", c=P), m,
                                                 bank_row[4 + j].rearrange("p (k c) -> p k c", c=P))
                    last.then_inc(hg_taken, 1)
                if 1 <= lvl <= 6:
                    meet(lvl + 2)
            skip(2)
            skip(1)
            rs = reciprocal_root()
            for h in range(HG):
                link(stt(HO[:, h], HO[:, h], v("hg_norm", h), rs[:, h]))
            tt(HQ, HO, MT[:, OG0:OG0 + 6]).then_inc(norm_done, 1)
            dve.wait_ge(norm_done, 3)

            units.skip(2, False)
            for n in range(S5_STATES):
                dve.wait_ge(s5_scaled, n + 1)
                stt(SR[:, n], bank[4 + n % 4][:, 1], nci[:, n:n + 1], SR[:, n], M, ADD)
                stt(SI[:, n], bank[4 + n % 4][:, 0], ci[:, n:n + 1], SI[:, n], M, ADD).then_inc(s5_in, 1)
            dve.wait_ge(s5_in, S5_STATES)
            with dve.Fori(0, S5_TILES) as i:
                chain.enter(i, 5 + 6 + 1 + 5)
                four = bass.ds(i * 4, 4)
                size = [P, 4, S5_SIDE, S5_SIDE]
                lo_c, lo_s = (powers[:, j, four].rearrange("p n (o a) -> p n o a", o=1).broadcast_to(size)
                              for j in (0, 1))
                hi_c, hi_s = (powers[:, j, four].rearrange("p n (a o) -> p n a o", o=1).broadcast_to(size)
                              for j in (2, 3))
                c4, s4, t4 = (x.rearrange("p n (a b) -> p n a b", b=S5_SIDE) for x in (turn_c, turn_s, tmp_r))
                link(tt(c4, hi_c, lo_c))
                link(tt(t4, hi_s, lo_s))
                link(tt(c4, c4, t4, SUB))
                link(tt(s4, hi_c, lo_s))
                link(tt(t4, hi_s, lo_c))
                tt(s4, s4, t4, ADD).then_inc(s5_tabled, 1)
                dve.wait_ge(s5_tabled, i + 1)
                xr, xi = SR[:, four], SI[:, four]
                link(tt(tmp_r, turn_s, xr))
                link(tt(tmp_i, turn_s, xi))
                link(tt(xr, turn_c, xr))
                link(tt(xi, turn_c, xi))
                link(tt(xr, xr, tmp_i, ADD))
                link(tt(xi, xi, tmp_r, SUB))
                for n in range(4):
                    m = mag[:, bass.ds(i * 4 + n, 1)].broadcast_to([P, T])
                    one = bass.ds(i * 4 + n, 1)
                    for o, x in ((tmp_r, SR), (tmp_i, SI)):
                        last = V.tensor_tensor_scan(o[:, n], m, x[:, one].rearrange("p k t -> p (k t)"), 0.0, M, ADD)
                link(last)
                link(tt(xr, turn_c, tmp_r))
                link(tt(xi, turn_s, tmp_r))
                link(tt(tmp_r, turn_s, tmp_i))
                link(tt(xr, xr, tmp_r, SUB))
                link(tt(tmp_i, turn_c, tmp_i))
                tt(xi, xi, tmp_i, ADD).then_inc(s5_states, 1)
            chain.leave(S5_TILES)
            skip(6)
            units.skip(1, False)
            s, _, _, there, _ = units.next(False)
            dve.wait_ge(consumed[s], there)
            for f in range(S5_TILES):
                link(stt(GA[:, f], MT[:, U0 + f], v("s5_d", f), bank[4 + f][:, 0], M, ADD))
                last = tt(GA[:, f], GA[:, f], bank[4 + f][:, 1], SUB)
            last.then_inc(s5_pre, 1)
            units.next(False)
            dve.wait_ge(s5_gate, 1)
            tt(MT[:, U0:U0 + 4], MT[:, U0:U0 + 4], GA).then_inc(s5_done, 1)

            def rounds_split(n, body):
                with dve.Fori(0, n) as i:
                    units.enter(i)
                    ahead.enter(i, drained=0, split=1)
                    for j in range(RING):
                        s, _, _, there, _ = units.next()
                        lower_weights(UNIT)
                        dve.wait_ge(consumed[s], there)
                        body(s, i * RING + j).then_inc(drained[s], 1)
                units.leave(n)
                ahead.leave(n)

            def looped(n, per, body):
                with dve.Fori(0, n) as i:
                    units.enter(i)
                    chain.enter(i, per)
                    body(i)
                units.leave(n)
                chain.leave(n)

            def gated(parts):
                def body(i):
                    for j in range(RING):
                        s, _, _, there, _ = units.next()
                        if i is None and j >= RING - AHEAD:
                            lower_weights(UNIT)
                        dve.wait_ge(consumed[s], there)
                        n = (3 if i is None else i) * RING + j
                        o = hT[:, bass.ds(n, 1)]
                        tmp = xtmp[:].rearrange("p (k t) -> p k t", k=1)
                        for m, (g, at, b, half) in enumerate(parts):
                            x = bank[b + s][:, half:half + 1]
                            gate = g[:, bass.ds(n + at, 1)]
                            if m == 0:
                                link(tt(o, gate, x))
                            else:
                                link(tt(tmp, gate, x))
                                last = tt(o, o, tmp, ADD)
                                if m < len(parts) - 1:
                                    link(last)
                        last.then_inc(drained[s], 1)
                return body

            def add_residual(s, n):
                return tt(xT[:, bass.ds(n, 1)], xT[:, bass.ds(n, 1)], bank[s][:, 0:1], ADD)

            def down(after):
                def turn(i, cols):
                    for b in range(2):
                        for q in range(4):
                            s, _, _, there, _ = units.next(False)
                            if cols[4 * b + q]:
                                lower_weights(cols[4 * b + q])
                        dve.wait_ge(consumed[s], there)
                        n = i * 2 + b
                        tt(xT[:, bass.ds(n, 1)], xT[:, bass.ds(n, 1)], bank[4 + b][:, 0:1], ADD)\
                            .then_inc(down_drained[b], 1)

                with dve.Fori(0, 7) as i:
                    units.enter(i, turns=2, drained=0)
                    ahead.enter(i, turns=2, drained=0, split=1)
                    turn(i, [DOWN * P] * 8)
                units.leave(7)
                ahead.leave(7)
                turn(7, [DOWN * P] * 6 + [after] * AHEAD)

            def merge(parts):
                body = gated(parts)
                looped(3, (2 * len(parts) - 2) * RING, body)
                ahead.skip(units.pos + RING - ahead.pos, False)
                body(None)

            merge([(G, 0, 0, 0), (G, 16, 0, 1), (G, 32, 4, 0)])
            rounds_split(4, add_residual)
            drained_all()
            normalise_split("ffn_norm", up_high, h_low)

            pairs = Count(silu_pair)

            def conv_pairs(i, cols):
                for j in range(2):
                    for half in range(2):
                        s, _, _, there, free = units.next()
                        lower_weights(cols[2 * j + half])
                        dve.wait_ge(consumed[s], there)
                        n = i * RING + (2 * j + half)
                        o, x = cv[:, 2 * j + half], bank[s][:, 0]

                        def w(c):
                            return vec[:, bass.ds(n * 4 + (VAT["ffn_conv"] + c), 1)]

                        link(V.tensor_scalar(o, x, w(2), w(3), M, ADD))
                        link(stt(o[:, 1:], x[:, 0:T - 1], w(1), o[:, 1:], M, ADD))
                        stt(o[:, 2:], x[:, 0:T - 2], w(0), o[:, 2:], M, ADD).then_inc(drained[s], 1)
                    dve.wait_ge(drained[s], free + 1)
                    pairs.add()
                    dve.wait_ge(silu_pair, pairs.value())
                    tt(ACTS[:, bass.ds(i * 2 + j, 1)], cv[:, 2 * j:2 * j + 1], cv[:, 2 * j + 1:2 * j + 2])\
                        .then_inc(ff_done, 1)

            with dve.Fori(0, 21) as i:
                units.enter(i)
                ahead.enter(i, drained=0, split=1)
                chain.enter(i, 8)
                pairs.enter(i, 2)
                conv_pairs(i, [UNIT] * RING)
            units.leave(21)
            ahead.leave(21)
            chain.leave(21)
            pairs.leave(21)
            conv_pairs(21, [UNIT] * 2 + [DOWN * P] * 2)
            down(UNIT)
            for b in range(2):
                dve.wait_ge(down_drained[b], 1 + KT // 2)
            normalise(xT, xT, "final_norm")
            dve.wait_ge(norm_done, 5)
            normalise_split("g_mix", in2_high, in2_low)

            lower_rounds(6, UNIT)
            skip(6)
            units.skip(2)
            skip(2)
            drained_all()
            for src, gain in ((CQ, "g_cq"), (CKV, "g_ckv")):
                rs = reciprocal_root()
                for k in range(4):
                    last = stt(src[:, k], src[:, k], v(gain, k), rs[:, 0])
                last.then_inc(norm_done, 1)
            units.skip(7)
            drained_all()
            cos, sin = band[:, 4:5], band[:, 5:6]

            def rope(x1, x2, n):
                c, s = cos.broadcast_to([P, n, T]), sin.broadcast_to([P, n, T])
                a, b, c2 = MS[:, 0:n], MS[:, 2:2 + n], MS[:, 4:4 + n]
                link(tt(a, x1, c))
                link(tt(b, x2, s))
                link(tt(c2, x1, s))
                link(tt(x1, a, b, SUB))
                link(tt(b, x2, c))
                tt(x2, c2, b, ADD).then_inc(norm_done, 1)

            def heads(x, gain):
                rs = reciprocal_root()
                n = x.shape[1]
                link(tt(x, x, rs))
                V.tensor_scalar(x, x, v(gain), None, M).then_inc(norm_done, 1)

            rs = reciprocal_root()
            for half in range(2):
                last = stt(KR[:, half], KR[:, half], v("g_k_rope", half), rs[:, 0])
            link(last)
            dve.wait_ge(band_landed, 16)
            rope(KR[:, 0:1], KR[:, 1:2], 1)
            heads(QD, "g_q_dil")
            heads(KD, "g_k_dil")
            skip(1)
            heads(QN, "g_q_nope")
            rs = reciprocal_root()
            for half in range(2):
                for g in range(2):
                    k = 2 * half + g
                    last = stt(QR[:, k], QR[:, k], v("g_q_rope", half), rs[:, g])
            link(last)
            rope(QR[:, 0:2], QR[:, 2:4], 2)
            heads(KN, "g_k_nope")
            skip(2)
            dve.wait_ge(norm_done, 14)

            for h in range(2 * HEADS):
                e, m = ES[h % 2], small[:, h % 2]
                s = bank[4 + h % 2]
                dve.wait_ge(at_scored, h + 1)
                if h < HEADS:
                    link(V.tensor_reduce(m[:, 0:2], s[:], axis=AX.X, op=MAX))
                    V.tensor_scalar(m[:, 2:4], m[:, 0:2], -(192 ** -0.5), None, M).then_inc(at_max, 1)
                    dve.wait_ge(at_exp, h + 1)
                else:
                    dve.wait_ge(at_bias, h - HEADS + 1)
                    if h >= 2:
                        dve.wait_ge(at_turned, h - 1)
                    link(stt(e, s[:], P ** -0.5, BS[h % 2], M, ADD))
                    link(V.tensor_reduce(m[:, 0:2], e, axis=AX.X, op=MAX))
                    V.tensor_scalar(m[:, 2:4], m[:, 0:2], -1.0, None, M).then_inc(at_max, 1)
                    dve.wait_ge(at_exp, h + 1)
                    for b in range(TB):
                        last = stt(e[:, b], e[:, b], 1.0, band[:, 2 + b], M, M, accum_out=m[:, 4 + b:5 + b])
                    link(last)
                link(V.reciprocal(m[:, 4:6], m[:, 4:6]))
                for b in range(TB):
                    last = V.tensor_scalar(e[:, b], e[:, b], m[:, 4 + b:5 + b], None, M)
                last.then_inc(at_p, 1)
            skip(5)
            merge([(G2, 0, 0, 0), (G2, 16, 0, 1)])
            rounds_split(4, add_residual)
            drained_all()
            normalise_split("g_ffn", up_high, h_low)

            def gate_pairs(i, cols):
                for j in range(2):
                    lower_weights(cols[2 * j])
                    lower_weights(cols[2 * j + 1])
                    sg, _, _, _, gate_free = units.next()
                    s, _, _, there, _ = units.next()
                    dve.wait_ge(consumed[s], there)
                    dve.wait_ge(drained[sg], gate_free + 1)
                    tt(ACTS[:, bass.ds(i * 2 + j, 1)], cv[:, 2 * j:2 * j + 1], bank[s][:, 0:1]).then_inc(drained[s], 1)

            with dve.Fori(0, 21) as i:
                units.enter(i)
                ahead.enter(i, drained=0, split=1)
                gate_pairs(i, [UNIT] * RING)
            units.leave(21)
            ahead.leave(21)
            gate_pairs(21, [UNIT] * 2 + [DOWN * P] * 2)
            down(0)

        @block.gpsimd
        def _(pool):
            splits, merged, acts = [0], Count(merged_rounded), Count(acts_rounded)

            def lower(low, whole, high):
                return nc.gpsimd.tensor_tensor(low, whole, high.bitcast(F32), ALU.subtract)

            def lower_input(high, low):
                for g in range(2):
                    c = slice(4 * g, 4 * g + 4)
                    pool.wait_ge(h_rounded, 4 * splits[0] + g + 1)
                    lower(low[:, c], hT[:, c], high[:, c]).then_inc(h_lowered_pool, 1)
                splits[0] += 1

            def lower_merged(high):
                with pool.Fori(0, KT) as i:
                    merged.enter(i, 1)
                    merged.add()
                    pool.wait_ge(merged_rounded, merged.value())
                    c = bass.ds(i, 1)
                    lower(h_low[:, c], hT[:, c], high[:, c]).then_inc(merged_lowered, 1)
                merged.leave(KT)

            def lower_acts():
                with pool.Fori(0, SPLIT_UP) as i:
                    acts.enter(i, 1)
                    acts.add()
                    pool.wait_ge(acts_rounded, acts.value())
                    c = bass.ds(i, 1)
                    lower(acts_low[:, c], ACTS[:, c], acts_high[:, c]).then_inc(acts_lowered, 1)
                acts.leave(SPLIT_UP)
                acts.add()
                pool.wait_ge(acts_rounded, acts.value())
                lower(acts_low[:, SPLIT_UP:], ACTS[:, SPLIT_UP:], acts_high[:, SPLIT_UP:]).then_inc(acts_lowered, 1)

            lower_input(mix_high, mix_low)
            lower_merged(out_high)
            lower_input(up_high, h_low)
            lower_acts()
            lower_input(in2_high, in2_low)
            lower_merged(out2_high)
            lower_input(up_high, h_low)
            lower_acts()


_OUT = (P, KT, T)


def kernel(**inputs):
    import concourse.bacc as _bacc
    from concourse.bass_utils import run_bass_kernel_spmd as _run

    arrays = host_layout({k: np.asarray(a) for k, a in inputs.items()})
    nc = _bacc.Bacc("TRN2", target_bir_lowering=False, num_devices=1)
    t = {k: nc.dram_tensor("in_" + k, a.shape, mybir.dt.from_np(a.dtype), kind="ExternalInput").ap()
         for k, a in arrays.items()}
    out = nc.dram_tensor("out", _OUT, F32, kind="ExternalOutput").ap()
    build(nc, t, out)
    r = _run(nc, [{"in_" + k: a for k, a in arrays.items()}], core_ids=[0])
    y = np.asarray(r.results[0]["out"])
    return np.ascontiguousarray(y.transpose(2, 1, 0)).reshape(1, T, D)


def unit_tiles(w, group=1):
    K, N = w.shape
    a = w.reshape(K // P, P, N // P, P).transpose(2, 1, 0, 3).reshape(N // P // group, group, P, K)
    return np.ascontiguousarray(a.transpose(0, 2, 1, 3)).reshape(N // P // group, P, group * K)


def down_tiles(w):
    a = w.reshape(4, DOWN, P, KT, P).transpose(3, 0, 2, 1, 4)
    return np.ascontiguousarray(a).reshape(4 * KT, P, DOWN * P)


def columns(x):
    return x.reshape(-1, P).T


def host_layout(g):
    a = {}
    w = g["w_in"][0]
    at = np.cumsum([0, 512, 768, 768, 768, 768, 768, 768, 768, 4, 4])
    cut = [w[:, at[n]:at[n + 1]] for n in range(10)]
    a["w_mix"] = unit_tiles(np.concatenate([cut[n] for n in (0, 5, 3, 6, 2, 7, 1, 4)], axis=1))
    a["w_gates"] = unit_tiles(w[:, at[10]:])
    a["w_if"] = np.ascontiguousarray(w[:, at[8]:at[10]].reshape(KT, P, 8).transpose(1, 0, 2))
    qk = np.zeros((2, P, ML, 2, ML_DH), np.float32)
    for h in range(ML):
        for n, (_, lo, hi, e) in enumerate(PIECES[h]):
            for part in range(2):
                qk[part, lo:hi, h, n] = g["ml_w_qk"][0][h, e:e + hi - lo, part * ML_DH:(part + 1) * ML_DH]
    a["w_qk"] = qk.reshape(2, P, 8 * ML_DH)
    s5b = np.zeros((2, P, S5_STATES, P), np.float32)
    s5c = np.zeros((2, P, S5_STATES, P), np.float32)
    for part in range(2):
        b = g[("s5_b_re", "s5_b_im")[part]][0]
        c = g[("s5_c_re", "s5_c_im")[part]][0]
        for q in range(32):
            f, n, s = 16 * (q % 8), q // 2, 64 * (q % 2)
            s5b[part, f:f + 16, n, s:s + 64] = b[q].T
            s5c[part, s:s + 64, n, f:f + 16] = c[q].T
    a["s5_b"], a["s5_c"] = s5b.reshape(2, P, UNIT), s5c.reshape(2, P, UNIT)
    a["w_glu"] = unit_tiles(g["s5_w_glu"][0], 4)
    a["w_branch"] = unit_tiles(g["w_branch"][0])
    a["w_out"] = unit_tiles(g["w_out"][0])
    swap = np.stack([np.arange(FF_TILES), FF_TILES + np.arange(FF_TILES)], axis=1).ravel()
    a["w_up"] = unit_tiles(g["ffn_w_up"][0])[swap]
    a["w_down"] = down_tiles(g["ffn_w_down"][0])

    w = g["w_in_2"][0]
    x1, x2 = w[:, 1024:1056], w[:, 1056:1088]
    a["w_in2"] = unit_tiles(np.concatenate([w[:, 0:1024], x1, x1, x1, x1, x2, x2, x2, x2, w[:, 1088:]], axis=1))
    uq = g["w_uq_2"][0].reshape(512, HEADS, 192)
    a["w_uq"] = unit_tiles(np.concatenate([uq[:, :, 0:128].reshape(512, -1), uq[:, :, 128:160].reshape(512, -1),
                                           uq[:, :, 160:192].reshape(512, -1)], axis=1), 4)
    ukv = g["w_ukv_2"][0].reshape(512, HEADS, 256)
    vals = ukv[:, :, 128:].reshape(4, P, 2, 512).transpose(2, 1, 0, 3).reshape(2, P, UNIT)
    a["w_ukv"] = np.concatenate([unit_tiles(ukv[:, :, 0:128].reshape(512, -1), 4), vals], axis=0)
    a["w_mix2"] = unit_tiles(np.concatenate([g["w_o_mla_2"][0], g["w_o_dil_2"][0]], axis=0))
    a["w_o2"] = unit_tiles(g["w_o_2"][0])
    a["w_up2"] = unit_tiles(g["w_gate_up_2"][0])[swap]
    a["w_down2"] = down_tiles(g["w_down_2"][0])

    vec = np.zeros((P, VCOLS), np.float32)

    def put(name, cols, rows=P):
        vec[0:rows, VAT[name]:VAT[name] + cols.shape[1]] = cols

    put("mix_norm", columns(g["mix_norm"][0]))
    put("final_norm", columns(g["final_norm"]))
    put("ffn_norm", columns(g["ffn_norm"][0]))
    put("g_mix", columns(g["g_mix_2"][0]))
    put("g_ffn", columns(g["g_ffn_2"][0]))
    put("b_gate", columns(g["b_gate_2"][0]))
    taps = np.concatenate([g["ffn_conv_w"][0], g["ffn_conv_b"]], axis=0).reshape(4, 2 * FF_TILES, P)
    put("ffn_conv", taps[:, swap].transpose(2, 1, 0).reshape(P, -1))
    taps = np.concatenate([g["ml_conv_w"][0], g["ml_conv_b"]], axis=0).reshape(5, ML_TILES, P)
    put("ml_conv", taps.transpose(2, 1, 0).reshape(P, -1))
    put("s5_d", columns(g["s5_d"][0]))
    put("b_glu", columns(g["s5_b_glu"][0]))
    put("hg_lb", columns(g["hg_lower_bounds"][0]))
    put("hg_norm", columns(g["hg_norm"][0]))
    put("ml_norm", columns(g["ml_norm"][0]))
    put("g_cq", columns(g["g_cq_2"][0]))
    put("g_ckv", columns(g["g_ckv_2"][0]))
    for name in ("g_q_nope", "g_k_nope", "g_q_dil", "g_k_dil"):
        put(name, g[name + "_2"][0].reshape(P, 1))
    for name in ("g_q_rope", "g_k_rope"):
        put(name, np.tile(g[name + "_2"][0].reshape(2, 32).T, (4, 1)))
    put("lam_re", columns(g["s5_lam_re"][0].reshape(-1)))
    put("lam_im", columns(g["s5_lam_im"][0].reshape(-1)))
    put("log_dt", columns(np.repeat(g["s5_log_dt"][0], 64)))
    put("b_ig", g["ml_b_ig"][0].reshape(ML, 1), ML)
    put("b_fg", g["ml_b_fg"][0].reshape(ML, 1), ML)
    a["vec"] = vec
    a["xT"] = np.ascontiguousarray(g["x"][0].T.reshape(KT, P, T).transpose(1, 0, 2))

    i = np.arange(P)
    cst = np.zeros((P, 5, P), np.float32)
    cst[:, 0] = i[:, None] // 32 == i[None] // 32
    cst[:, 1] = np.eye(P)
    cst[:, 2] = i[:, None] <= i[None]
    cst[:, 3] = i[:, None] < 64
    cst[:, 4] = i[:, None] >= 64
    a["cst"] = cst
    a["sel"] = np.ascontiguousarray(np.repeat(np.eye(ML, dtype=np.float32)[:, :, None], P, axis=2))
    hm = np.zeros((P, 8, P), np.int32)
    hm[:, 0] = np.eye(P)
    for lvl in range(1, 8):
        B = 1 << (lvl - 1)
        s, q = i[:, None], i[None]
        hm[:, lvl] = (s // (2 * B) == q // (2 * B)) & (s // B % 2 == 0) & (q // B % 2 == 1)
    a["hmask"] = hm
    d = np.abs(np.arange(T)[:, None] - np.arange(T)[None])
    cover = sum(((d % dil == 0) & (d // dil <= win // (2 * dil))).astype(np.float32)
                for win, dil in ((128, 1), (512, 4), (2048, 16)))
    away = np.where(cover > 0, -d, MASKED).astype(np.float32)
    inv = np.float32(10000.0) ** (-np.arange(0, 64, 2, dtype=np.float32) / np.float32(64))
    ang = np.arange(T, dtype=np.float32)[None] * inv[:, None]
    band = np.zeros((P, 6, T), np.float32)
    band[:, 0:2] = away.reshape(2, P, T).transpose(1, 0, 2)
    band[:, 2:4] = cover.reshape(2, P, T).transpose(1, 0, 2)
    band[:, 4] = np.tile(np.cos(ang), (4, 1))
    band[:, 5] = np.tile(np.sin(ang), (4, 1))
    a["band"] = band
    return a
```

```python
from contextlib import ExitStack

import numpy as np
import concourse.bass as bass
from concourse import mybir

F32 = mybir.dt.float32
R32 = mybir.dt.float32r
I32 = mybir.dt.int32
ALU = mybir.AluOpType
ACT = mybir.ActivationFunctionType
AX = mybir.AxisListType

P = 128
T = 256
TB = T // P
D = 2048
KT = D // P
EPS = 1e-6
RING = 4
UNIT = KT * P
POOL_TURN = 2
AHEAD = 2

S5_TILES = 4
S5_STATES = 16
S5_STEPS = 8
S5_SIDE = 16
HG = 6
ML = 4
ML_DH = 192
ML_TILES = 6
FF = 5632
FF_TILES = FF // P
DOWN = FF_TILES // 4
H_GROUPS = [(0, 2), (2, 4), (4, 8), (8, 12), (12, 16)]
H_POOL = 3
SPLIT_UP = 34
HEADS = 8
SLOPES = [2.0 ** -(h + 1) for h in range(HEADS)]
MASKED = -1e30
TWO_PI = 2 * np.pi
PI_HI, PI_MID = 6.28125, 0.0019350051879882812
PI_LO = TWO_PI - PI_HI - PI_MID
ROUND = 1.5 * 2 ** 23
PI_IN = 3.1415925

VEC = [("mix_norm", 16), ("final_norm", 16), ("ffn_norm", 16), ("g_mix", 16), ("g_ffn", 16),
       ("b_gate", 32), ("ffn_conv", 4 * 88), ("ml_conv", 5 * 6), ("s5_d", 4), ("b_glu", 4), ("hg_lb", 6),
       ("hg_norm", 6), ("ml_norm", 6), ("g_cq", 4), ("g_ckv", 4), ("g_q_nope", 1), ("g_k_nope", 1),
       ("g_q_rope", 2), ("g_k_rope", 2), ("g_q_dil", 1), ("g_k_dil", 1), ("lam_re", 16), ("lam_im", 16),
       ("log_dt", 16), ("b_ig", 1), ("b_fg", 1)]
VAT, _n = {}, 0
for _name, _w in VEC:
    VAT[_name] = _n
    _n += _w
VCOLS = _n

U0, CX0, F0, O0, Q0, OG0 = 0, 4, 10, 16, 22, 28
M_TILES = 34

PIECES = []
for _h in range(ML):
    _j = 3 * (_h // 2)
    PIECES.append([(_j, 0, 128, 0), (_j + 1, 0, 64, 128)] if _h % 2 == 0
                  else [(_j + 1, 64, 128, 0), (_j + 2, 0, 128, 64)])


def gates_beside(h):
    return 1 if h < 12 else 2


class Count:

    def __init__(self, sem):
        self.sem, self.base, self.i, self.per, self.k = sem, 0, None, 0, 0

    def add(self, n=1):
        self.k += n

    def value(self):
        if self.i is None or self.per == 0:
            return self.base + self.k
        return self.i * self.per + (self.base + self.k)

    def enter(self, i, per):
        self.base, self.k, self.i, self.per = self.base + self.k, 0, i, per

    def leave(self, rounds):
        assert self.k == self.per, (self.k, self.per)
        self.base, self.k, self.i, self.per = self.base + self.per * rounds, 0, None, 0


class Units:

    def __init__(self, landed, rounded, lowered, consumed, drained):
        self.pos = 0
        self.landed, self.rounded, self.lowered, self.consumed, self.drained = (
            [Count(s) for s in sems] for sems in (landed, rounded, lowered, consumed, drained))

    def next(self, drained=True, split=False):
        s = self.pos % RING
        self.pos += 1
        self.landed[s].add(16)
        before, free = self.consumed[s].value(), self.drained[s].value()
        self.consumed[s].add()
        if split:
            self.rounded[s].add()
            self.lowered[s].add()
        if drained:
            self.drained[s].add()
        return s, self.landed[s].value(), before, self.consumed[s].value(), free

    def enter(self, i, turns=1, drained=1, split=0):
        self.turns = turns
        for counts, per in ((self.landed, 16), (self.rounded, split), (self.lowered, split),
                            (self.consumed, 1), (self.drained, drained)):
            for c in counts:
                c.enter(i, per * turns)

    def leave(self, n):
        self.pos += (n - 1) * self.turns * RING
        for c in self.landed + self.rounded + self.lowered + self.consumed + self.drained:
            c.leave(n)

    def skip(self, n, drained=True, split=False):
        for _ in range(n):
            self.next(drained, split)

    def token_flags(self, odd):
        return [(q < 2) == odd for q in range(RING)]

    def token_banks(self, odd):
        return [(self.pos + q) % RING for q, kept in enumerate(self.token_flags(odd)) if kept]

    def skip_tokens(self, groups):
        for g in range(groups):
            for kept in self.token_flags(g % 2 == 1):
                self.next(kept, True)

    def all_drained(self):
        return [(c.sem, c.value()) for c in self.drained]


def build(nc, t, out):
    with ExitStack() as ctx:
        def sb(name, shape, dt=F32):
            return ctx.enter_context(nc.sbuf_tensor(name, shape, dt))

        def alias(name, base, shape, at=0):
            return nc.alloc_sbuf_tensor_at(name, shape, R32, offset=base + at * T * 4)

        ring = sb("ring", [P, RING, UNIT])
        ring_base = nc.sbuf_base - RING * UNIT * 4
        xT = sb("xT", [P, KT, T])
        hT = sb("hT", [P, KT, T])
        hT_base = nc.sbuf_base - KT * T * 4
        vec = sb("vec", [P, VCOLS])
        cst = sb("cst", [P, 3, P])
        pick = sb("pick", [P, 3, 2 * HEADS - 1])
        w_if = sb("w_if", [P, KT, 8])
        ones = sb("ones", [P, P])
        acol = sb("acol", [P, TB, ML])
        lb = sb("lb", [P, 4, HG])
        s5c = sb("s5c", [P, 16, S5_STATES])
        s5p = sb("s5p", [P, S5_STEPS, 2, S5_STATES])
        small = sb("small", [P, 2, 8])
        xms = sb("xms", [P, T])
        xrs = sb("xrs", [P, T])
        xtmp = sb("xtmp", [P, T])
        ARENA = nc.sbuf_bytes_remaining // 4 // 16 * 16
        arena = sb("arena", [P, ARENA])
        arena_base = nc.sbuf_base - ARENA * 4

        def tiles(at, n):
            assert at + n * T <= ARENA, (at + n * T, ARENA)
            return arena[:, at:at + n * T].rearrange("p (k t) -> p k t", t=T)

        w_low = alias("w_low", ring_base, [P, RING, UNIT])
        w_high = alias("w_high", arena_base, [P, RING, UNIT], 94)
        h_low = alias("h_low", hT_base, [P, KT, T])
        mix_high, mix_low = (alias(f"mix_{n}", arena_base, [P, KT, T], a) for n, a in (("high", 46), ("low", 62)))
        in2_high, in2_low = (alias(f"in2_{n}", arena_base, [P, KT, T], a) for n, a in (("high", 34), ("low", 50)))
        out_high = alias("out_high", arena_base, [P, KT, T], 28)
        out2_high = alias("out2_high", arena_base, [P, KT, T], 18)
        up_high = alias("up_high", arena_base, [P, KT, T], 78)
        acts_low = alias("acts_low", arena_base, [P, FF_TILES, T], 0)
        acts_high = alias("acts_high", arena_base, [P, FF_TILES, T], 44)

        MT = tiles(0, M_TILES)
        VN = arena[:, 34 * T:46 * T].rearrange("p (b h c) -> p b h c", b=TB, c=P)
        G = tiles(46 * T, 48)
        W = 94 * T
        CA, QH, KH = tiles(78 * T, 6), tiles(W + 6 * T, 6), tiles(W + 12 * T, 6)
        rows = arena[0:ML, W + 18 * T:W + 24 * T].rearrange("p (k t) -> p k t", t=T)
        MB, TH = tiles(W + 24 * T, 4), tiles(W + 28 * T, 4)
        PM = arena[:, 78 * T:84 * T].rearrange("p (h c) -> p h c", h=ML)
        HH, MSQ = CA, QH
        HK, HPR, HX1 = tiles(W, 6), tiles(W + 6 * T, 6), tiles(W + 12 * T, 6)
        HX0, HF, HQ = MT[:, CX0:CX0 + 6], MT[:, F0:F0 + 6], MT[:, Q0:Q0 + 6]
        PD = tiles(W + 18 * T, 6)
        PO = arena[:, W + 24 * T:W + 27 * T].rearrange("p (h c) -> p h c", h=HG)
        hmask = arena[:, W + 32 * T:W + 36 * T].bitcast(I32).rearrange("p (l c) -> p l c", l=8)
        HO, HSQ = HX1, HX0
        SR = tiles(W, S5_STATES)
        SI = tiles(OG0 * T, S5_STATES)
        turn_c, turn_s = tiles(W + 16 * T, 4), tiles(W + 20 * T, 4)
        tmp_r, tmp_i = tiles(W + 24 * T, 4), tiles(W + 28 * T, 4)
        GA = tiles(W + 32 * T, 4)
        powers = arena[:, 90 * T:94 * T].rearrange("p (j n a) -> p j n a", j=4, a=S5_SIDE)
        ACTS = tiles(0, FF_TILES)
        cv = tiles(126 * T, 4)
        P2 = tiles(0, 26)
        VD = arena[:, 26 * T:34 * T].rearrange("p (b h c) -> p b h c", b=TB, c=P)
        G2 = tiles(34 * T, 32)
        QN, QR, KN = tiles(66 * T, 8), tiles(74 * T, 4), tiles(78 * T, 8)
        VM = arena[:, 86 * T:94 * T].rearrange("p (b h c) -> p b h c", b=TB, c=P)
        LSQ, LMS, LRS = tiles(78 * T, 4), tiles(82 * T, 1), tiles(83 * T, 1)
        SQ, MS, RS = tiles(94 * T, 8), tiles(102 * T, 8), tiles(110 * T, 8)
        band = tiles(118 * T, 6)
        CQ, CKV, KR = P2[:, 0:4], P2[:, 4:8], P2[:, 8:10]
        QD, KD = P2[:, 10:18], P2[:, 18:26]
        OA = P2[:, 0:8]
        ES = [SQ[:, 0:2], SQ[:, 2:4]]
        PS = [SQ[:, 4:6], SQ[:, 6:8]]
        BS = [MS[:, 0:2], MS[:, 2:4]]

        bank = [ctx.enter_context(nc.psum_tensor(f"bank{i}", [P, 2, T], F32)) for i in range(8)]
        bank_row = [b[:].rearrange("p a t -> p (a t)") for b in bank]

        def sem(name):
            return ctx.enter_context(nc.semaphore(name))

        landed = [sem(f"unit_landed{s}") for s in range(RING)]
        rounded = [sem(f"unit_rounded{s}") for s in range(RING)]
        lowered = [sem(f"unit_lowered{s}") for s in range(RING)]
        consumed = [sem(f"unit_consumed{s}") for s in range(RING)]
        drained = [sem(f"bank_drained{s}") for s in range(RING)]
        x_landed = [sem(f"x_landed{g}") for g in range(4)]
        vec_landed, cst_landed = sem("vec_landed"), sem("cst_landed")
        hmask_landed, band_landed, x_stored = sem("hmask_landed"), sem("band_landed"), sem("x_stored")
        ones_set = sem("ones_set")
        dve_chain, act_chain = sem("dve_chain"), sem("act_chain")
        norm_squared, norm_summed = sem("norm_squared"), sem("norm_summed")
        norm_mean, norm_rooted, norm_done = sem("norm_mean"), sem("norm_rooted"), sem("norm_done")
        x_squared, x_paired, x_scaled = sem("x_squared"), sem("x_squares_paired"), sem("x_scaled")
        norm_rows, norm_spread = sem("norm_rows_ready"), sem("norm_rows_spread")
        conv_ready, conv_act, qk_ready = sem("ml_conv_ready"), sem("ml_conv_act"), sem("ml_qk_ready")
        if_summed, rows_abs, rows_log, rows_ready, rows_thr = (sem("ml_if_summed"), sem("ml_rows_abs"),
                                                               sem("ml_rows_log"), sem("ml_rows_ready"),
                                                               sem("ml_rows_threshold"))
        cast_done, cast_taken = sem("ml_broadcast_done"), sem("ml_broadcast_taken")
        ml_scored, ml_arg, ml_exp, ml_p = sem("ml_scored"), sem("ml_arg"), sem("ml_exp"), sem("ml_p")
        ml_den_taken = sem("ml_den_taken")
        ml_den, ml_rden, ml_num, ml_h = sem("ml_den"), sem("ml_rden"), sem("ml_num"), sem("ml_h")
        ml_done = sem("ml_done")
        hg_x, hg_scored, hg_taken, hg_out, hg_kept = (sem("hg_x"), sem("hg_scored"), sem("hg_taken"),
                                                      sem("hg_out"), sem("hg_kept"))
        hg_done = sem("hg_done")
        lb_arg, lb_exp = sem("hg_bound_arg"), sem("hg_bound_exp")
        s5_arg, s5_fn = sem("s5_arg"), sem("s5_function")
        s5_fed, s5_in, s5_states = sem("s5_fed"), sem("s5_input_kept"), sem("s5_states")
        s5_scaled, s5_tabled = sem("s5_input_scaled"), sem("s5_turns_made")
        s5_pre, s5_gelu = sem("s5_pre"), sem("s5_gelu")
        s5_gate, s5_done = sem("s5_gate"), sem("s5_done")
        silu_pair, ff_done = sem("silu_pair"), sem("ff_act_done")
        h_scaled, h_rounded = sem("h_scaled"), sem("h_rounded")
        h_lowered_pool, h_lowered_vector = sem("h_lowered_by_pool"), sem("h_lowered_by_vector")
        merged_rounded, merged_lowered = sem("merged_rounded"), sem("merged_lowered")
        acts_rounded, acts_lowered = sem("acts_rounded"), sem("acts_lowered")
        down_drained = [sem(f"down_drained{b}") for b in range(2)]
        at_scored, at_max, at_exp, at_p = sem("at_scored"), sem("at_max"), sem("at_exp"), sem("at_p")
        at_turned, at_pt, at_out, at_kept = sem("at_turned"), sem("at_pt"), sem("at_out"), sem("at_kept")
        at_bias, at_sum = sem("at_bias"), sem("at_biased")

        block = ctx.enter_context(nc.Block())

        def v(name, n=0, rows_=P):
            c = VAT[name] + n
            return vec[0:rows_, c:c + 1]

        def x_tiles():
            return [[(ones[:], hT[:, 4 * g + k]) for g in range(4) for k in range(2)]]

        def all_tiles(sq, n):
            return [[(ones[:], sq[:, k]) for k in range(n)]]

        def picked(h, part=0):
            return pick[:, part, HEADS - 1 - h:2 * HEADS - 1 - h]

        def each_tile(sq, n):
            return [[(picked(k), sq[:, k])] for k in range(n)]

        blk32, ident, causal = cst[:, 0], cst[:, 1], cst[:, 2]

        def spread(h, n):
            return ident[0:n, h:h + 1].broadcast_to([n, P])

        NORMS = [
            dict(src=xT, sq=hT, ms=xms, rs=xrs, groups=x_tiles(), n=D),
            dict(src=HH, sq=MSQ, rows=ML, n=ML_DH, groups=[
                [(picked(h, 1 + a // 64 if b - a < P else 0), MSQ[:, k]) for k, a, b, _ in PIECES[h]]
                for h in range(ML)]),
            dict(src=HO, sq=HSQ, rows=HG, groups=each_tile(HSQ, HG), n=P),
            dict(src=xT, sq=hT, ms=xms, rs=xrs, groups=x_tiles(), n=D),
            dict(src=xT, sq=hT, ms=xms, rs=xrs, groups=x_tiles(), n=D),
            dict(src=xT, sq=hT, ms=xms, rs=xrs, groups=x_tiles(), n=D),
            dict(src=CQ, sq=LSQ, ms=LMS, rs=LRS, groups=all_tiles(LSQ, 4), n=512),
            dict(src=CKV, sq=LSQ, ms=LMS, rs=LRS, groups=all_tiles(LSQ, 4), n=512),
            dict(src=KR, sq=SQ[:, 0:2], ms=MS[:, 0:1], rs=RS[:, 0:1], n=64,
                 groups=[[(blk32, SQ[:, 0]), (blk32, SQ[:, 1])]]),
            dict(src=QD, sq=SQ, rows=HEADS, groups=each_tile(SQ, HEADS), n=P),
            dict(src=KD, sq=SQ, rows=HEADS, groups=each_tile(SQ, HEADS), n=P),
            dict(src=QN, sq=SQ, rows=HEADS, groups=each_tile(SQ, HEADS), n=P),
            dict(src=QR, sq=SQ[:, 0:4], ms=MS[:, 0:2], rs=RS[:, 0:2], n=64,
                 groups=[[(blk32, SQ[:, g]), (blk32, SQ[:, 2 + g])] for g in range(2)]),
            dict(src=KN, sq=SQ, rows=HEADS, groups=each_tile(SQ, HEADS), n=P),
            dict(src=xT, sq=hT, ms=xms, rs=xrs, groups=x_tiles(), n=D),
        ]

        @block.sync
        def _(sp):
            units = Units(landed, rounded, lowered, consumed, drained)
            for g in range(4):
                sp.dma_start(xT[:, 4 * g:4 * g + 4], t["xT"][:, 4 * g:4 * g + 4]).then_inc(x_landed[g], 16)
            sp.dma_start(vec[:], t["vec"]).then_inc(vec_landed, 16)

            def load(src, cols=UNIT):
                s, _, before, _, _ = units.next(False)
                if not isinstance(before, int) or before > 0:
                    sp.wait_ge(consumed[s], before)
                sp.dma_start(ring[:, s, 0:cols], src).then_inc(landed[s], 16)

            def stream(src, rounds, cols=UNIT):
                with sp.Fori(0, rounds) as i:
                    units.enter(i, drained=0)
                    for j in range(RING):
                        load(src[i * RING + j], cols)
                units.leave(rounds)

            w = t["w_mix"]
            for j in range(RING):
                load(w[j])
            sp.dma_start(cst[:], t["cst"]).then_inc(cst_landed, 16)
            sp.dma_start(pick[:], t["pick"]).then_inc(cst_landed, 16)
            sp.dma_start(w_if[:], t["w_if"]).then_inc(cst_landed, 16)
            sp.dma_start(hmask, t["hmask"]).then_inc(hmask_landed, 16)
            for j in range(RING, 10):
                load(w[j])
            stream(w[10:46], 9)
            for part in range(2):
                load(t["w_qk"][part], 8 * ML_DH)
            stream(t["w_gates"][0:24], 6)
            for part in range(2):
                load(t["s5_b"][part])
            stream(t["w_gates"][24:48], 6)
            for part in range(2):
                load(t["s5_c"][part])
            load(t["w_glu"][0])
            stream(t["w_branch"], 4)
            stream(t["w_out"], 4)
            stream(t["w_up"], 22)
            stream(t["w_down"], 16, DOWN * P)
            stream(t["w_in2"][0:24], 6)
            for j in (24, 25):
                load(t["w_in2"][j])
            stream(t["w_in2"][26:34], 2)
            for j in range(3):
                load(t["w_uq"][j])
            for j in range(4):
                load(t["w_ukv"][j])
            sp.dma_start(band, t["band"]).then_inc(band_landed, 16)
            stream(t["w_in2"][34:66], 8)
            stream(t["w_mix2"], 4)
            stream(t["w_o2"], 4)
            stream(t["w_up2"], 22)
            stream(t["w_down2"], 16, DOWN * P)
            for b in range(2):
                sp.wait_ge(down_drained[b], 1 + 2 * KT // 2)
            sp.dma_start(out, xT[:]).then_inc(x_stored, 16)
            sp.wait_ge(x_stored, 16)

        @block.tensor
        def _(pe):
            units = Units(landed, rounded, lowered, consumed, drained)
            down_free = [Count(s) for s in down_drained]
            for c in down_free:
                c.base = 1
            norm = [0]

            def mm(o, lhsT, rhs, first=True, last=True):
                return nc.tensor.matmul(o, lhsT, rhs, start=first, stop=last)

            def take():
                s, there, _, _, _ = units.next(False)
                pe.wait_ge(landed[s], there)
                return s

            def unit(body):
                s, there, _, _, free = units.next()
                pe.wait_ge(landed[s], there)
                if not isinstance(free, int) or free > 0:
                    pe.wait_ge(drained[s], free)
                body(s).then_inc(consumed[s], 1)

            def unit_split(body):
                s, _, _, _, free = units.next(split=True)
                pe.wait_ge(lowered[s], units.lowered[s].value())
                if not isinstance(free, int) or free > 0:
                    pe.wait_ge(drained[s], free)
                body(s).then_inc(consumed[s], 1)

            def rounds(n, body):
                with pe.Fori(0, n) as i:
                    units.enter(i)
                    for j in range(RING):
                        unit(body)
                units.leave(n)

            def rounds_split(n, body):
                with pe.Fori(0, n) as i:
                    units.enter(i, split=1)
                    for j in range(RING):
                        unit_split(body)
                units.leave(n)

            def mm3(o, s, c, high, low, first, last):
                c = slice(c * P, (c + 1) * P)
                mm(o, w_high[:, s, c], high, first, False)
                mm(o, w_high[:, s, c], low, False, False)
                return mm(o, w_low[:, s, c], high, False, last)

            def project_split(high, low, waits=None):
                def body(s):
                    for k in range(KT):
                        if waits:
                            waits(k)
                        last = mm3(bank[s][:, 0], s, k, high[:, k], low[:, k], k == 0, k == KT - 1)
                    return last
                return body

            splits = [0]

            def after_norm(high, low):
                n = splits[0]
                splits[0] += 1

                def waits(k):
                    for g, (first, _) in enumerate(H_GROUPS):
                        if k == first and g < H_POOL:
                            pe.wait_ge(h_lowered_pool, H_POOL * n + g + 1)
                        elif k == first:
                            pe.wait_ge(h_lowered_vector, (len(H_GROUPS) - H_POOL) * n + g - H_POOL + 1)
                unit_split(project_split(high, low, waits))

            def project(s):
                for k in range(KT):
                    last = mm(bank[s][:, 0], ring[:, s, k * P:(k + 1) * P], hT[:, k], k == 0, k == KT - 1)
                return last

            def tokens(odd, high, low):
                banks = units.token_banks(odd)
                for s in banks:
                    pe.wait_ge(drained[s], units.drained[s].value())
                for q, kept in enumerate(units.token_flags(odd)):
                    s, _, _, _, _ = units.next(kept, True)
                    pe.wait_ge(lowered[s], units.lowered[s].value())
                    for b in range(TB):
                        o, tok = bank_row[banks[b]], slice(b * P, (b + 1) * P)
                        for j in range(4):
                            k, c = 4 * q + j, slice(512 * j, 512 * (j + 1))
                            mm(o, high[:, k, tok], w_high[:, s, c], k == 0, False)
                            mm(o, high[:, k, tok], w_low[:, s, c], False, False)
                            last = mm(o, low[:, k, tok], w_high[:, s, c], False, k == KT - 1)
                    last.then_inc(consumed[s], 1)

            def drained_all():
                for s, n in units.all_drained():
                    pe.wait_ge(s, n)

            x_sums = [0]

            def sum_squares():
                n = NORMS[norm[0]]
                norm[0] += 1
                if n["src"] is xT:
                    x_sums[0] += 4
                    for k, (one, sq) in enumerate(n["groups"][0]):
                        if k % 2 == 0:
                            pe.wait_ge(x_paired, x_sums[0] - 3 + k // 2)
                        last = mm(bank[4][:, 0], one, sq, k == 0, k == 7)
                    last.then_inc(norm_summed, 1)
                    return
                pe.wait_ge(norm_squared, norm[0] - x_sums[0] // 4)
                if "rows" in n:
                    parts = [x for parts in n["groups"] for x in parts]
                    for k, (one, sq) in enumerate(parts):
                        last = mm(bank[4][0:HEADS, 0], one, sq, k == 0, k == len(parts) - 1)
                    last.then_inc(norm_summed, 1)
                    return
                for g, parts in enumerate(n["groups"]):
                    for k, (one, sq) in enumerate(parts):
                        last = mm(bank[4 + g // 2][:, g % 2], one, sq, k == 0, k == len(parts) - 1)
                last.then_inc(norm_summed, 1)

            casts = [0]

            def spread_rows():
                rows_ = NORMS[norm[0] - 1]["rows"]
                casts[0] += 1
                pe.wait_ge(norm_rows, casts[0])
                for h in range(rows_):
                    last = mm(bank[4 + h // 2][:, h % 2], spread(h, rows_), xrs[0:rows_])
                last.then_inc(norm_spread, 1)

            def rows_back():
                pe.wait_ge(norm_done, norm[0])

            def banks_back():
                pe.wait_ge(norm_mean, norm[0])

            def down(acts_before):
                pe.wait_ge(acts_lowered, acts_before + SPLIT_UP)
                with pe.Fori(0, 8) as i:
                    units.enter(i, turns=2, drained=0, split=1)
                    for c in down_free:
                        c.enter(i, 1)
                    for b in range(2):
                        pe.wait_ge(down_drained[b], down_free[b].value())
                        down_free[b].add()
                        for q in range(4):
                            s, _, _, _, _ = units.next(False, split=True)
                            pe.wait_ge(lowered[s], units.lowered[s].value())
                            for k in range(DOWN):
                                n = q * DOWN + k
                                if n == SPLIT_UP:
                                    pe.wait_ge(acts_lowered, acts_before + SPLIT_UP + 1)
                                last = mm3(bank[4 + b][:, 0], s, k, acts_high[:, n], acts_low[:, n],
                                           n == 0, n == FF_TILES - 1)
                            last.then_inc(consumed[s], 1)
                units.leave(8)
                for c in down_free:
                    c.leave(8)

            pe.wait_ge(ones_set, 1)
            sum_squares()
            after_norm(mix_high, mix_low)
            for j in range(9):
                unit_split(project_split(mix_high, mix_low))
            for g in range(3):
                tokens(g % 2 == 1, mix_high, mix_low)
            rounds_split(6, project_split(mix_high, mix_low))

            pe.wait_ge(cst_landed, 48)
            for g in range(2):
                for k in range(KT):
                    last = mm(bank[7][0:ML, g], w_if[:, k, g * ML:(g + 1) * ML], hT[:, k], k == 0, k == KT - 1)
            last.then_inc(if_summed, 1)

            pe.wait_ge(conv_act, 1)
            for part in range(2):
                s = take()
                if part:
                    pe.wait_ge(qk_ready, 1)
                for h in range(ML):
                    for o, q0, q1, e in PIECES[h]:
                        for n, (k, _, _, _) in enumerate(PIECES[h]):
                            c = (2 * h + n) * ML_DH + e
                            last = mm(bank[4 + o // 2][q0:q1, o % 2], ring[:, s, c:c + q1 - q0], CA[:, k],
                                      n == 0, n == 1)
                last.then_inc(consumed[s], 1)
            rounds(1, project)

            pe.wait_ge(rows_ready, 1)
            pe.wait_ge(qk_ready, 2)
            for b in range(TB):
                mm(bank[4][:, 0, b * ML:(b + 1) * ML], rows[:, 2, b * P:(b + 1) * P], ident[0:ML, 0:ML])
            for h in range(ML):
                last = mm(bank[5 + h // 2][:, h % 2], spread(h, ML), rows[:, 3])
            last.then_inc(cast_done, 1)
            pe.wait_ge(rows_thr, 1)
            pe.wait_ge(cast_taken, 1)
            for h in range(ML):
                last = mm(bank[5 + h // 2][:, h % 2], spread(h, ML), rows[:, 5])
            last.then_inc(cast_done, 1)
            pe.wait_ge(cast_taken, 2)
            for h in range(ML):
                for b in range(TB):
                    for n, (k, p0, p1, _) in enumerate(PIECES[h]):
                        last = mm(bank[4 + h][:, b, b * P:T], KH[p0:p1, k, b * P:(b + 1) * P],
                                  QH[p0:p1, k, b * P:T], n == 0, n == 1)
                last.then_inc(ml_scored, 1)
            rounds(1, project)
            pe.wait_ge(ml_p, ML)
            for h in range(ML):
                mm(bank[4 + h // 2][:, h % 2], ones[:], PM[:, h, 0:T], True, False)
                last = mm(bank[4 + h // 2][:, h % 2, P:T], ones[:], PM[:, h, T:T + P], False, True)
            last.then_inc(ml_den, 1)
            pe.wait_ge(ml_den_taken, 1)
            vals = VN[:, :, 6:12].rearrange("p b h c -> p b (h c)")
            for h in range(ML):
                for k, p0, p1, e in PIECES[h]:
                    c = h * ML_DH + e
                    mm(bank[4 + k // 2][p0:p1, k % 2], vals[:, 0, c:c + p1 - p0], PM[:, h, 0:T], True, False)
                    last = mm(bank[4 + k // 2][p0:p1, k % 2, P:T], vals[:, 1, c:c + p1 - p0],
                              PM[:, h, T:T + P], False, True)
            last.then_inc(ml_num, 1)
            unit(project)
            unit(project)
            sum_squares()
            unit(project)
            spread_rows()
            unit(project)
            rows_back()

            for lvl in range(9):
                pe.wait_ge(hg_x, lvl + 1)
                if lvl:
                    pe.wait_ge(hg_taken, lvl)
                X = [HX0, HX1][lvl % 2]
                for h in range(HG):
                    if lvl == 8:
                        last = mm(bank_row[4 + h // 4][:, h % 4 * P:(h % 4 + 1) * P], X[:, h, 0:P], X[:, h, P:T])
                    else:
                        for b in range(TB):
                            c = slice(b * P, (b + 1) * P)
                            last = mm(bank[4 + h // 2][:, h % 2, c], (X if lvl else HK)[:, h, c],
                                      (X if lvl else HQ)[:, h, c])
                last.then_inc(hg_scored, 1)
                if lvl in (1, 4):
                    rounds(1, project)
            pe.wait_ge(hg_taken, 9)
            for h in range(HG):
                mm(bank[4 + h // 2][:, h % 2, 0:P], VN[:, 0, h], PD[:, h, 0:P])
                mm(bank[4 + h // 2][:, h % 2, P:T], VN[:, 0, h], PO[:, h], True, False)
                last = mm(bank[4 + h // 2][:, h % 2, P:T], VN[:, 1, h], PD[:, h, P:T], False, True)
            last.then_inc(hg_out, 1)
            unit(project)
            unit(project)
            sum_squares()
            unit(project)
            spread_rows()
            unit(project)
            rows_back()

            sre, sim_ = take(), take()
            pe.wait_ge(norm_done, 3)
            for n in range(S5_STATES):
                if n >= 4:
                    pe.wait_ge(s5_in, n - 3)
                c = slice(n * P, (n + 1) * P)
                last = mm(bank[4 + n % 4][:, 0], ring[:, sre, c], MT[:, U0 + n // 4])
                if n == S5_STATES - 1:
                    last.then_inc(consumed[sre], 1)
                last = mm(bank[4 + n % 4][:, 1], ring[:, sim_, c], MT[:, U0 + n // 4])
                last.then_inc(consumed[sim_] if n == S5_STATES - 1 else s5_fed, 1)
            rounds(6, project)

            cre, cim = take(), take()
            for f in range(S5_TILES):
                pe.wait_ge(s5_states, f + 1)
                for part, (slot, st) in enumerate(((cre, SR), (cim, SI))):
                    for n in range(4):
                        c = (4 * f + n) * P
                        last = mm(bank[4 + f][:, part], ring[:, slot, c:c + P], st[:, 4 * f + n], n == 0, n == 3)
                    if f == S5_TILES - 1:
                        last.then_inc(consumed[slot], 1)
            pe.wait_ge(s5_gelu, 1)
            s = take()
            for f in range(S5_TILES):
                for k in range(S5_TILES):
                    c = (f * S5_TILES + k) * P
                    last = mm(bank[4 + f // 2][:, f % 2], ring[:, s, c:c + P], GA[:, k], k == 0, k == 3)
            last.then_inc(consumed[s], 1)

            Y = [MT[:, U0 + k] for k in range(4)] + [HQ[:, k] for k in range(6)] + [MT[:, O0 + k] for k in range(6)]

            def branches(s):
                for o, lo, hi in ((bank[s][:, 0], 0, 4), (bank[s][:, 1], 4, 10), (bank[4 + s][:, 0], 10, 16)):
                    for k in range(lo, hi):
                        last = mm(o, ring[:, s, k * P:(k + 1) * P], Y[k], k == lo, k == hi - 1)
                return last

            pe.wait_ge(s5_done, 1)
            rounds(4, branches)
            drained_all()
            pe.wait_ge(merged_lowered, KT)
            rounds_split(4, project_split(out_high, h_low))
            sum_squares()
            after_norm(up_high, h_low)
            for j in range(3):
                unit_split(project_split(up_high, h_low))
            rounds_split(21, project_split(up_high, h_low))
            down(0)
            sum_squares()
            banks_back()
            sum_squares()
            after_norm(in2_high, in2_low)
            unit_split(project_split(in2_high, in2_low))
            rounds_split(6, project_split(in2_high, in2_low))
            tokens(False, in2_high, in2_low)
            sum_squares()
            tokens(True, in2_high, in2_low)
            banks_back()
            sum_squares()
            banks_back()

            def latent(src):
                def body(s):
                    for o in range(4):
                        for k in range(4):
                            c = (o * 4 + k) * P
                            last = mm(bank[s if o < 2 else 4 + s][:, o % 2], ring[:, s, c:c + P], src[:, k],
                                      k == 0, k == 3)
                    return last
                return body

            def latent_tokens(s):
                for b in range(TB):
                    for k in range(4):
                        last = mm(bank_row[s + 4 * b], CKV[:, k, b * P:(b + 1) * P],
                                  ring[:, s, k * 512:(k + 1) * 512], k == 0, k == 3)
                return last

            pe.wait_ge(norm_done, 7)
            for j in range(3):
                unit(latent(CQ))
            pe.wait_ge(norm_done, 8)
            for j in range(2):
                unit(latent(CKV))
            for j in range(2):
                unit(latent_tokens)
            drained_all()
            for j in range(6):
                sum_squares()
                unit(project)
                if j in (0, 4):
                    banks_back()
                else:
                    spread_rows()
                unit(project)
                if j not in (0, 4):
                    rows_back()

            pe.wait_ge(norm_done, 14)

            def scores(h):
                if h >= 2:
                    pe.wait_ge(at_exp, h - 1)
                for b in range(TB):
                    c = slice(b * P, (b + 1) * P)
                    if h < HEADS:
                        r = slice(32 * (h % 4), 32 * (h % 4) + 32)
                        mm(bank[4 + h % 2][:, b], QN[:, h, c], KN[:, h], True, False)
                        mm(bank[4 + h % 2][:, b], QR[r, h // 4, c], KR[r, 0], False, False)
                        last = mm(bank[4 + h % 2][:, b], QR[r, 2 + h // 4, c], KR[r, 1], False, True)
                    else:
                        last = mm(bank[4 + h % 2][:, b], QD[:, h - HEADS, c], KD[:, h - HEADS])
                last.then_inc(at_scored, 1)

            scores(0)
            for h in range(2 * HEADS):
                if h + 1 < 2 * HEADS:
                    scores(h + 1)
                for _ in range(gates_beside(h)):
                    unit(project)
                pe.wait_ge(at_p, h + 1)
                if h:
                    pe.wait_ge(at_pt, h)
                for b in range(TB):
                    for c in range(TB):
                        last = nc.tensor.transpose(bank[6][:, c, b * P:(b + 1) * P],
                                                   ES[h % 2][:, b, c * P:(c + 1) * P], ident)
                last.then_inc(at_turned, 1)
                pe.wait_ge(at_pt, h + 1)
                if h:
                    pe.wait_ge(at_kept, h)
                for b in range(TB):
                    last = mm(bank[7][:, 0], (VM if h < HEADS else VD)[:, b, h % HEADS], PS[h % 2][:, b],
                              b == 0, b == TB - 1)
                last.then_inc(at_out, 1)

            def branches2(s):
                for half, y in enumerate((OA, QD)):
                    for k in range(HEADS):
                        c = (half * HEADS + k) * P
                        last = mm(bank[s][:, half], ring[:, s, c:c + P], y[:, k], k == 0, k == HEADS - 1)
                return last

            pe.wait_ge(at_kept, 2 * HEADS)
            rounds(4, branches2)
            drained_all()
            pe.wait_ge(merged_lowered, 2 * KT)
            rounds_split(4, project_split(out2_high, h_low))
            sum_squares()
            after_norm(up_high, h_low)
            for j in range(3):
                unit_split(project_split(up_high, h_low))
            rounds_split(21, project_split(up_high, h_low))
            drained_all()
            down(SPLIT_UP + 1)

        @block.scalar
        def _(act):
            units = Units(landed, rounded, lowered, consumed, drained)
            chain = Count(act_chain)
            norm = [0]
            A = nc.scalar.activation

            def link(ins):
                ins.then_inc(act_chain, 1)
                chain.add()
                act.wait_ge(act_chain, chain.value())

            def drain(body):
                s, _, _, there, _ = units.next()
                act.wait_ge(consumed[s], there)
                body(s).then_inc(drained[s], 1)

            def rounds(n, body, split=0):
                with act.Fori(0, n) as i:
                    units.enter(i)
                    if split:
                        ahead.enter(i, drained=0, split=1)
                    for j in range(RING):
                        if split:
                            round_weights(UNIT)
                        drain(lambda s: body(s, i * RING + j))
                units.leave(n)
                if split:
                    ahead.leave(n)

            ahead = Units(landed, rounded, lowered, consumed, drained)

            def round_weights(cols):
                s, there, _, _, _ = ahead.next(False, split=True)
                act.wait_ge(landed[s], there)
                A(w_high[:, s, 0:cols], ring[:, s, 0:cols], ACT.Copy).then_inc(rounded[s], 1)

            def round_rounds(n, cols):
                with act.Fori(0, n) as i:
                    ahead.enter(i, drained=0, split=1)
                    for j in range(RING):
                        round_weights(cols)
                ahead.leave(n)

            splits = [0]

            def round_input(high):
                for g, (a, b) in enumerate(H_GROUPS):
                    act.wait_ge(h_scaled, len(H_GROUPS) * splits[0] + g + 1)
                    A(high[:, a:b], hT[:, a:b], ACT.Copy).then_inc(h_rounded, 1)
                splits[0] += 1

            def tokens(dst, g, split):
                banks = units.token_banks(g % 2 == 1)
                for kept in units.token_flags(g % 2 == 1):
                    s, _, _, there, _ = units.next(kept, True)
                    if split:
                        round_weights(UNIT)
                act.wait_ge(consumed[s], there)
                for b in range(TB):
                    A(dst[:, b, 4 * g:4 * g + 4].rearrange("p h c -> p (h c)"), bank_row[banks[b]],
                      ACT.Copy).then_inc(drained[banks[b]], 1)

            def round_merged(n, high):
                s, _, _, _, free = units.next()
                act.wait_ge(drained[s], free + 1)
                A(high[:, bass.ds(n, 1)], hT[:, bass.ds(n, 1)], ACT.Copy).then_inc(merged_rounded, 1)

            def merge(high):
                with act.Fori(0, 3) as i:
                    units.enter(i)
                    for j in range(RING):
                        round_merged(i * RING + j, high)
                units.leave(3)
                ahead.skip(units.pos + RING - ahead.pos, False)
                for j in range(RING):
                    if j >= RING - AHEAD:
                        round_weights(UNIT)
                    round_merged(3 * RING + j, high)

            def skip(n, turns=1, kept=True):
                units.skip(n * RING * turns, kept)

            def square():
                n = NORMS[norm[0]]
                norm[0] += 1
                if norm[0] > 1:
                    if norm[0] - 1 == 5:
                        act.wait_ge(norm_summed, 5)
                    else:
                        act.wait_ge(norm_done, norm[0] - 1)
                if n["src"] is xT:
                    for g in range(4):
                        c = slice(4 * g, 4 * g + 4)
                        if norm[0] == 1:
                            act.wait_ge(x_landed[g], 16)
                        if norm[0] - 1 == 5:
                            act.wait_ge(x_scaled, g + 1)
                        A(hT[:, c], xT[:, c], ACT.Square).then_inc(x_squared, 1)
                    return
                A(n["sq"], n["src"], ACT.Square).then_inc(norm_squared, 1)

            def root():
                n = NORMS[norm[0] - 1]
                act.wait_ge(norm_mean, norm[0])
                if "rows" in n:
                    m, r = xms[0:n["rows"]], xrs[0:n["rows"]]
                else:
                    m, r = ((n[k][:] if n[k] in (xms, xrs) else n[k]) for k in ("ms", "rs"))
                A(r, m, ACT.Sqrt).then_inc(norm_rooted, 1)

            def drained_all():
                for s, n in units.all_drained():
                    act.wait_ge(s, n)

            square()
            round_weights(UNIT)
            root()
            round_weights(UNIT)
            round_input(mix_high)

            for j in range(10):
                round_weights(UNIT)
                drain(lambda s: A(MT[:, U0 + j], bank[s][:, 0], ACT.Copy))
            act.wait_ge(vec_landed, 16)
            c = VAT["log_dt"]
            A(s5c[:, 0], vec[:, c:c + S5_STATES], ACT.Exp).then_inc(s5_fn, 1)
            act.wait_ge(s5_arg, 1)
            A(s5c[:, 7], s5c[:, 1], ACT.Exp)
            act.wait_ge(lb_arg, 1)
            A(lb[:, 1], lb[:, 0], ACT.Exp).then_inc(lb_exp, 1)
            A(s5c[:, 8], s5c[:, 4], ACT.Sin)
            A(s5c[:, 9], s5c[:, 6], ACT.Sin).then_inc(s5_fn, 1)

            for g in range(3):
                tokens(VN, g, True)
            rounds(3, lambda s, n: A(MT[:, bass.ds(n + F0, 1)], bank[s][:, 0:1], ACT.Sigmoid), split=1)
            rounds(2, lambda s, n: A(MT[:, bass.ds(n + Q0, 1)], bank[s][:, 0:1], ACT.Silu), split=1)
            for j in range(RING):
                if j < AHEAD:
                    round_weights(UNIT)
                drain(lambda s: A(MT[:, Q0 + 2 * RING + j], bank[s][:, 0], ACT.Silu))

            def gates(at, n):
                def body(s, m):
                    if isinstance(m, int):
                        return A(G[:, at + m], bank[s][:, 0], ACT.Sigmoid)
                    return A(G[:, bass.ds(m + at, 1)], bank[s][:, 0:1], ACT.Sigmoid)
                rounds(n, body)

            def gate(n):
                drain(lambda s: A(G[:, n], bank[s][:, 0], ACT.Sigmoid))

            act.wait_ge(conv_ready, 1)
            A(CA, CA, ACT.Silu).then_inc(conv_act, 1)
            act.wait_ge(rows_abs, 1)
            link(A(rows[:, 0], rows[:, 0], ACT.Exp, scale=-1.0))
            A(rows[:, 0], rows[:, 0], ACT.Ln, bias=1.0).then_inc(rows_log, 1)
            for dst, scale in ((QH, 1.0), (KH, ML_DH ** -0.5)):
                s, _, _, there, _ = units.next(False)
                act.wait_ge(consumed[s], there)
                for j in range(3):
                    last = A(dst[:, 2 * j:2 * j + 2], bank[4 + j][:], ACT.Copy, scale=scale)
                last.then_inc(qk_ready, 1)
            act.wait_ge(rows_ready, 1)
            A(rows[:, 5], rows[:, 4], ACT.Exp, scale=-1.0).then_inc(rows_thr, 1)
            gates(0, 1)
            act.wait_ge(cast_done, 1)
            A(acol[:], bank[4][:, 0, 0:TB * ML].rearrange("p (b h) -> p b h", h=ML), ACT.Copy)
            for j in range(2):
                last = A(MB[:, 2 * j:2 * j + 2], bank[5 + j][:], ACT.Copy)
            last.then_inc(cast_taken, 1)
            act.wait_ge(cast_done, 2)
            for j in range(2):
                last = A(TH[:, 2 * j:2 * j + 2], bank[5 + j][:], ACT.Copy)
            last.then_inc(cast_taken, 1)
            for h in range(ML):
                act.wait_ge(ml_arg, h + 1)
                A(PM[:, h], PM[:, h], ACT.Exp, scale=-1.0).then_inc(ml_exp, 1)
            gates(4, 1)
            gate(8)
            act.wait_ge(ml_h, 1)
            square()
            gate(9)
            root()
            gate(10)
            gate(11)

            gates(12, 1)
            gates(16, 1)
            act.wait_ge(hg_out, 1)
            for j in range(3):
                last = A(HO[:, 2 * j:2 * j + 2], bank[4 + j][:], ACT.Copy)
            link(last)
            square()
            gate(20)
            gate(21)
            root()
            gate(22)
            gate(23)

            units.next(False)
            _s, _, _, last_fed, _ = units.next(False)
            for n in range(S5_STATES):
                if n < S5_STATES - 1:
                    act.wait_ge(s5_fed, n + 1)
                else:
                    act.wait_ge(consumed[_s], last_fed)
                A(SR[:, n], bank[4 + n % 4][:, 0], ACT.Copy, scale=s5c[:, 11, n:n + 1])
                A(SI[:, n], bank[4 + n % 4][:, 1], ACT.Copy, scale=s5c[:, 11, n:n + 1]).then_inc(s5_scaled, 1)
            gates(24, 5)
            act.wait_ge(s5_tabled, S5_TILES)
            gates(44, 1)
            units.next(False)
            units.next(False)
            act.wait_ge(s5_pre, 1)
            A(GA, GA, ACT.Gelu_apprx_tanh).then_inc(s5_gelu, 1)
            s, _, _, there, _ = units.next(False)
            act.wait_ge(consumed[s], there)
            for f in range(S5_TILES):
                last = A(MT[:, U0 + f], bank[4 + f // 2][:, f % 2], ACT.Sigmoid, bias=v("b_glu", f))
            last.then_inc(s5_gate, 1)
            merge(out_high)
            round_rounds(4, UNIT)
            skip(4)
            drained_all()
            square()
            root()
            round_input(up_high)

            acts = Count(ff_done)

            def round_act(n):
                A(acts_high[:, bass.ds(n, 1)], ACTS[:, bass.ds(n, 1)], ACT.Copy).then_inc(acts_rounded, 1)

            def conv_round(i, cols, split):
                for j in range(2):
                    s, _, _, _, free = units.next()
                    round_weights(cols[2 * j])
                    round_weights(cols[2 * j + 1])
                    act.wait_ge(drained[s], free + 1)
                    A(cv[:, 2 * j], cv[:, 2 * j], ACT.Silu).then_inc(silu_pair, 1)
                    units.next()
                    acts.add()
                    if split:
                        act.wait_ge(ff_done, acts.value())
                        round_act(i * 2 + j)

            def conv_rounds(first, n, split):
                with act.Fori(0, n) as i:
                    units.enter(i)
                    ahead.enter(i, drained=0, split=1)
                    acts.enter(i, 2)
                    conv_round(i + first if first else i, [UNIT] * RING, split)
                units.leave(n)
                ahead.leave(n)
                acts.leave(n)

            def last_acts():
                A(acts_high[:, SPLIT_UP:], ACTS[:, SPLIT_UP:], ACT.Copy).then_inc(acts_rounded, 1)

            conv_rounds(0, SPLIT_UP // 2, True)
            conv_rounds(SPLIT_UP // 2, 21 - SPLIT_UP // 2, False)
            conv_round(21, [UNIT] * 2 + [DOWN * P] * 2, False)
            act.wait_ge(ff_done, FF_TILES)
            last_acts()
            round_rounds(15, DOWN * P)
            for j in range(2):
                round_weights(DOWN * P)
            for j in range(AHEAD):
                round_weights(UNIT)
            skip(16, kept=False)
            for b in range(2):
                act.wait_ge(down_drained[b], 1 + KT // 2)
            square()
            root()
            square()
            root()
            round_input(in2_high)

            rounds(6, lambda s, n: A(P2[:, bass.ds(n, 1)], bank[s][:, 0:1], ACT.Copy), split=1)
            for j in (24, 25):
                round_weights(UNIT)
                drain(lambda s: A(P2[:, j], bank[s][:, 0], ACT.Copy))
            drained_all()
            square()
            tokens(VD, 0, True)
            root()
            for j in range(2):
                round_weights(UNIT)
            square()
            tokens(VD, 1, False)
            root()

            def two_banks(a, b):
                def body(s):
                    A(a, bank[s][:], ACT.Copy)
                    return A(b, bank[4 + s][:], ACT.Copy)
                return body

            def tokens(j):
                def body(s):
                    A(VM[:, 0, 4 * j:4 * j + 4].rearrange("p h c -> p (h c)"), bank_row[s], ACT.Copy)
                    return A(VM[:, 1, 4 * j:4 * j + 4].rearrange("p h c -> p (h c)"), bank_row[4 + s], ACT.Copy)
                return body

            for dst, j in ((QN, 0), (QN, 1), (QR, 0), (KN, 0), (KN, 1)):
                drain(two_banks(dst[:, 4 * j:4 * j + 2], dst[:, 4 * j + 2:4 * j + 4]))
            for j in range(2):
                drain(tokens(j))
            drained_all()

            def gate2(n):
                drain(lambda s: A(G2[:, n], bank[s][:, 0], ACT.Sigmoid, bias=v("b_gate", n)))

            for j in range(6):
                square()
                if j:
                    gate2(2 * j - 1)
                root()
                gate2(2 * j)
            gate2(11)
            at = 12

            act.wait_ge(band_landed, 16)
            for h in range(2 * HEADS):
                e, p = ES[h % 2], PS[h % 2]
                if h == HEADS:
                    for g in (0, 1):
                        A(BS[g], band[:, 0:2], ACT.Copy, scale=SLOPES[g]).then_inc(at_bias, 1)
                act.wait_ge(at_max, h + 1)
                if h >= 2:
                    act.wait_ge(at_turned, h - 1)
                if h < HEADS:
                    for b in range(TB):
                        last = A(e[:, b], bank[4 + h % 2][:, b], ACT.Exp, bias=small[:, h % 2, 2 + b:3 + b],
                                 scale=192 ** -0.5, accum_out=small[:, h % 2, 4 + b:5 + b])
                else:
                    for b in range(TB):
                        last = A(e[:, b], e[:, b], ACT.Exp, bias=small[:, h % 2, 2 + b:3 + b])
                last.then_inc(at_exp, 1)
                if HEADS <= h < 2 * HEADS - 2:
                    A(BS[h % 2], band[:, 0:2], ACT.Copy, scale=SLOPES[h + 2 - HEADS]).then_inc(at_bias, 1)
                for j in range(gates_beside(h)):
                    gate2(at)
                    at += 1
                act.wait_ge(at_turned, h + 1)
                if h >= 2:
                    act.wait_ge(at_out, h - 1)
                A(p, bank[6][:], ACT.Copy).then_inc(at_pt, 1)
                act.wait_ge(at_out, h + 1)
                A((OA if h < HEADS else QD)[:, h % HEADS], bank[7][:, 0], ACT.Copy).then_inc(at_kept, 1)
            merge(out2_high)
            round_rounds(4, UNIT)
            skip(4)
            drained_all()
            square()
            root()
            round_input(up_high)

            def gate_round(i, cols, split):
                for j in range(2):
                    s, _, _, there, _ = units.next()
                    su, _, _, _, used = units.next()
                    round_weights(cols[2 * j])
                    act.wait_ge(consumed[s], there)
                    act.wait_ge(drained[su], used)
                    A(cv[:, 2 * j], bank[s][:, 0], ACT.Silu).then_inc(drained[s], 1)
                    round_weights(cols[2 * j + 1])
                    if split:
                        act.wait_ge(drained[su], used + 1)
                        round_act(i * 2 + j)

            def gate_rounds(first, n, split):
                with act.Fori(0, n) as i:
                    units.enter(i)
                    ahead.enter(i, drained=0, split=1)
                    gate_round(i + first if first else i, [UNIT] * RING, split)
                units.leave(n)
                ahead.leave(n)

            gate_rounds(0, SPLIT_UP // 2, True)
            gate_rounds(SPLIT_UP // 2, 21 - SPLIT_UP // 2, False)
            gate_round(21, [UNIT] * 2 + [DOWN * P] * 2, False)
            drained_all()
            last_acts()
            round_rounds(15, DOWN * P)
            for j in range(2):
                round_weights(DOWN * P)

        @block.vector
        def _(dve):
            V = nc.vector
            units = Units(landed, rounded, lowered, consumed, drained)
            chain = Count(dve_chain)
            norm = [0]
            M, ADD, SUB, MAX, MIN = ALU.mult, ALU.add, ALU.subtract, ALU.max, ALU.min

            def link(ins):
                ins.then_inc(dve_chain, 1)
                chain.add()
                dve.wait_ge(dve_chain, chain.value())

            def stt(o, a, s, b, op0=M, op1=M, **kw):
                return V.scalar_tensor_tensor(out=o, in0=a, scalar=s, in1=b, op0=op0, op1=op1, **kw)

            def tt(o, a, b, op=M):
                return V.tensor_tensor(o, a, b, op)

            ahead = Units(landed, rounded, lowered, consumed, drained)

            def lower_weights(cols):
                s, _, _, _, _ = ahead.next(False, split=True)
                dve.wait_ge(rounded[s], ahead.rounded[s].value())
                tt(w_low[:, s, 0:cols], ring[:, s, 0:cols], w_high[:, s, 0:cols].bitcast(F32), SUB)\
                    .then_inc(lowered[s], 1)

            def lower_rounds(n, cols):
                with dve.Fori(0, n) as i:
                    ahead.enter(i, drained=0, split=1)
                    for j in range(RING):
                        lower_weights(cols)
                ahead.leave(n)

            splits = [0]

            def normalise_split(gain, high, low):
                rs = reciprocal_root()
                if splits[0] == 0:
                    dve.wait_ge(vec_landed, 16)
                for k in range(KT):
                    last = stt(hT[:, k], xT[:, k], v(gain, k), rs)
                    if k + 1 in [b for _, b in H_GROUPS]:
                        last.then_inc(h_scaled, 1)
                if splits[0] == 0:
                    lower_weights(UNIT)
                for g in range(H_POOL, len(H_GROUPS)):
                    c = slice(*H_GROUPS[g])
                    dve.wait_ge(h_rounded, len(H_GROUPS) * splits[0] + g + 1)
                    last = tt(low[:, c], hT[:, c], high[:, c].bitcast(F32), SUB)
                    last.then_inc(h_lowered_vector, 1)
                dve.wait_ge(h_lowered_pool, H_POOL * (splits[0] + 1))
                splits[0] += 1
                V.tensor_copy(xtmp[:, 0:1], rs[:, 0:1]).then_inc(norm_done, 1)

            paired = [0]

            def pair(g):
                paired[0] += 1
                dve.wait_ge(x_squared, paired[0])
                tt(hT[:, 4 * g:4 * g + 2], hT[:, 4 * g:4 * g + 2], hT[:, 4 * g + 2:4 * g + 4], ADD)\
                    .then_inc(x_paired, 1)

            def reciprocal_root():
                n = NORMS[norm[0]]
                if n["src"] is xT and norm[0] != 5:
                    for g in range(4):
                        pair(g)
                if norm[0] == 0:
                    lower_weights(UNIT)
                norm[0] += 1
                dve.wait_ge(norm_summed, norm[0])
                G_ = len(n["groups"])
                one = n["ms"] is xms
                ms, rs = (n["ms"][:], n["rs"][:]) if one else (n["ms"], n["rs"])
                if G_ == 1:
                    last = V.tensor_scalar(ms if one else ms[:, 0], bank[4][:, 0], 1.0 / n["n"], EPS, M, ADD)
                else:
                    for j in range(G_ // 2):
                        last = V.tensor_scalar(ms[:, 2 * j:2 * j + 2], bank[4 + j][:], 1.0 / n["n"], EPS, M, ADD)
                last.then_inc(norm_mean, 1)
                dve.wait_ge(norm_rooted, norm[0])
                tmp = xtmp[:] if one else n["sq"][:, 0:G_]
                link(V.reciprocal(rs, rs))
                link(tt(tmp, ms, rs))
                link(tt(tmp, tmp, rs))
                link(V.tensor_scalar(tmp, tmp, -0.5, 1.5, M, ADD))
                link(tt(rs, rs, tmp))
                return rs

            casts = [0]

            def row_factors():
                n = NORMS[norm[0]]
                norm[0] += 1
                casts[0] += 1
                dve.wait_ge(norm_summed, norm[0])
                ms, rs, tmp = xms[0:n["rows"]], xrs[0:n["rows"]], xtmp[0:n["rows"]]
                V.tensor_scalar(ms, bank[4][0:n["rows"], 0], 1.0 / n["n"], EPS, M, ADD).then_inc(norm_mean, 1)
                dve.wait_ge(norm_rooted, norm[0])
                link(V.reciprocal(rs, rs))
                link(tt(tmp, ms, rs))
                link(tt(tmp, tmp, rs))
                link(V.tensor_scalar(tmp, tmp, -0.5, 1.5, M, ADD))
                tt(rs, rs, tmp).then_inc(norm_rows, 1)
                dve.wait_ge(norm_spread, casts[0])

            def factor(h):
                return bank[4 + h // 2][:, h % 2]

            def final_norm():
                rs = reciprocal_root()
                for k in range(KT):
                    last = stt(xT[:, k], xT[:, k], v("final_norm", k), rs)
                    if k % 4 == 3:
                        last.then_inc(x_scaled, 1)
                        if k > 3:
                            pair(k // 4 - 1)
                pair(3)
                V.tensor_copy(xtmp[:, 0:1], rs[:, 0:1]).then_inc(norm_done, 1)

            def drained_all():
                for s, n in units.all_drained():
                    dve.wait_ge(s, n)

            def skip(n, kept=True):
                units.skip(n * RING, kept)

            V.memset(ones[:], 1.0).then_inc(ones_set, 1)
            for b in range(2):
                V.memset(small[:, b], 0.0).then_inc(down_drained[b], 1)
            normalise_split("mix_norm", mix_high, mix_low)
            for j in range(8):
                lower_weights(UNIT)

            c = VAT["lam_re"]
            lr, li = vec[:, c:c + S5_STATES], vec[:, c + S5_STATES:c + 2 * S5_STATES]
            dt_, e_, th, kk, r1, kc, r2, mag, sn, cs, den, cr, ci, nci, t1, am1 = (s5c[:, j] for j in range(16))
            dve.wait_ge(s5_fn, 1)
            link(tt(e_, lr, dt_))
            link(tt(th, li, dt_))

            def reduced(o, k, shift):
                link(V.tensor_scalar(k, th, 1.0 / TWO_PI, shift / TWO_PI, M, ADD))
                link(V.tensor_scalar(k, k, ROUND, None, ADD))
                link(V.tensor_scalar(k, k, ROUND, None, SUB))
                link(stt(o, k, -PI_HI, th, M, ADD))
                link(stt(o, k, -PI_MID, o, M, ADD))
                link(stt(o, k, -PI_LO, o, M, ADD))
                link(V.tensor_scalar(o, o, shift, PI_IN, ADD, MIN))
                return V.tensor_scalar(o, o, -PI_IN, None, MAX)

            reduced(r1, kk, 0.0)
            reduced(r2, kc, float(np.pi / 2)).then_inc(s5_arg, 1)
            c = VAT["hg_lb"]
            tt(lb[:, 0], vec[:, c:c + HG], vec[:, c:c + HG], SUB).then_inc(lb_arg, 1)
            dve.wait_ge(lb_exp, 1)
            link(V.reciprocal(lb[:, 2], lb[:, 1]))
            link(tt(lb[:, 2], lb[:, 2], lb[:, 1]))
            link(tt(lb[:, 0], lb[:, 2], lb[:, 2], SUB))
            link(V.tensor_scalar(lb[:, 1], lb[:, 0], -1.0, 1.0, M, ADD))
            dve.wait_ge(s5_fn, 2)
            zr, zi = s5c[:, 2], s5c[:, 3]
            link(tt(zr, mag, cs))
            link(tt(zi, mag, sn))

            def unit_modulus(re, im):
                link(tt(den, re, re))
                link(tt(t1, im, im))
                link(tt(den, den, t1, ADD))
                link(V.tensor_scalar(den, den, -0.5, 1.5, M, ADD))
                link(tt(re, re, den))
                link(tt(im, im, den))

            link(V.tensor_copy(s5p[:, 0, 0], cs))
            link(V.tensor_copy(s5p[:, 0, 1], sn))
            unit_modulus(s5p[:, 0, 0], s5p[:, 0, 1])
            for k in range(1, S5_STEPS):
                a, b = s5p[:, k - 1], s5p[:, k]
                link(tt(t1, a[:, 1], a[:, 1]))
                link(tt(b[:, 0], a[:, 0], a[:, 0]))
                link(tt(b[:, 0], b[:, 0], t1, SUB))
                link(stt(b[:, 1], a[:, 0], 2.0, a[:, 1]))
                unit_modulus(b[:, 0], b[:, 1])
            for j in range(2):
                link(V.memset(powers[:, 2 * j, :, 0:1], 1.0))
                link(V.memset(powers[:, 2 * j + 1, :, 0:1], 0.0))
                tmp = xtmp[:].rearrange("p (n a) -> p n a", a=S5_SIDE)
                for k in range(4):
                    d = 1 << k
                    re, im = powers[:, 2 * j, :, 0:d], powers[:, 2 * j + 1, :, 0:d]
                    to_re, to_im = powers[:, 2 * j, :, d:2 * d], powers[:, 2 * j + 1, :, d:2 * d]
                    cw, sw = (s5p[:, 4 * j + k, c].rearrange("p (n o) -> p n o", o=1)
                              .broadcast_to([P, S5_STATES, d]) for c in range(2))
                    link(tt(to_re, re, cw))
                    link(tt(tmp[:, :, 0:d], im, sw))
                    link(tt(to_re, to_re, tmp[:, :, 0:d], SUB))
                    link(tt(to_im, re, sw))
                    link(tt(tmp[:, :, 0:d], im, cw))
                    link(tt(to_im, to_im, tmp[:, :, 0:d], ADD))
            link(tt(den, lr, lr))
            link(tt(t1, li, li))
            link(tt(den, den, t1, ADD))
            link(V.reciprocal(den, den))
            link(V.tensor_scalar(am1, zr, -1.0, None, ADD))
            link(tt(cr, am1, lr))
            link(tt(t1, zi, li))
            link(tt(cr, cr, t1, ADD))
            link(tt(cr, cr, den))
            link(tt(ci, zi, lr))
            link(tt(t1, am1, li))
            link(tt(ci, ci, t1, SUB))
            link(tt(ci, ci, den))
            link(V.tensor_scalar(nci, ci, -1.0, None, M))

            units.skip(10)
            drained_all()
            ahead.skip(12, False, split=True)
            for k in range(ML_TILES):
                x, o = MT[:, CX0 + k], CA[:, k]
                w = [v("ml_conv", 5 * k + j) for j in range(5)]
                link(V.tensor_scalar(o, x, w[3], w[4], M, ADD))
                for j in range(1, 4):
                    last = stt(o[:, j:], x[:, 0:T - j], w[3 - j], o[:, j:], M, ADD)
                    if k < ML_TILES - 1 or j < 3:
                        link(last)
            last.then_inc(conv_ready, 1)
            lower_rounds(6, UNIT)
            units.skip_tokens(3)
            skip(6)
            dve.wait_ge(if_summed, 1)
            link(V.tensor_scalar(rows[:, 2], bank[7][0:ML, 0], v("b_ig", 0, ML), None, ADD))
            link(V.tensor_scalar(rows[:, 3], bank[7][0:ML, 1], v("b_fg", 0, ML), None, ADD))
            stt(rows[:, 0], rows[:, 3], -1.0, rows[:, 3], M, MAX).then_inc(rows_abs, 1)
            link(V.tensor_scalar(rows[:, 3], rows[:, 3], 0.0, None, MIN))
            dve.wait_ge(rows_log, 1)
            link(tt(rows[:, 3], rows[:, 3], rows[:, 0], SUB))
            link(V.memset(rows[:, 4], 1.0))
            link(V.tensor_tensor_scan(rows[:, 1], rows[:, 4], rows[:, 3], 0.0, M, ADD))
            link(tt(rows[:, 2], rows[:, 2], rows[:, 1], SUB))
            link(V.tensor_tensor_scan(rows[:, 3], rows[:, 2], rows[:, 2], 0.0, MAX, MAX))
            tt(rows[:, 4], rows[:, 1], rows[:, 3], ADD).then_inc(rows_ready, 1)
            units.skip(2, False)
            skip(1)
            dve.wait_ge(qk_ready, 2)
            dve.wait_ge(cast_taken, 1)
            for h in range(ML):
                V.tensor_scalar(PM[:, h, 0:T], MB[:, h], acol[:, 0, h:h + 1], 0.0, SUB, MAX)
                V.tensor_scalar(PM[:, h, T:], MB[:, h, P:], acol[:, 1, h:h + 1], 0.0, SUB, MAX).then_inc(ml_arg, 1)
            dve.wait_ge(cst_landed, 48)
            for h in range(ML):
                dve.wait_ge(ml_exp, h + 1)
                dve.wait_ge(ml_scored, h + 1)
                link(tt(PM[:, h, 0:T], PM[:, h, 0:T], bank[4 + h][:, 0]))
                link(tt(PM[:, h, T:], PM[:, h, T:], bank[4 + h][:, 1, P:]))
                for at in (0, T):
                    last = tt(PM[:, h, at:at + P], PM[:, h, at:at + P], causal)
                last.then_inc(ml_p, 1)
            skip(1)
            dve.wait_ge(cast_taken, 2)
            dve.wait_ge(ml_den, 1)
            for j in range(2):
                th = TH[:, 2 * j:2 * j + 2]
                link(stt(th, bank[4 + j][:], -1.0, th, M, MAX))
                last = tt(th, bank[4 + j][:], th, MAX)
                if j == 0:
                    link(last)
            last.then_inc(ml_den_taken, 1)
            dve.wait_ge(ml_den_taken, 1)
            V.reciprocal(TH, TH).then_inc(ml_rden, 1)
            dve.wait_ge(ml_rden, 1)
            dve.wait_ge(ml_num, 1)
            for h in range(ML):
                for k, p0, p1, _ in PIECES[h]:
                    last = tt(HH[p0:p1, k], bank[4 + k // 2][p0:p1, k % 2], TH[p0:p1, h])
            last.then_inc(ml_h, 1)
            for h in range(HG):
                last = (V.tensor_scalar(HF[:, h], HF[:, h], lb[:, 1, h:h + 1], lb[:, 0, h:h + 1], M, ADD))
            link(last)
            V.tensor_scalar(HK, HF, -1.0, 1.0, M, ADD).then_inc(hg_x, 1)
            V.memset(PD, 0.0)
            skip(1)
            row_factors()
            for h in range(ML):
                for k, p0, p1, _ in PIECES[h]:
                    c = VAT["ml_norm"] + k
                    last = stt(HH[p0:p1, k], HH[p0:p1, k], vec[p0:p1, c:c + 1], factor(h)[p0:p1])
            link(last)
            drained_all()
            tt(MT[:, O0:O0 + 6], HH, MT[:, O0:O0 + 6]).then_inc(norm_done, 1)
            dve.wait_ge(norm_done, 2)

            link(V.memset(HPR, 1.0))
            dve.wait_ge(hg_x, 1)
            dve.wait_ge(hmask_landed, 16)

            def halves(ap, B):
                return ap.rearrange("p k t -> p (k t)").rearrange("p (n two b) -> p n two b", two=2, b=B)

            def meet(lvl):
                B = 1 << (lvl - 1)
                X = [HX0, HX1][lvl % 2]
                if lvl >= 3:
                    dve.wait_ge(hg_scored, lvl - 1)
                x, q, k, pf, pr = (halves(a, B) for a in (X, HQ, HK, HF, HPR))
                tt(x[:, :, 1], q[:, :, 1], pf[:, :, 1])
                tt(x[:, :, 0], k[:, :, 0], pr[:, :, 0]).then_inc(hg_x, 1)
                if B < P:
                    n = [P, HG * T // (2 * B), B]
                    link(tt(pr[:, :, 0], pr[:, :, 0], pf[:, :, 1, B - 1:B].broadcast_to(n)))
                    link(tt(pf[:, :, 1], pf[:, :, 1], pf[:, :, 0, B - 1:B].broadcast_to(n)))

            meet(1)
            meet(2)
            for lvl in range(9):
                dve.wait_ge(hg_scored, lvl + 1)
                if lvl == 8:
                    V.tensor_copy(PO[:, 0:4].rearrange("p h c -> p (h c)"), bank_row[4])
                    V.tensor_copy(PO[:, 4:6].rearrange("p h c -> p (h c)"), bank_row[5][:, 0:2 * P]).then_inc(hg_taken, 1)
                else:
                    m = hmask[:, lvl:lvl + 1].broadcast_to([P, 4, P])
                    for j in range(3):
                        last = V.copy_predicated(PD[:, 2 * j:2 * j + 2].rearrange("p k (b c) -> p (k b) c", c=P), m,
                                                 bank_row[4 + j].rearrange("p (k c) -> p k c", c=P))
                    last.then_inc(hg_taken, 1)
                if 1 <= lvl <= 6:
                    meet(lvl + 2)
            skip(2)
            skip(1)
            row_factors()
            for h in range(HG):
                last = stt(HO[:, h], HO[:, h], v("hg_norm", h), factor(h))
            link(last)
            tt(HQ, HO, MT[:, OG0:OG0 + 6]).then_inc(norm_done, 1)
            dve.wait_ge(norm_done, 3)

            units.skip(2, False)
            for n in range(S5_STATES):
                dve.wait_ge(s5_scaled, n + 1)
                stt(SR[:, n], bank[4 + n % 4][:, 1], nci[:, n:n + 1], SR[:, n], M, ADD)
                stt(SI[:, n], bank[4 + n % 4][:, 0], ci[:, n:n + 1], SI[:, n], M, ADD).then_inc(s5_in, 1)
            dve.wait_ge(s5_in, S5_STATES)
            with dve.Fori(0, S5_TILES) as i:
                chain.enter(i, 5 + 6 + 1 + 5)
                four = bass.ds(i * 4, 4)
                size = [P, 4, S5_SIDE, S5_SIDE]
                lo_c, lo_s = (powers[:, j, four].rearrange("p n (o a) -> p n o a", o=1).broadcast_to(size)
                              for j in (0, 1))
                hi_c, hi_s = (powers[:, j, four].rearrange("p n (a o) -> p n a o", o=1).broadcast_to(size)
                              for j in (2, 3))
                c4, s4, t4 = (x.rearrange("p n (a b) -> p n a b", b=S5_SIDE) for x in (turn_c, turn_s, tmp_r))
                link(tt(c4, hi_c, lo_c))
                link(tt(t4, hi_s, lo_s))
                link(tt(c4, c4, t4, SUB))
                link(tt(s4, hi_c, lo_s))
                link(tt(t4, hi_s, lo_c))
                tt(s4, s4, t4, ADD).then_inc(s5_tabled, 1)
                dve.wait_ge(s5_tabled, i + 1)
                xr, xi = SR[:, four], SI[:, four]
                link(tt(tmp_r, turn_s, xr))
                link(tt(tmp_i, turn_s, xi))
                link(tt(xr, turn_c, xr))
                link(tt(xi, turn_c, xi))
                link(tt(xr, xr, tmp_i, ADD))
                link(tt(xi, xi, tmp_r, SUB))
                for n in range(4):
                    m = mag[:, bass.ds(i * 4 + n, 1)].broadcast_to([P, T])
                    one = bass.ds(i * 4 + n, 1)
                    for o, x in ((tmp_r, SR), (tmp_i, SI)):
                        last = V.tensor_tensor_scan(o[:, n], m, x[:, one].rearrange("p k t -> p (k t)"), 0.0, M, ADD)
                link(last)
                link(tt(xr, turn_c, tmp_r))
                link(tt(xi, turn_s, tmp_r))
                link(tt(tmp_r, turn_s, tmp_i))
                link(tt(xr, xr, tmp_r, SUB))
                link(tt(tmp_i, turn_c, tmp_i))
                tt(xi, xi, tmp_i, ADD).then_inc(s5_states, 1)
            chain.leave(S5_TILES)
            skip(6)
            units.skip(1, False)
            s, _, _, there, _ = units.next(False)
            dve.wait_ge(consumed[s], there)
            for f in range(S5_TILES):
                link(stt(GA[:, f], MT[:, U0 + f], v("s5_d", f), bank[4 + f][:, 0], M, ADD))
                last = tt(GA[:, f], GA[:, f], bank[4 + f][:, 1], SUB)
            last.then_inc(s5_pre, 1)
            units.next(False)
            dve.wait_ge(s5_gate, 1)
            tt(MT[:, U0:U0 + 4], MT[:, U0:U0 + 4], GA).then_inc(s5_done, 1)

            def rounds_split(n, body):
                with dve.Fori(0, n) as i:
                    units.enter(i)
                    ahead.enter(i, drained=0, split=1)
                    for j in range(RING):
                        s, _, _, there, _ = units.next()
                        lower_weights(UNIT)
                        dve.wait_ge(consumed[s], there)
                        body(s, i * RING + j).then_inc(drained[s], 1)
                units.leave(n)
                ahead.leave(n)

            def looped(n, per, body):
                with dve.Fori(0, n) as i:
                    units.enter(i)
                    chain.enter(i, per)
                    body(i)
                units.leave(n)
                chain.leave(n)

            def gated(parts):
                def body(i):
                    for j in range(RING):
                        s, _, _, there, _ = units.next()
                        if i is None and j >= RING - AHEAD:
                            lower_weights(UNIT)
                        dve.wait_ge(consumed[s], there)
                        n = (3 if i is None else i) * RING + j
                        o = hT[:, bass.ds(n, 1)]
                        tmp = xtmp[:].rearrange("p (k t) -> p k t", k=1)
                        for m, (g, at, b, half) in enumerate(parts):
                            x = bank[b + s][:, half:half + 1]
                            gate = g[:, bass.ds(n + at, 1)]
                            if m == 0:
                                link(tt(o, gate, x))
                            else:
                                link(tt(tmp, gate, x))
                                last = tt(o, o, tmp, ADD)
                                if m < len(parts) - 1:
                                    link(last)
                        last.then_inc(drained[s], 1)
                return body

            def add_residual(s, n):
                return tt(xT[:, bass.ds(n, 1)], xT[:, bass.ds(n, 1)], bank[s][:, 0:1], ADD)

            def down(after):
                def turn(i, cols):
                    for b in range(2):
                        for q in range(4):
                            s, _, _, there, _ = units.next(False)
                            if cols[4 * b + q]:
                                lower_weights(cols[4 * b + q])
                        dve.wait_ge(consumed[s], there)
                        n = i * 2 + b
                        tt(xT[:, bass.ds(n, 1)], xT[:, bass.ds(n, 1)], bank[4 + b][:, 0:1], ADD)\
                            .then_inc(down_drained[b], 1)

                with dve.Fori(0, 7) as i:
                    units.enter(i, turns=2, drained=0)
                    ahead.enter(i, turns=2, drained=0, split=1)
                    turn(i, [DOWN * P] * 8)
                units.leave(7)
                ahead.leave(7)
                turn(7, [DOWN * P] * 6 + [after] * AHEAD)

            def merge(parts):
                body = gated(parts)
                looped(3, (2 * len(parts) - 2) * RING, body)
                ahead.skip(units.pos + RING - ahead.pos, False)
                body(None)

            merge([(G, 0, 0, 0), (G, 16, 0, 1), (G, 32, 4, 0)])
            rounds_split(4, add_residual)
            drained_all()
            normalise_split("ffn_norm", up_high, h_low)

            pairs = Count(silu_pair)

            def conv_pairs(i, cols):
                for j in range(2):
                    for half in range(2):
                        s, _, _, there, free = units.next()
                        if 2 * j + half == POOL_TURN:
                            ahead.next(False, split=True)
                        else:
                            lower_weights(cols[2 * j + half])
                        dve.wait_ge(consumed[s], there)
                        n = i * RING + (2 * j + half)
                        o, x = cv[:, 2 * j + half], bank[s][:, 0]

                        def w(c):
                            return vec[:, bass.ds(n * 4 + (VAT["ffn_conv"] + c), 1)]

                        link(V.tensor_scalar(o, x, w(2), w(3), M, ADD))
                        link(stt(o[:, 1:], x[:, 0:T - 1], w(1), o[:, 1:], M, ADD))
                        stt(o[:, 2:], x[:, 0:T - 2], w(0), o[:, 2:], M, ADD).then_inc(drained[s], 1)
                    dve.wait_ge(drained[s], free + 1)
                    pairs.add()
                    dve.wait_ge(silu_pair, pairs.value())
                    tt(ACTS[:, bass.ds(i * 2 + j, 1)], cv[:, 2 * j:2 * j + 1], cv[:, 2 * j + 1:2 * j + 2])\
                        .then_inc(ff_done, 1)

            with dve.Fori(0, 21) as i:
                units.enter(i)
                ahead.enter(i, drained=0, split=1)
                chain.enter(i, 8)
                pairs.enter(i, 2)
                conv_pairs(i, [UNIT] * RING)
            units.leave(21)
            ahead.leave(21)
            chain.leave(21)
            pairs.leave(21)
            conv_pairs(21, [UNIT] * 2 + [DOWN * P] * 2)
            down(UNIT)
            for b in range(2):
                dve.wait_ge(down_drained[b], 1 + KT // 2)
            final_norm()
            dve.wait_ge(norm_done, 5)
            normalise_split("g_mix", in2_high, in2_low)

            lower_rounds(6, UNIT)
            ahead.skip(8, False, split=True)
            skip(6)
            units.skip(2)
            drained_all()
            for src, gain in ((CQ, "g_cq"), (CKV, "g_ckv")):
                rs = reciprocal_root()
                for k in range(4):
                    last = stt(src[:, k], src[:, k], v(gain, k), rs[:, 0])
                last.then_inc(norm_done, 1)
            units.skip_tokens(2)
            units.skip(7)
            drained_all()
            cos, sin = band[:, 4:5], band[:, 5:6]

            def rope(x1, x2, n):
                c, s = cos.broadcast_to([P, n, T]), sin.broadcast_to([P, n, T])
                a, b, c2 = MS[:, 0:n], MS[:, 2:2 + n], MS[:, 4:4 + n]
                link(tt(a, x1, c))
                link(tt(b, x2, s))
                link(tt(c2, x1, s))
                link(tt(x1, a, b, SUB))
                link(tt(b, x2, c))
                tt(x2, c2, b, ADD).then_inc(norm_done, 1)

            def heads(x, gain):
                row_factors()
                for j in range(HEADS // 2):
                    last = stt(x[:, 2 * j:2 * j + 2], x[:, 2 * j:2 * j + 2], v(gain), bank[4 + j][:])
                last.then_inc(norm_done, 1)

            rs = reciprocal_root()
            for half in range(2):
                last = stt(KR[:, half], KR[:, half], v("g_k_rope", half), rs[:, 0])
            link(last)
            dve.wait_ge(band_landed, 16)
            rope(KR[:, 0:1], KR[:, 1:2], 1)
            heads(QD, "g_q_dil")
            heads(KD, "g_k_dil")
            skip(1)
            heads(QN, "g_q_nope")
            rs = reciprocal_root()
            for half in range(2):
                for g in range(2):
                    k = 2 * half + g
                    last = stt(QR[:, k], QR[:, k], v("g_q_rope", half), rs[:, g])
            link(last)
            rope(QR[:, 0:2], QR[:, 2:4], 2)
            heads(KN, "g_k_nope")
            skip(2)
            dve.wait_ge(norm_done, 14)

            for h in range(2 * HEADS):
                e, m = ES[h % 2], small[:, h % 2]
                s = bank[4 + h % 2]
                dve.wait_ge(at_scored, h + 1)
                if h < HEADS:
                    link(V.tensor_reduce(m[:, 0:2], s[:], axis=AX.X, op=MAX))
                    V.tensor_scalar(m[:, 2:4], m[:, 0:2], -(192 ** -0.5), None, M).then_inc(at_max, 1)
                    dve.wait_ge(at_exp, h + 1)
                else:
                    dve.wait_ge(at_bias, h - HEADS + 1)
                    if h >= 2:
                        dve.wait_ge(at_turned, h - 1)
                    link(stt(e, s[:], P ** -0.5, BS[h % 2], M, ADD))
                    link(V.tensor_reduce(m[:, 0:2], e, axis=AX.X, op=MAX))
                    V.tensor_scalar(m[:, 2:4], m[:, 0:2], -1.0, None, M).then_inc(at_max, 1)
                    dve.wait_ge(at_exp, h + 1)
                    for b in range(TB):
                        last = stt(e[:, b], e[:, b], 1.0, band[:, 2 + b], M, M, accum_out=m[:, 4 + b:5 + b])
                    link(last)
                link(V.reciprocal(m[:, 4:6], m[:, 4:6]))
                for b in range(TB):
                    last = V.tensor_scalar(e[:, b], e[:, b], m[:, 4 + b:5 + b], None, M)
                last.then_inc(at_p, 1)
            skip(5)
            merge([(G2, 0, 0, 0), (G2, 16, 0, 1)])
            rounds_split(4, add_residual)
            drained_all()
            normalise_split("g_ffn", up_high, h_low)

            def gate_pairs(i, cols):
                for j in range(2):
                    lower_weights(cols[2 * j])
                    lower_weights(cols[2 * j + 1])
                    sg, _, _, _, gate_free = units.next()
                    s, _, _, there, _ = units.next()
                    dve.wait_ge(consumed[s], there)
                    dve.wait_ge(drained[sg], gate_free + 1)
                    tt(ACTS[:, bass.ds(i * 2 + j, 1)], cv[:, 2 * j:2 * j + 1], bank[s][:, 0:1]).then_inc(drained[s], 1)

            with dve.Fori(0, 21) as i:
                units.enter(i)
                ahead.enter(i, drained=0, split=1)
                gate_pairs(i, [UNIT] * RING)
            units.leave(21)
            ahead.leave(21)
            gate_pairs(21, [UNIT] * 2 + [DOWN * P] * 2)
            down(0)

        @block.gpsimd
        def _(pool):
            ahead = Units(landed, rounded, lowered, consumed, drained)
            splits, merged, acts = [0], Count(merged_rounded), Count(acts_rounded)

            def lower(low, whole, high):
                return nc.gpsimd.tensor_tensor(low, whole, high.bitcast(F32), ALU.subtract)

            def lower_input(high, low):
                for g in range(H_POOL):
                    c = slice(*H_GROUPS[g])
                    pool.wait_ge(h_rounded, len(H_GROUPS) * splits[0] + g + 1)
                    lower(low[:, c], hT[:, c], high[:, c]).then_inc(h_lowered_pool, 1)
                splits[0] += 1

            def lower_merged(high):
                with pool.Fori(0, KT) as i:
                    merged.enter(i, 1)
                    merged.add()
                    pool.wait_ge(merged_rounded, merged.value())
                    c = bass.ds(i, 1)
                    lower(h_low[:, c], hT[:, c], high[:, c]).then_inc(merged_lowered, 1)
                merged.leave(KT)

            def lower_round(i, cols, split):
                for j in range(2):
                    if 2 * j == POOL_TURN:
                        ahead.skip(POOL_TURN, False, split=True)
                        s, _, _, _, _ = ahead.next(False, split=True)
                        pool.wait_ge(rounded[s], ahead.rounded[s].value())
                        lower(w_low[:, s, 0:cols], ring[:, s, 0:cols], w_high[:, s, 0:cols]).then_inc(lowered[s], 1)
                        ahead.skip(RING - 1 - POOL_TURN, False, split=True)
                    if split:
                        acts.add()
                        pool.wait_ge(acts_rounded, acts.value())
                        c = bass.ds(i * 2 + j, 1)
                        lower(acts_low[:, c], ACTS[:, c], acts_high[:, c]).then_inc(acts_lowered, 1)

            def lower_conv_ffn():
                for n, split in ((SPLIT_UP // 2, True), (21 - SPLIT_UP // 2, False)):
                    with pool.Fori(0, n) as i:
                        ahead.enter(i, drained=0, split=1)
                        acts.enter(i, 2 * split)
                        lower_round(i, UNIT, split)
                    ahead.leave(n)
                    acts.leave(n)
                lower_round(21, DOWN * P, False)
                acts.add()
                pool.wait_ge(acts_rounded, acts.value())
                lower(acts_low[:, SPLIT_UP:], ACTS[:, SPLIT_UP:], acts_high[:, SPLIT_UP:]).then_inc(acts_lowered, 1)

            def lower_acts():
                with pool.Fori(0, SPLIT_UP) as i:
                    acts.enter(i, 1)
                    acts.add()
                    pool.wait_ge(acts_rounded, acts.value())
                    c = bass.ds(i, 1)
                    lower(acts_low[:, c], ACTS[:, c], acts_high[:, c]).then_inc(acts_lowered, 1)
                acts.leave(SPLIT_UP)
                acts.add()
                pool.wait_ge(acts_rounded, acts.value())
                lower(acts_low[:, SPLIT_UP:], ACTS[:, SPLIT_UP:], acts_high[:, SPLIT_UP:]).then_inc(acts_lowered, 1)

            def lower_weights():
                s, _, _, _, _ = ahead.next(False, split=True)
                pool.wait_ge(rounded[s], ahead.rounded[s].value())
                lower(w_low[:, s], ring[:, s], w_high[:, s]).then_inc(lowered[s], 1)

            lower_input(mix_high, mix_low)
            ahead.skip(10, False, split=True)
            for j in range(12):
                lower_weights()
            lower_merged(out_high)
            lower_input(up_high, h_low)
            for n, split in ((24, True), (2 + 24 + 2 + 24 + 3 + 16, False), (16 + AHEAD, True)):
                ahead.skip(n, False, split)
            lower_conv_ffn()
            lower_input(in2_high, in2_low)
            ahead.skip(62 + 26, False, split=True)
            for j in range(8):
                lower_weights()
            lower_merged(out2_high)
            lower_input(up_high, h_low)
            lower_acts()


_OUT = (P, KT, T)


def kernel(**inputs):
    import concourse.bacc as _bacc
    from concourse.bass_utils import run_bass_kernel_spmd as _run

    arrays = host_layout({k: np.asarray(a) for k, a in inputs.items()})
    nc = _bacc.Bacc("TRN2", target_bir_lowering=False, num_devices=1)
    t = {k: nc.dram_tensor("in_" + k, a.shape, mybir.dt.from_np(a.dtype), kind="ExternalInput").ap()
         for k, a in arrays.items()}
    out = nc.dram_tensor("out", _OUT, F32, kind="ExternalOutput").ap()
    build(nc, t, out)
    r = _run(nc, [{"in_" + k: a for k, a in arrays.items()}], core_ids=[0])
    y = np.asarray(r.results[0]["out"])
    return np.ascontiguousarray(y.transpose(2, 1, 0)).reshape(1, T, D)


def unit_tiles(w, group=1):
    K, N = w.shape
    a = w.reshape(K // P, P, N // P, P).transpose(2, 1, 0, 3).reshape(N // P // group, group, P, K)
    return np.ascontiguousarray(a.transpose(0, 2, 1, 3)).reshape(N // P // group, P, group * K)


def token_units(w):
    n = w.shape[1] // 512
    return np.ascontiguousarray(w.reshape(4, 4, P, n, 512).transpose(3, 0, 2, 1, 4)).reshape(4 * n, P, UNIT)


def down_tiles(w):
    a = w.reshape(4, DOWN, P, KT, P).transpose(3, 0, 2, 1, 4)
    return np.ascontiguousarray(a).reshape(4 * KT, P, DOWN * P)


def columns(x):
    return x.reshape(-1, P).T


def host_layout(g):
    a = {}
    w = g["w_in"][0]
    at = np.cumsum([0, 512, 768, 768, 768, 768, 768, 768, 768, 4, 4])
    cut = [w[:, at[n]:at[n + 1]] for n in range(10)]
    a["w_mix"] = unit_tiles(np.concatenate([cut[n] for n in (0, 5, 3, 6, 2, 7, 1, 4)], axis=1))
    a["w_mix"][10:22] = token_units(np.concatenate([cut[3], cut[6]], axis=1))
    a["w_gates"] = unit_tiles(w[:, at[10]:])
    a["w_if"] = np.ascontiguousarray(w[:, at[8]:at[10]].reshape(KT, P, 8).transpose(1, 0, 2))
    qk = np.zeros((2, P, ML, 2, ML_DH), np.float32)
    for h in range(ML):
        for n, (_, lo, hi, e) in enumerate(PIECES[h]):
            for part in range(2):
                qk[part, lo:hi, h, n] = g["ml_w_qk"][0][h, e:e + hi - lo, part * ML_DH:(part + 1) * ML_DH]
    a["w_qk"] = qk.reshape(2, P, 8 * ML_DH)
    s5b = np.zeros((2, P, S5_STATES, P), np.float32)
    s5c = np.zeros((2, P, S5_STATES, P), np.float32)
    for part in range(2):
        b = g[("s5_b_re", "s5_b_im")[part]][0]
        c = g[("s5_c_re", "s5_c_im")[part]][0]
        for q in range(32):
            f, n, s = 16 * (q % 8), q // 2, 64 * (q % 2)
            s5b[part, f:f + 16, n, s:s + 64] = b[q].T
            s5c[part, s:s + 64, n, f:f + 16] = c[q].T
    a["s5_b"], a["s5_c"] = s5b.reshape(2, P, UNIT), s5c.reshape(2, P, UNIT)
    a["w_glu"] = unit_tiles(g["s5_w_glu"][0], 4)
    a["w_branch"] = unit_tiles(g["w_branch"][0])
    a["w_out"] = unit_tiles(g["w_out"][0])
    swap = np.stack([np.arange(FF_TILES), FF_TILES + np.arange(FF_TILES)], axis=1).ravel()
    a["w_up"] = unit_tiles(g["ffn_w_up"][0])[swap]
    a["w_down"] = down_tiles(g["ffn_w_down"][0])

    w = g["w_in_2"][0]
    x1, x2 = w[:, 1024:1056], w[:, 1056:1088]
    a["w_in2"] = unit_tiles(np.concatenate([w[:, 0:1024], x1, x1, x1, x1, x2, x2, x2, x2, w[:, 1088:]], axis=1))
    a["w_in2"][26:34] = token_units(w[:, 3136:4160])
    uq = g["w_uq_2"][0].reshape(512, HEADS, 192)
    a["w_uq"] = unit_tiles(np.concatenate([uq[:, :, 0:128].reshape(512, -1), uq[:, :, 128:160].reshape(512, -1),
                                           uq[:, :, 160:192].reshape(512, -1)], axis=1), 4)
    ukv = g["w_ukv_2"][0].reshape(512, HEADS, 256)
    vals = ukv[:, :, 128:].reshape(4, P, 2, 512).transpose(2, 1, 0, 3).reshape(2, P, UNIT)
    a["w_ukv"] = np.concatenate([unit_tiles(ukv[:, :, 0:128].reshape(512, -1), 4), vals], axis=0)
    a["w_mix2"] = unit_tiles(np.concatenate([g["w_o_mla_2"][0], g["w_o_dil_2"][0]], axis=0))
    a["w_o2"] = unit_tiles(g["w_o_2"][0])
    a["w_up2"] = unit_tiles(g["w_gate_up_2"][0])[swap]
    a["w_down2"] = down_tiles(g["w_down_2"][0])

    vec = np.zeros((P, VCOLS), np.float32)

    def put(name, cols, rows=P):
        vec[0:rows, VAT[name]:VAT[name] + cols.shape[1]] = cols

    put("mix_norm", columns(g["mix_norm"][0]))
    put("final_norm", columns(g["final_norm"]))
    put("ffn_norm", columns(g["ffn_norm"][0]))
    put("g_mix", columns(g["g_mix_2"][0]))
    put("g_ffn", columns(g["g_ffn_2"][0]))
    put("b_gate", columns(g["b_gate_2"][0]))
    taps = np.concatenate([g["ffn_conv_w"][0], g["ffn_conv_b"]], axis=0).reshape(4, 2 * FF_TILES, P)
    put("ffn_conv", taps[:, swap].transpose(2, 1, 0).reshape(P, -1))
    taps = np.concatenate([g["ml_conv_w"][0], g["ml_conv_b"]], axis=0).reshape(5, ML_TILES, P)
    put("ml_conv", taps.transpose(2, 1, 0).reshape(P, -1))
    put("s5_d", columns(g["s5_d"][0]))
    put("b_glu", columns(g["s5_b_glu"][0]))
    put("hg_lb", columns(g["hg_lower_bounds"][0]))
    put("hg_norm", columns(g["hg_norm"][0]))
    put("ml_norm", columns(g["ml_norm"][0]))
    put("g_cq", columns(g["g_cq_2"][0]))
    put("g_ckv", columns(g["g_ckv_2"][0]))
    for name in ("g_q_nope", "g_k_nope", "g_q_dil", "g_k_dil"):
        put(name, g[name + "_2"][0].reshape(P, 1))
    for name in ("g_q_rope", "g_k_rope"):
        put(name, np.tile(g[name + "_2"][0].reshape(2, 32).T, (4, 1)))
    put("lam_re", columns(g["s5_lam_re"][0].reshape(-1)))
    put("lam_im", columns(g["s5_lam_im"][0].reshape(-1)))
    put("log_dt", columns(np.repeat(g["s5_log_dt"][0], 64)))
    put("b_ig", g["ml_b_ig"][0].reshape(ML, 1), ML)
    put("b_fg", g["ml_b_fg"][0].reshape(ML, 1), ML)
    a["vec"] = vec
    a["xT"] = np.ascontiguousarray(g["x"][0].T.reshape(KT, P, T).transpose(1, 0, 2))

    i = np.arange(P)
    cst = np.zeros((P, 3, P), np.float32)
    cst[:, 0] = i[:, None] // 32 == i[None] // 32
    cst[:, 1] = np.eye(P)
    cst[:, 2] = i[:, None] <= i[None]
    a["cst"] = cst
    pick = np.zeros((P, 3, 2 * HEADS - 1), np.float32)
    pick[:, 0, HEADS - 1] = 1
    pick[:, 1, HEADS - 1] = i < 64
    pick[:, 2, HEADS - 1] = i >= 64
    a["pick"] = pick
    hm = np.zeros((P, 8, P), np.int32)
    hm[:, 0] = np.eye(P)
    for lvl in range(1, 8):
        B = 1 << (lvl - 1)
        s, q = i[:, None], i[None]
        hm[:, lvl] = (s // (2 * B) == q // (2 * B)) & (s // B % 2 == 0) & (q // B % 2 == 1)
    a["hmask"] = hm
    d = np.abs(np.arange(T)[:, None] - np.arange(T)[None])
    cover = sum(((d % dil == 0) & (d // dil <= win // (2 * dil))).astype(np.float32)
                for win, dil in ((128, 1), (512, 4), (2048, 16)))
    away = np.where(cover > 0, -d, MASKED).astype(np.float32)
    inv = np.float32(10000.0) ** (-np.arange(0, 64, 2, dtype=np.float32) / np.float32(64))
    ang = np.arange(T, dtype=np.float32)[None] * inv[:, None]
    band = np.zeros((P, 6, T), np.float32)
    band[:, 0:2] = away.reshape(2, P, T).transpose(1, 0, 2)
    band[:, 2:4] = cover.reshape(2, P, T).transpose(1, 0, 2)
    band[:, 4] = np.tile(np.cos(ang), (4, 1))
    band[:, 5] = np.tile(np.sin(ang), (4, 1))
    a["band"] = band
    return a
```
